# Optimizing a Trainium2 kernel written in Bass

```python
import math
import jax, jax.numpy as jnp
from jax import lax
import numpy as np

D_MODEL = 1024
BATCH = 1
SEQ = 1024
DEPTH = 2

N_DIFF_HEADS = 4
DIFF_QK_DIM = 64
DIFF_V_DIM = 2 * DIFF_QK_DIM
ATTN_WIDTH = N_DIFF_HEADS * DIFF_V_DIM
Q_BLOCK = 128

SSD_HEAD_DIM = 64
SSD_WIDTH = D_MODEL // 2
SSD_HEADS = SSD_WIDTH // SSD_HEAD_DIM
SSD_GROUPS = 2
SSD_HEADS_PER_GROUP = SSD_HEADS // SSD_GROUPS
SSD_STATE = 64
SSD_CONV = 5
SSD_CHUNK = 128
SSD_CONV_CH = SSD_WIDTH + 2 * SSD_GROUPS * SSD_STATE
DT_MIN = 1e-3
DT_MAX = 1e-1

Q_COLS = N_DIFF_HEADS * 2 * DIFF_QK_DIM
K_COLS = Q_COLS
V_COLS = ATTN_WIDTH
Z_COLS = SSD_WIDTH
DT_COLS = 2 * SSD_HEADS
IN_COLS = Q_COLS + K_COLS + V_COLS + Z_COLS + SSD_CONV_CH + DT_COLS
SPLIT_POINTS = [Q_COLS, Q_COLS + K_COLS, Q_COLS + K_COLS + V_COLS,
                Q_COLS + K_COLS + V_COLS + Z_COLS,
                Q_COLS + K_COLS + V_COLS + Z_COLS + SSD_CONV_CH]
MIX_WIDTH = ATTN_WIDTH + SSD_WIDTH

FOURIER_GROUPS = 4
FOURIER_GROUP_DIM = D_MODEL // FOURIER_GROUPS

MOE_GROUPS = 4
MOE_EXPERTS_PER_GROUP = 8
MOE_EXPERTS = MOE_GROUPS * MOE_EXPERTS_PER_GROUP
MOE_TOP_K = 2
MOE_HIDDEN = 256
MOE_BLOCK = 128

RMS_EPS = 1e-6
N_EVEN = (DEPTH + 1) // 2
N_ODD = DEPTH // 2

kernel_name = 'hybrid_diffattn_ssd_fnet_hmoe_encoder'

def rmsnorm(x, w):
    xf = x.astype(jnp.float32)
    y = xf * lax.rsqrt(jnp.mean(xf * xf, axis=-1, keepdims=True) + RMS_EPS)
    return (y * w.astype(jnp.float32)).astype(x.dtype)

def alibi_slopes(n):
    return jnp.asarray(np.array([2.0 ** (-8.0 * (h + 1) / n) for h in range(n)], dtype=np.float32))

def diff_attention(q, k, v, lam, subln_w, lambda_init):
    b, s = q.shape[0], q.shape[1]
    nb = s // Q_BLOCK
    scale = DIFF_QK_DIM ** -0.5
    slopes = alibi_slopes(N_DIFF_HEADS)
    kf = k.astype(jnp.float32)
    vf = v.astype(jnp.float32)
    key_pos = jnp.arange(s, dtype=jnp.float32)
    qb = q.astype(jnp.float32).reshape(b, nb, Q_BLOCK, N_DIFF_HEADS, 2, DIFF_QK_DIM).transpose(1, 0, 2, 3, 4, 5)
    starts = jnp.arange(nb, dtype=jnp.int32) * Q_BLOCK

    def block(args):
        qi, start = args
        scores = jnp.einsum('bqhcd,bkhcd->bhcqk', qi, kf) * scale
        q_pos = (start + jnp.arange(Q_BLOCK, dtype=jnp.int32)).astype(jnp.float32)
        dist = jnp.abs(q_pos[:, None] - key_pos[None, :])
        scores = scores - slopes[None, :, None, None, None] * dist
        probs = jax.nn.softmax(scores, axis=-1)
        weights = probs[:, :, 0] - lam * probs[:, :, 1]
        return jnp.einsum('bhqk,bkhd->bqhd', weights, vf)

    o = lax.map(block, (qb, starts))
    o = o.transpose(1, 0, 2, 3, 4).reshape(b, s, N_DIFF_HEADS, DIFF_V_DIM)
    o = rmsnorm(o, subln_w) * (1.0 - lambda_init)
    return o.reshape(b, s, ATTN_WIDTH)

def segsum(a):
    t = a.shape[-1]
    rep = jnp.broadcast_to(a[..., :, None], a.shape + (t,))
    strict = jnp.tril(jnp.ones((t, t), dtype=bool), -1)
    rep = jnp.where(strict, rep, 0.0)
    ss = jnp.cumsum(rep, axis=-2)
    return jnp.where(jnp.tril(jnp.ones((t, t), dtype=bool)), ss, -jnp.inf)

def ssd_scan(xdt, dta, bh, ch):
    b, s, h, p = xdt.shape
    n = bh.shape[-1]
    c = s // SSD_CHUNK
    xc = xdt.reshape(b, c, SSD_CHUNK, h, p)
    bc = bh.reshape(b, c, SSD_CHUNK, h, n)
    cc = ch.reshape(b, c, SSD_CHUNK, h, n)
    ac = dta.reshape(b, c, SSD_CHUNK, h).transpose(0, 3, 1, 2)
    a_cs = jnp.cumsum(ac, axis=-1)
    l_mat = jnp.exp(segsum(ac))
    y_diag = jnp.einsum('bclhn,bcshn,bhcls,bcshp->bclhp', cc, bc, l_mat, xc)
    decay_states = jnp.exp(a_cs[..., -1:] - a_cs)
    states = jnp.einsum('bclhn,bhcl,bclhp->bchpn', bc, decay_states, xc)
    states = jnp.concatenate([jnp.zeros_like(states[:, :1]), states], axis=1)
    chunk_decay = jnp.exp(segsum(jnp.pad(a_cs[..., -1], ((0, 0), (0, 0), (1, 0)))))
    states = jnp.einsum('bhzc,bchpn->bzhpn', chunk_decay, states)[:, :-1]
    y_off = jnp.einsum('bclhn,bchpn,bhcl->bclhp', cc, states, jnp.exp(a_cs))
    return (y_diag + y_off).reshape(b, s, h, p)

def centred_dwconv(x, w, bias):
    k = w.shape[0]
    y = lax.conv_general_dilated(x, w[:, None, :], window_strides=(1,), padding=[(k // 2, k // 2)],
                                 dimension_numbers=('NWC', 'WIO', 'NWC'), feature_group_count=x.shape[-1])
    return y + bias

def ssd_mixer(z, xbc, dt_raw, conv_w, conv_b, dt_bias, a_log, d_skip, norm_w):
    b, s, _ = xbc.shape
    f32 = jnp.float32
    xbc = jax.nn.silu(centred_dwconv(xbc.astype(f32), conv_w.astype(f32), conv_b.astype(f32)))
    xs = xbc[..., :SSD_WIDTH].reshape(b, s, SSD_HEADS, SSD_HEAD_DIM)
    bm = xbc[..., SSD_WIDTH:SSD_WIDTH + SSD_GROUPS * SSD_STATE].reshape(b, s, SSD_GROUPS, SSD_STATE)
    cm = xbc[..., SSD_WIDTH + SSD_GROUPS * SSD_STATE:].reshape(b, s, SSD_GROUPS, SSD_STATE)
    bh = jnp.repeat(bm, SSD_HEADS_PER_GROUP, axis=2)
    ch = jnp.repeat(cm, SSD_HEADS_PER_GROUP, axis=2)
    dt = jax.nn.softplus(dt_raw.astype(f32).reshape(b, s, 2, SSD_HEADS) + dt_bias.astype(f32))
    a = -jnp.exp(a_log.astype(f32))
    dt_f, dt_b = dt[:, :, 0], dt[:, :, 1]
    y_f = ssd_scan(xs * dt_f[..., None], dt_f * a[0], bh, ch)
    flip = lambda t: jnp.flip(t, axis=1)
    y_b = flip(ssd_scan(flip(xs * dt_b[..., None]), flip(dt_b * a[1]), flip(bh), flip(ch)))
    y = y_f + y_b + d_skip.astype(f32)[:, None] * xs
    y = y.reshape(b, s, SSD_WIDTH) * jax.nn.silu(z.astype(f32))
    return rmsnorm(y, norm_w)

def diff_ssd_mixer(h, w_in, q_norm, k_norm, lq1, lk1, lq2, lk2, subln, conv_w, conv_b,
                   dt_bias, a_log, d_skip, ssd_norm, w_out, lambda_init):
    b, s, _ = h.shape
    f32 = jnp.float32
    proj = h @ w_in
    q, k, v, z, xbc, dt_raw = jnp.split(proj, SPLIT_POINTS, axis=-1)
    q = rmsnorm(q.reshape(b, s, N_DIFF_HEADS, 2, DIFF_QK_DIM), q_norm)
    k = rmsnorm(k.reshape(b, s, N_DIFF_HEADS, 2, DIFF_QK_DIM), k_norm)
    v = v.reshape(b, s, N_DIFF_HEADS, DIFF_V_DIM)
    lam = (jnp.exp(jnp.sum(lq1.astype(f32) * lk1.astype(f32)))
           - jnp.exp(jnp.sum(lq2.astype(f32) * lk2.astype(f32))) + lambda_init)
    attn = diff_attention(q, k, v, lam, subln, lambda_init)
    ssd = ssd_mixer(z, xbc, dt_raw, conv_w, conv_b, dt_bias, a_log, d_skip, ssd_norm)
    mixed = jnp.concatenate([attn.astype(h.dtype), ssd.astype(h.dtype)], axis=-1)
    return mixed @ w_out

def fourier_mixer(h, w_f):
    b, s, d = h.shape
    hg = h.astype(jnp.float32).reshape(b, s, FOURIER_GROUPS, FOURIER_GROUP_DIM)
    f = jnp.fft.fft2(hg, axes=(1, 3), norm='ortho').real
    return f.reshape(b, s, d).astype(h.dtype) @ w_f

def expert_dispatch(xf, expert_idx, gates, w1, w3, w2):
    t, d = xf.shape
    n_assign = t * MOE_TOP_K
    n_blocks = -(-n_assign // MOE_BLOCK) + MOE_EXPERTS
    p_rows = n_blocks * MOE_BLOCK
    flat_e = expert_idx.reshape(n_assign)
    flat_tok = jnp.repeat(jnp.arange(t, dtype=jnp.int32), MOE_TOP_K)
    flat_g = gates.reshape(n_assign)
    order = jnp.argsort(flat_e)
    se, st, sg = flat_e[order], flat_tok[order], flat_g[order]
    counts = jnp.bincount(flat_e, length=MOE_EXPERTS)
    padded = (counts + MOE_BLOCK - 1) // MOE_BLOCK * MOE_BLOCK
    start = jnp.cumsum(counts) - counts
    pad_end = jnp.cumsum(padded)
    pad_start = pad_end - padded
    dest = pad_start[se] + (jnp.arange(n_assign, dtype=jnp.int32) - start[se])
    tok_buf = jnp.full((p_rows,), t, dtype=jnp.int32).at[dest].set(st)
    block_start = jnp.arange(n_blocks, dtype=jnp.int32) * MOE_BLOCK
    block_expert = jnp.minimum(jnp.sum(block_start[:, None] >= pad_end[None, :], axis=1), MOE_EXPERTS - 1)
    x_pad = jnp.concatenate([xf, jnp.zeros((1, d), xf.dtype)], axis=0)
    xb = x_pad[tok_buf].reshape(n_blocks, MOE_BLOCK, d)

    def run_block(args):
        xblk, e = args
        hid = jax.nn.silu(xblk @ w1[e]) * (xblk @ w3[e])
        return hid @ w2[e]

    yb = lax.map(run_block, (xb, block_expert)).reshape(p_rows, d)
    y_assign = yb[dest] * sg[:, None].astype(yb.dtype)
    return jnp.zeros((t, d), yb.dtype).at[st].add(y_assign)

def hier_moe(h, rg_w, rg_b, re_w, re_b, w1, w3, w2):
    b, s, d = h.shape
    t = b * s
    f32 = jnp.float32
    xf = h.reshape(t, d)
    x32 = xf.astype(f32)
    g_prob = jax.nn.softmax(x32 @ rg_w.astype(f32) + rg_b.astype(f32), axis=-1)
    g_p, g_idx = lax.top_k(g_prob, 1)
    g_p, g_idx = g_p[:, 0], g_idx[:, 0]
    e_logits = jnp.einsum('td,dge->tge', x32, re_w.astype(f32)) + re_b.astype(f32)
    e_sel = e_logits[jnp.arange(t), g_idx]
    e_prob = jax.nn.softmax(e_sel, axis=-1)
    e_p, e_local = lax.top_k(e_prob, MOE_TOP_K)
    e_p = e_p / jnp.sum(e_p, axis=-1, keepdims=True)
    gates = g_p[:, None] * e_p
    expert_idx = g_idx[:, None] * MOE_EXPERTS_PER_GROUP + e_local
    y = expert_dispatch(xf, expert_idx, gates, w1, w3, w2)
    return y.reshape(b, s, d).astype(h.dtype)

def setup_inputs(seed: int = 0) -> dict:
    key = jax.random.key(seed)
    ks = jax.random.split(key, 26)
    f32 = jnp.float32
    nrm = lambda k, shape, scale: jax.random.normal(k, shape, f32) * scale
    gain = lambda k, shape: 1.0 + 0.02 * jax.random.normal(k, shape, f32)
    u = jax.random.uniform(ks[13], (N_EVEN, 2, SSD_HEADS), f32)
    dt0 = jnp.exp(u * (math.log(DT_MAX) - math.log(DT_MIN)) + math.log(DT_MIN))
    dt_bias = dt0 + jnp.log(-jnp.expm1(-dt0))
    a_log = jnp.log(jax.random.uniform(ks[14], (N_EVEN, 2, SSD_HEADS), f32, minval=1.0, maxval=16.0))
    return {
        'x': nrm(ks[0], (BATCH, SEQ, D_MODEL), 1.0),
        'norm_mix': gain(ks[1], (DEPTH, D_MODEL)),
        'norm_ffn': gain(ks[2], (DEPTH, D_MODEL)),
        'w_in': nrm(ks[3], (N_EVEN, D_MODEL, IN_COLS), D_MODEL ** -0.5),
        'q_norm': gain(ks[4], (N_EVEN, DIFF_QK_DIM)),
        'k_norm': gain(ks[5], (N_EVEN, DIFF_QK_DIM)),
        'lambda_q1': nrm(ks[6], (N_EVEN, DIFF_QK_DIM), 0.1),
        'lambda_k1': nrm(ks[7], (N_EVEN, DIFF_QK_DIM), 0.1),
        'lambda_q2': nrm(ks[8], (N_EVEN, DIFF_QK_DIM), 0.1),
        'lambda_k2': nrm(ks[9], (N_EVEN, DIFF_QK_DIM), 0.1),
        'attn_subln': gain(ks[10], (N_EVEN, DIFF_V_DIM)),
        'conv_w': nrm(ks[11], (N_EVEN, SSD_CONV, SSD_CONV_CH), SSD_CONV ** -0.5),
        'conv_b': nrm(ks[12], (N_EVEN, SSD_CONV_CH), 0.02),
        'dt_bias': dt_bias,
        'a_log': a_log,
        'd_skip': gain(ks[15], (N_EVEN, SSD_HEADS)),
        'ssd_norm': gain(ks[16], (N_EVEN, SSD_WIDTH)),
        'w_out': nrm(ks[17], (N_EVEN, MIX_WIDTH, D_MODEL), MIX_WIDTH ** -0.5),
        'w_fourier': nrm(ks[18], (N_ODD, D_MODEL, D_MODEL), D_MODEL ** -0.5),
        'router_group_w': nrm(ks[19], (DEPTH, D_MODEL, MOE_GROUPS), D_MODEL ** -0.5),
        'router_group_b': nrm(ks[20], (DEPTH, MOE_GROUPS), 0.01),
        'router_expert_w': nrm(ks[21], (DEPTH, D_MODEL, MOE_GROUPS, MOE_EXPERTS_PER_GROUP), D_MODEL ** -0.5),
        'router_expert_b': nrm(ks[22], (DEPTH, MOE_GROUPS, MOE_EXPERTS_PER_GROUP), 0.01),
        'expert_w1': nrm(ks[23], (DEPTH, MOE_EXPERTS, D_MODEL, MOE_HIDDEN), D_MODEL ** -0.5),
        'expert_w3': nrm(ks[24], (DEPTH, MOE_EXPERTS, D_MODEL, MOE_HIDDEN), D_MODEL ** -0.5),
        'expert_w2': nrm(ks[25], (DEPTH, MOE_EXPERTS, MOE_HIDDEN, D_MODEL), MOE_HIDDEN ** -0.5),
    }

def reference(x, norm_mix, norm_ffn, w_in, q_norm, k_norm, lambda_q1, lambda_k1, lambda_q2, lambda_k2,
              attn_subln, conv_w, conv_b, dt_bias, a_log, d_skip, ssd_norm, w_out, w_fourier,
              router_group_w, router_group_b, router_expert_w, router_expert_b,
              expert_w1, expert_w3, expert_w2):
    for l in range(DEPTH):
        i = l // 2
        h = rmsnorm(x, norm_mix[l])
        if l % 2 == 0:
            lambda_init = 0.8 - 0.6 * math.exp(-0.3 * l)
            x = x + diff_ssd_mixer(h, w_in[i], q_norm[i], k_norm[i], lambda_q1[i], lambda_k1[i],
                                   lambda_q2[i], lambda_k2[i], attn_subln[i], conv_w[i], conv_b[i],
                                   dt_bias[i], a_log[i], d_skip[i], ssd_norm[i], w_out[i], lambda_init)
        else:
            x = x + fourier_mixer(h, w_fourier[i])
        h = rmsnorm(x, norm_ffn[l])
        x = x + hier_moe(h, router_group_w[l], router_group_b[l], router_expert_w[l], router_expert_b[l],
                         expert_w1[l], expert_w3[l], expert_w2[l])
    return x


_drawn_inputs = setup_inputs


def setup_inputs(seed=0):
    import zlib

    import numpy as np

    out = dict(_drawn_inputs(seed))
    spreads = {}
    factors = {'q_norm': 2.711,
     'lambda_k2': 4.426,
     'd_skip': 4.909,
     'router_group_b': 3.472,
     'router_expert_b': 5.253}
    for name, (base, spread) in spreads.items():
        noise = np.random.default_rng([zlib.crc32(name.encode()), seed]).standard_normal(out[name].shape)
        drawn = base * np.exp(spread * noise) if base else spread * noise
        out[name] = __import__('jax').numpy.asarray(drawn.astype(out[name].dtype))
    for name, factor in factors.items():
        out[name] = (out[name] * factor).astype(out[name].dtype)
    return out
```

```python
from contextlib import ExitStack, contextmanager

import concourse.bass as bass
from concourse import mybir

F32 = mybir.dt.float32
I32 = mybir.dt.int32
U32 = mybir.dt.uint32
ALU = mybir.AluOpType
ACT = mybir.ActivationFunctionType
AX = mybir.AxisListType.X

P = 128
D = 1024
SEQ = 1024
T = SEQ // P
KT = D // P
HALF = 512
HEADS = 4
QK = 64
VD = 128
SSD_H = 8
SSD_W = 512
XBC = 768
XBC_T = XBC // P
CONV = 5
COL_V, COL_Z, COL_XBC, COL_DT = 1024, 1536, 2048, 2816
EXPERTS = 32
GROUPS = 4
PER_GROUP = EXPERTS // GROUPS
HID = 256
MAX_BLOCKS = 48
SLOT_BLOCKS = MAX_BLOCKS + 1
BIG = 1.0e30
EPS = 1e-6
SLOPES = [2.0 ** (-8.0 * (h + 1) / HEADS) for h in range(HEADS)]
LAMBDA_INIT = 0.8 - 0.6
ROW_CONVW, ROW_CONVB, ROW_SSDN, ROW_SUBLN, ROW_QN, ROW_KN, N_ROWS = 0, 30, 36, 40, 41, 42, 43
M_LE, M_GT, M_GE, M_LT, M_ONE = range(5)


def wait(eng, sem, value):
    if isinstance(value, int) and value <= 0:
        return
    eng.wait_ge(sem, value)


class Chain:

    def __init__(self, eng, sem):
        self.eng, self.sem, self.n = eng, sem, 0

    def __call__(self, ins):
        ins.then_inc(self.sem, 1)
        self.n = self.n + 1
        self.eng.wait_ge(self.sem, self.n)


def tt(e, out, a, b, op):
    return e.tensor_tensor(out=out, in0=a, in1=b, op=op)


def load_constants(nc, g):
    io = g.io
    with ExitStack() as ctx:
        rows = ctx.enter_context(nc.sbuf_tensor("rows", [P, P], F32))
        zero = ctx.enter_context(nc.sbuf_tensor("zero", [P, D], F32))
        lam4 = ctx.enter_context(nc.sbuf_tensor("lam4", [P, 4, QK], F32))
        lamp = ctx.enter_context(nc.sbuf_tensor("lamp", [P, 2, QK], F32))
        lams = ctx.enter_context(nc.sbuf_tensor("lams", [P, 2], F32))
        cst, rowl = g.sem("constants_loaded"), g.sem("vector_rows_loaded")
        zs, rt = g.sem("zero_ready"), g.sem("rows_transposed")
        ds, ls, es = g.sem("dve_const_step"), g.sem("lambda_sums_ready"), g.sem("lambda_exps_ready")
        n_cst = 8
        with nc.Block() as block:
            @block.sync
            def _(sp):
                sp.dma_start(g.ident[:], io["c_ident"]).then_inc(cst, 16)
                sp.dma_start(g.masks[:], io["c_masks"]).then_inc(cst, 16)
                sp.dma_start(g.small[:], io["c_small"].partition_broadcast(P)).then_inc(cst, 16)
                for t in range(T):
                    base = t // 4 + 2 * P * (t % 4)
                    sp.dma_start(g.x[:, t, :], io["x"][0, base:base + 2 * P - 1:2, :]).then_inc(g.x_loaded, 16)

            @block.scalar
            def _(act):
                act.dma_start(rows[0:30, :], io["conv_w"][0].rearrange("k (c p) -> (k c) p", p=P)).then_inc(rowl, 16)
                act.dma_start(rows[30:36, :], io["conv_b"][0].rearrange("(c p) -> c p", p=P)).then_inc(rowl, 16)
                act.dma_start(rows[36:40, :], io["ssd_norm"][0].rearrange("(c p) -> c p", p=P)).then_inc(rowl, 16)
                act.dma_start(rows[40:41, :], io["attn_subln"]).then_inc(rowl, 16)
                for c in range(2):
                    act.dma_start(rows[41:42, c * QK:(c + 1) * QK], io["q_norm"]).then_inc(rowl, 16)
                    act.dma_start(rows[42:43, c * QK:(c + 1) * QK], io["k_norm"]).then_inc(rowl, 16)
                act.dma_start(g.dtb[:, 0:16], io["dt_bias"][0].rearrange("a h -> (a h)").partition_broadcast(P)).then_inc(cst, 16)
                act.dma_start(g.dtb[:, 16:32], io["a_log"][0].rearrange("a h -> (a h)").partition_broadcast(P)).then_inc(cst, 16)
                act.dma_start(g.dskip[:], io["d_skip"][0].partition_broadcast(P)).then_inc(cst, 16)
                for n, name in enumerate(("lambda_q1", "lambda_k1", "lambda_q2", "lambda_k2")):
                    if n < 2:
                        act.dma_start(lam4[:, n, :], io[name][0].partition_broadcast(P)).then_inc(cst, 16)
                    else:
                        act.dma_start(lam4[:, n, :], io[name][0].partition_broadcast(P)).then_inc(rowl, 16)
                act.wait_ge(ls, 1)
                nc.scalar.activation(lams[:], lams[:], ACT.Exp).then_inc(es, 1)
                act.wait_ge(cst, 16 * n_cst)
                nc.scalar.activation(g.dtb[:, 16:32], g.dtb[:, 16:32], ACT.Exp).then_inc(es, 1)

            @block.gpsimd
            def _(pool):
                nc.gpsimd.memset(g.mhalf[:], -0.5).then_inc(zs, 1)
                nc.gpsimd.memset(zero[:], 0.0).then_inc(zs, 1)
                pool.wait_ge(zs, 2)
                for b in range(SLOT_BLOCKS):
                    pool.dma_start(g.slots[b * P:(b + 1) * P, :], zero[:]).then_inc(g.slots_cleared, 16)
                pool.wait_ge(g.slots_cleared, 16 * SLOT_BLOCKS)

            @block.tensor
            def _(pe):
                pe.wait_ge(rowl, 16 * 10)
                pe.wait_ge(cst, 16 * n_cst)
                nc.tensor.transpose(g.ps[:, 0, 0:N_ROWS], rows[0:N_ROWS, :], g.ident[0:N_ROWS, 0:N_ROWS]).then_inc(rt, 1)

            @block.vector
            def _(dve):
                step = Chain(dve, ds)
                dve.wait_ge(rowl, 16 * 10)
                dve.wait_ge(cst, 16 * n_cst)
                step(tt(nc.vector, lamp[:, 0, :], lam4[:, 0, :], lam4[:, 1, :], ALU.mult))
                step(tt(nc.vector, lamp[:, 1, :], lam4[:, 2, :], lam4[:, 3, :], ALU.mult))
                nc.vector.tensor_reduce(out=lams[:], in_=lamp[:], axis=AX, op=ALU.add).then_inc(ls, 1)
                dve.wait_ge(es, 2)
                step(tt(nc.vector, g.neglam[:], lams[:, 1:2], lams[:, 0:1], ALU.subtract))
                step(nc.vector.tensor_scalar(g.neglam[:], g.neglam[:], -LAMBDA_INIT, None, ALU.add))
                step(nc.vector.tensor_scalar(g.dtb[:, 16:32], g.dtb[:, 16:32], -1.0, None, ALU.mult))
                dve.wait_ge(rt, 1)
                step(nc.vector.tensor_copy(g.vecs[:, 0:N_ROWS], g.ps[:, 0, 0:N_ROWS]))
                for h in range(HEADS):
                    step(nc.vector.tensor_scalar(g.qscale[:, h:h + 1], g.vecs[:, ROW_QN:ROW_QN + 1],
                                                 QK ** -0.5 / SLOPES[h], None, ALU.mult))
                    step(nc.vector.memset(g.negslope[:, h:h + 1], -SLOPES[h]))
                step(nc.vector.tensor_scalar(g.vecs[:, ROW_SUBLN:ROW_SUBLN + 1], g.vecs[:, ROW_SUBLN:ROW_SUBLN + 1],
                                             1.0 - LAMBDA_INIT, None, ALU.mult))


def norm_transpose(nc, g, tag, gain, hT, h, order, blocked, first=False):
    slots = h.shape[1]
    with ExitStack() as ctx:
        sb = lambda n, s: ctx.enter_context(nc.sbuf_tensor(f"{n}_{tag}", s, F32))
        gb, junk, ss, rs = sb("gain_b", [P, D]), sb("squares", [P, D]), sb("sumsq", [P, T]), sb("rstd", [P, T])
        gl, ssr, rsr = g.sem(f"gain_loaded_{tag}"), g.sem(f"sumsq_ready_{tag}"), g.sem(f"rstd_step_{tag}")
        hr, tr = g.sem(f"h_ready_{tag}"), g.sem(f"h_transposed_{tag}")
        ea, ed = g.sem(f"hT_low_ready_{tag}"), g.sem(f"hT_high_ready_{tag}")
        with nc.Block() as block:
            @block.sync
            def _(sp):
                sp.dma_start(gb[:], gain.partition_broadcast(P)).then_inc(gl, 16)

            @block.scalar
            def _(act):
                def squares(t):
                    if first:
                        act.wait_ge(g.x_loaded, 16 * T)
                    wait(act, ssr, t)
                    nc.scalar.activation(junk[:], g.x[:, t, :], ACT.Square, accum_out=ss[:, t:t + 1]).then_inc(ssr, 1)

                squares(0)
                squares(1)
                for t in range(T):
                    if t + 2 < T:
                        squares(t + 2)
                    act.wait_ge(tr, t + 1)
                    nc.scalar.activation(order(hT, t, 0), g.ps[:, 2 * (t % 2), :].rearrange("p (j n) -> p j n", n=P),
                                         ACT.Copy).then_inc(ea, 1)

            @block.gpsimd
            def _(pool):
                for t in range(T):
                    pool.wait_ge(ssr, t + 1)
                    nc.gpsimd.tensor_scalar(rs[:, t:t + 1], ss[:, t:t + 1], 1.0 / D, EPS, ALU.mult, ALU.add).then_inc(rsr, 1)
                    pool.wait_ge(rsr, 2 * t + 1)
                    tt(nc.gpsimd, rs[:, t:t + 1], rs[:, t:t + 1], g.mhalf[:, 0:1], ALU.pow).then_inc(rsr, 1)

            @block.vector
            def _(dve):
                dve.wait_ge(gl, 16)
                if first:
                    dve.wait_ge(g.x_loaded, 16 * T)

                def normed(t):
                    dve.wait_ge(rsr, 2 * t + 2)
                    if slots < T:
                        wait(dve, tr, t - slots + 1)
                    nc.vector.scalar_tensor_tensor(out=h[:, t % slots, :], in0=g.x[:, t, :], scalar=rs[:, t:t + 1], in1=gb[:],
                                                   op0=ALU.mult, op1=ALU.mult).then_inc(hr, 1)

                normed(0)
                for t in range(T):
                    if t + 1 < T:
                        normed(t + 1)
                    dve.wait_ge(tr, t + 1)
                    nc.vector.tensor_copy(order(hT, t, 1), g.ps[:, 2 * (t % 2) + 1, :].rearrange("p (j n) -> p j n", n=P)).then_inc(ed, 1)

            @block.tensor
            def _(pe):
                for t in range(T):
                    pe.wait_ge(hr, t + 1)
                    wait(pe, ea, t - 1)
                    wait(pe, ed, t - 1)
                    hv = h[:, t % slots, :]
                    for j in range(KT):
                        src = hv[:, j * P:(j + 1) * P] if blocked else hv.rearrange("p (q j) -> p j q", j=KT)[:, j, :]
                        last = nc.tensor.transpose(g.ps[:, 2 * (t % 2) + j // 4, (j % 4) * P:(j % 4 + 1) * P], src, g.ident[:])
                    last.then_inc(tr, 1)


def order_natural(hT, t, half):
    v = hT[:, :, :].rearrange("p j (i two) -> p j two i", two=2)
    return v[:, 4 * half:4 * half + 4, t // 4, (t % 4) * P:(t % 4 + 1) * P]


def order_tile(hT, t, half):
    return hT[:, 4 * half:4 * half + 4, t * P:(t + 1) * P]


def ssd_project(nc, g, hT, xbcT, xs, mixed, draw):
    io = g.io
    w_in = io["w_in"][0].rearrange("(p j) n -> p j n", j=KT)
    with ExitStack() as ctx:
        sb = lambda n, s: ctx.enter_context(nc.sbuf_tensor(n, s, F32))
        wx, wz, wd = sb("w_xbc", [P, KT, XBC]), sb("w_z", [P, KT, HALF]), sb("w_dt", [P, KT, 16])
        acc = sb("conv_acc", [P, 2, SEQ])
        wl, pr, ev = g.sem("w_xbc_loaded"), g.sem("ssd_unit_ready"), g.sem("ssd_unit_read")
        wzl, pads = g.sem("w_z_loaded"), g.sem("conv_pads_ready")
        cs, cv, sl, xt, xe = g.sem("conv_step"), g.sem("conv_ready"), g.sem("silu_ready"), g.sem("x_transposed"), g.sem("x_by_token_ready")
        NX = 2 * XBC_T
        with nc.Block() as block:
            @block.sync
            def _(sp):
                sp.dma_start(wx[:], w_in[:, :, COL_XBC:COL_XBC + XBC]).then_inc(wl, 16)
                sp.dma_start(wz[:], w_in[:, :, COL_Z:COL_Z + HALF]).then_inc(wzl, 16)
                sp.dma_start(wd[:], w_in[:, :, COL_DT:COL_DT + 16]).then_inc(wzl, 16)

            @block.gpsimd
            def _(pool):
                nc.gpsimd.memset(xbcT[:, :, 0:2], 0.0).then_inc(pads, 1)
                nc.gpsimd.memset(xbcT[:, :, SEQ + 2:SEQ + 4], 0.0).then_inc(pads, 1)

            @block.tensor
            def _(pe):
                pe.wait_ge(wl, 16)
                for u in range(NX):
                    ct, half = u // 2, u % 2
                    wait(pe, ev, u - 3)
                    for j in range(KT):
                        last = nc.tensor.matmul(g.ps[:, u % 4, :], wx[:, j, ct * P:(ct + 1) * P],
                                                hT[:, j, half * HALF:(half + 1) * HALF], start=j == 0, stop=j == KT - 1)
                    last.then_inc(pr, 1)
                pe.wait_ge(wzl, 32)
                for t in range(T):
                    u = NX + t
                    wait(pe, ev, u - 3)
                    for j in range(KT):
                        last = nc.tensor.matmul(g.ps[:, u % 4, :], hT[:, j, t * P:(t + 1) * P], wz[:, j, :], start=j == 0, stop=j == KT - 1)
                    last.then_inc(pr, 1)
                u = NX + T
                pe.wait_ge(ev, u - 3)
                for t in range(T):
                    for j in range(KT):
                        last = nc.tensor.matmul(g.ps[:, u % 4, t * 16:(t + 1) * 16], hT[:, j, t * P:(t + 1) * P], wd[:, j, :],
                                                start=j == 0, stop=j == KT - 1)
                last.then_inc(pr, 1)
                for c in range(T):
                    pe.wait_ge(sl, 5)
                    wait(pe, xe, c - 1)
                    for ct in range(5):
                        last = nc.tensor.transpose(g.ps[:, 4 + 2 * (c % 2) + ct // 4, (ct % 4) * P:(ct % 4 + 1) * P],
                                                   xbcT[:, ct, c * P:(c + 1) * P], g.ident[:])
                    last.then_inc(xt, 1)

            @block.scalar
            def _(act):
                for u in range(NX):
                    ct, half = u // 2, u % 2
                    act.wait_ge(pr, u + 1)
                    nc.scalar.activation(xbcT[:, ct, 2 + half * HALF:2 + (half + 1) * HALF], g.ps[:, u % 4, :], ACT.Copy).then_inc(ev, 1)
                done = 0
                for t in range(T):
                    u = NX + t
                    act.wait_ge(pr, u + 1)
                    nc.scalar.activation(mixed[:, t, SSD_W:], g.ps[:, u % 4, :], ACT.Silu).then_inc(ev, 1)
                    if t >= 2 and done < XBC_T:
                        act.wait_ge(cv, done + 1)
                        nc.scalar.activation(xbcT[:, done, 0:SEQ], acc[:, done % 2, :], ACT.Silu).then_inc(sl, 1)
                        done += 1
                act.wait_ge(pr, NX + T + 1)
                nc.scalar.activation(draw[:], g.ps[:, (NX + T) % 4, 0:P].rearrange("p (t n) -> p t n", n=16), ACT.Copy).then_inc(ev, 1)
                assert done == XBC_T
                for c in range(T):
                    act.wait_ge(xt, c + 1)
                    nc.scalar.activation(xs[:, c, 0:640], g.ps[:, 4 + 2 * (c % 2):6 + 2 * (c % 2), :].rearrange("p a n -> p (a n)")[:, 0:640],
                                         ACT.Copy).then_inc(xe, 1)

            @block.vector
            def _(dve):
                step = Chain(dve, cs)
                dve.wait_ge(pads, 2)
                for ct in range(XBC_T):
                    dve.wait_ge(ev, 2 * ct + 2)
                    wait(dve, sl, ct - 1)
                    a = acc[:, ct % 2, :]
                    w = lambda k: g.vecs[:, ROW_CONVW + k * XBC_T + ct:ROW_CONVW + k * XBC_T + ct + 1]
                    step(nc.vector.tensor_scalar(a, xbcT[:, ct, 0:SEQ], w(0), g.vecs[:, ROW_CONVB + ct:ROW_CONVB + ct + 1], ALU.mult, ALU.add))
                    for k in range(1, CONV):
                        ins = nc.vector.scalar_tensor_tensor(out=a, in0=xbcT[:, ct, k:k + SEQ], scalar=w(k), in1=a, op0=ALU.mult, op1=ALU.add)
                        if k < CONV - 1:
                            step(ins)
                    ins.then_inc(cv, 1)
                    dve.wait_ge(cv, ct + 1)


def ssd_scan(nc, g, xbcT, xs, mixed, draw):
    NC = T
    with ExitStack() as ctx:
        sb = lambda n, s: ctx.enter_context(nc.sbuf_tensor(n, s, F32))
        dt, a = sb("dt", [P, NC, 16]), sb("dta", [P, NC, 16])
        r1, r2 = sb("dt_pos", [P, NC, 16]), sb("dt_abs", [P, NC, 16])
        ex = sb("decays", [P, 384])
        bz = sb("b_by_group", [P, 2, SEQ])
        half_mask = lambda gr: g.masks[:, 5 * P + gr:5 * P + gr + 1]
        am = sb("a_masked", [P, 2, SSD_H, P])
        lm = sb("l_mat", [P, 2, SSD_H, P])
        cb = sb("cb_masked", [P, 2, 2, P])
        xd = sb("x_dt", [P, 2, SSD_W])
        xw = sb("x_decayed", [P, 2, SSD_W])
        st = sb("state", [P, 2, SSD_W])
        off = sb("y_off", [P, SSD_W])
        y = sb("y", [P, NC, SSD_W])
        ss, rs = sb("ssd_sumsq", [P, NC]), sb("ssd_rstd", [P, NC])
        dtm = [g.sem(f"softplus_{n}") for n in ("in", "exp", "ln")]
        ar, cum, exr = g.sem("dta_ready"), g.sem("cumsums_ready"), g.sem("decays_ready")
        vs, psd = g.sem("dve_ssd_step"), g.sem("pool_ssd_step")
        amr, seg, lr, mr = g.sem("a_masked_ready"), g.sem("segsum_ready"), g.sem("l_exp_ready"), g.sem("m_ready")
        cbr, yd, ydr = g.sem("cb_ready"), g.sem("y_diag_ready"), g.sem("y_diag_added")
        xdr, xwr, inc, inr = g.sem("x_dt_ready"), g.sem("x_decayed_ready"), g.sem("state_inc_ready"), g.sem("state_updated")
        yo, yor, cbu = g.sem("y_off_ready"), g.sem("y_off_added"), g.sem("cb_read")
        yg, sq, fin = g.sem("y_gated"), g.sem("ssd_squares_ready"), g.sem("ssd_rstd_step")
        y0 = g.sem("y_skip_ready")
        bzr = g.sem("b_by_group_ready")
        mask = lambda m: g.masks[:, m * P:(m + 1) * P]
        bh = lambda v: v.unsqueeze(2).to_broadcast([P, SSD_H, 64])
        hv = lambda v: v.rearrange("p (h n) -> p h n", h=SSD_H)
        dirs = lambda i: (i, NC - 1 - i)
        with nc.Block() as block:
            @block.scalar
            def _(act):
                act.wait_ge(dtm[0], 1)
                nc.scalar.activation(r2[:], r2[:], ACT.Exp, scale=-1.0).then_inc(dtm[1], 1)
                act.wait_ge(dtm[1], 1)
                nc.scalar.activation(r2[:], r2[:], ACT.Ln, bias=1.0).then_inc(dtm[2], 1)
                act.wait_ge(cum, 1)
                nc.scalar.activation(ex[:], g.ps[:, 7, 0:384], ACT.Exp).then_inc(exr, 1)
                for i in range(NC):
                    for d in range(2):
                        act.wait_ge(seg, 2 * i + d + 1)
                        wait(act, yd, i)
                        nc.scalar.activation(lm[:, d].rearrange("p h n -> p (h n)"), g.ps[:, 2 * d:2 * d + 2, :].rearrange("p a n -> p (a n)"),
                                             ACT.Exp).then_inc(lr, 1)
                for c in range(NC):
                    act.wait_ge(yg, c + 1)
                    wait(act, sq, c)
                    nc.scalar.activation(off[:], y[:, c, :], ACT.Square, accum_out=ss[:, c:c + 1]).then_inc(sq, 1)

            @block.tensor
            def _(pe):
                pe.wait_ge(ar, 1)
                for n, (m, d) in enumerate(((M_LE, 0), (M_GE, 1), (M_GT, 0), (M_LT, 1))):
                    nc.tensor.matmul(g.ps[:, 7, 64 * n:64 * n + 64], mask(m), a[:, :, 8 * d:8 * d + 8], start=True, stop=True)
                nc.tensor.matmul(g.ps[:, 7, 256:384], mask(M_ONE), a[:].rearrange("p c n -> p (c n)"), start=True, stop=True).then_inc(cum, 1)

                def segsums(i):
                    for d in range(2):
                        pe.wait_ge(amr, 2 * i + d + 1)
                        wait(pe, lr, 2 * i + d - 1)
                        for half in range(2):
                            last = nc.tensor.matmul(g.ps[:, 2 * d + half, :], mask((M_GT, M_LT)[d]),
                                                    am[:, d].rearrange("p h n -> p (h n)")[:, half * HALF:(half + 1) * HALF], start=True, stop=True)
                        last.then_inc(seg, 1)

                segsums(0)
                pe.wait_ge(bzr, 2)
                for i in range(NC):
                    wait(pe, cbu, 2 * i)
                    for gr in range(2):
                        last = nc.tensor.matmul(g.ps[:, 4, gr * P:(gr + 1) * P], bz[:, gr, i * P:(i + 1) * P],
                                                xbcT[:, 5, i * P:(i + 1) * P], start=True, stop=True)
                    last.then_inc(cbr, 1)
                    for d in range(2):
                        c = dirs(i)[d]
                        if i < NC - 1:
                            pe.wait_ge(xwr, 2 * i + d + 1)
                            wait(pe, inr, 2 * i + d)
                            if i == 0 and d == 0:
                                pe.wait_ge(exr, 1)
                            nc.tensor.matmul(g.ps[:, 7, :], xs[:, c, SSD_W:SSD_W + P], xw[:, d, :], start=True, stop=True).then_inc(inc, 1)
                        if i > 0:
                            pe.wait_ge(inr, 2 * (i - 1) + d + 1)
                            wait(pe, yor, 2 * (i - 1) + d)
                            nc.tensor.matmul(g.ps[:, 6, :], xbcT[:, 5, c * P:(c + 1) * P], st[:, d, :], start=True, stop=True).then_inc(yo, 1)
                    if i + 1 < NC:
                        segsums(i + 1)
                    pe.wait_ge(mr, 2 * i + 2)
                    pe.wait_ge(xdr, 2 * i + 2)
                    wait(pe, ydr, i)
                    for h in range(SSD_H):
                        for d in range(2):
                            last = nc.tensor.matmul(g.ps[:, 5, h * 64:h * 64 + 64], lm[:, d, h, :], xd[:, d, h * 64:h * 64 + 64],
                                                    start=d == 0, stop=d == 1)
                    last.then_inc(yd, 1)

            @block.gpsimd
            def _(pool):
                pool.wait_ge(ar, 1)

                def masked(i):
                    for d in range(2):
                        wait(pool, seg, 2 * (i - 1) + d + 1)
                        tt(nc.gpsimd, am[:, d], mask((M_LE, M_GE)[d]).unsqueeze(1).to_broadcast([P, SSD_H, P]),
                           a[:, i, 8 * d:8 * d + 8].unsqueeze(2).to_broadcast([P, SSD_H, P]), ALU.mult).then_inc(amr, 1)

                masked(0)
                for i in range(NC):
                    for d in range(2):
                        wait(pool, yd, i)
                        tt(nc.gpsimd, hv(xd[:, d, :]), hv(xs[:, i, 0:SSD_W]), bh(dt[:, i, 8 * d:8 * d + 8]), ALU.mult).then_inc(xdr, 1)
                    if i + 1 < NC:
                        masked(i + 1)
                for c in range(NC):
                    pool.wait_ge(sq, c + 1)
                    nc.gpsimd.tensor_scalar(rs[:, c:c + 1], ss[:, c:c + 1], 1.0 / SSD_W, EPS, ALU.mult, ALU.add).then_inc(fin, 1)
                    pool.wait_ge(fin, 2 * c + 1)
                    tt(nc.gpsimd, rs[:, c:c + 1], rs[:, c:c + 1], g.mhalf[:, 0:1], ALU.pow).then_inc(fin, 1)

            @block.vector
            def _(dve):
                step = Chain(dve, vs)
                V = nc.vector
                b3 = lambda v: v.unsqueeze(1).to_broadcast([P, NC, 16])
                step(tt(V, r1[:], draw[:], b3(g.dtb[:, 0:16]), ALU.add))
                V.scalar_tensor_tensor(out=r2[:], in0=r1[:], scalar=-1.0, in1=r1[:], op0=ALU.mult, op1=ALU.max).then_inc(dtm[0], 1)
                dve.wait_ge(dtm[0], 1)
                step(V.tensor_scalar(r1[:], r1[:], 0.0, None, ALU.max))
                step(V.memset(st[:], 0.0))
                dve.wait_ge(dtm[2], 1)
                step(tt(V, dt[:], r1[:], r2[:], ALU.add))
                tt(V, a[:], dt[:], b3(g.dtb[:, 16:32]), ALU.mult).then_inc(ar, 1)
                for gr in range(2):
                    V.tensor_scalar(bz[:, gr, :], xbcT[:, 4, 0:SEQ], half_mask(gr), None, ALU.mult).then_inc(bzr, 1)
                for c in range(NC):
                    step(tt(V, hv(y[:, c, :]), hv(xs[:, c, 0:SSD_W]), bh(g.dskip[:]), ALU.mult))
                dve.wait_ge(ar, 1)
                dve.wait_ge(exr, 1)
                e4 = ex[:, 0:256].rearrange("p (q c h) -> p q c h", q=4, h=SSD_H)
                e5 = ex[:, 256:384].rearrange("p (c q) -> p c q", q=16)
                for d in range(2):
                    step(tt(V, e4[:, 2 + d], e4[:, 2 + d], dt[:, :, 8 * d:8 * d + 8], ALU.mult))
                for i in range(NC):
                    if i < NC - 1:
                        for d in range(2):
                            c = dirs(i)[d]
                            wait(dve, inc, 2 * (i - 1) + d + 1)
                            tt(V, hv(xw[:, d, :]), hv(xs[:, c, 0:SSD_W]), bh(e4[:, 2 + d, c]), ALU.mult).then_inc(xwr, 1)
                    dve.wait_ge(cbr, i + 1)
                    wait(dve, mr, 2 * i)
                    for d in range(2):
                        tt(V, cb[:, d], g.ps[:, 4, 0:256].rearrange("p (g n) -> p g n", g=2),
                           mask((M_LE, M_GE)[d]).unsqueeze(1).to_broadcast([P, 2, P]), ALU.mult).then_inc(cbu, 1)
                    dve.wait_ge(cbu, 2 * i + 2)
                    for d in range(2):
                        c = dirs(i)[d]
                        if i > 0:
                            dve.wait_ge(yo, 2 * (i - 1) + d + 1)
                            step(tt(V, hv(off[:]), hv(g.ps[:, 6, :]), bh(e4[:, d, c]), ALU.mult))
                            tt(V, y[:, c, :], y[:, c, :], off[:], ALU.add).then_inc(yor, 1)
                            dve.wait_ge(yor, 2 * (i - 1) + d + 1)
                        if i < NC - 1:
                            step(tt(V, hv(st[:, d, :]), hv(st[:, d, :]), bh(e5[:, c, 8 * d:8 * d + 8]), ALU.mult))
                            dve.wait_ge(inc, 2 * i + d + 1)
                            for gr in range(2):
                                cols = slice(256 * gr, 256 * gr + 256)
                                ins = V.scalar_tensor_tensor(out=st[:, d, cols], in0=g.ps[:, 7, cols], scalar=half_mask(gr), in1=st[:, d, cols],
                                                             op0=ALU.mult, op1=ALU.add)
                            ins.then_inc(inr, 1)
                    for d in range(2):
                        dve.wait_ge(lr, 2 * i + d + 1)
                        for gr in range(2):
                            ins = tt(V, lm[:, d, 4 * gr:4 * gr + 4, :], lm[:, d, 4 * gr:4 * gr + 4, :],
                                     cb[:, d, gr, :].unsqueeze(1).to_broadcast([P, 4, P]), ALU.mult)
                        ins.then_inc(mr, 1)
                    dve.wait_ge(yd, i + 1)
                    tt(V, y[:, i, :], y[:, i, :], g.ps[:, 5, :], ALU.add).then_inc(ydr, 1)
                    dve.wait_ge(ydr, i + 1)
                for c in range(NC):
                    tt(V, y[:, c, :], y[:, c, :], mixed[:, c, SSD_W:], ALU.mult).then_inc(yg, 1)
                for c in range(NC):
                    dve.wait_ge(yg, NC)
                    dve.wait_ge(fin, 2 * c + 2)
                    step(V.tensor_scalar(mixed[:, c, SSD_W:], y[:, c, :], rs[:, c:c + 1], None, ALU.mult))


def attention(nc, g, hT, mixed):
    io = g.io
    w_in = io["w_in"][0].rearrange("(p j) n -> p j n", j=KT)
    with ExitStack() as ctx:
        sb = lambda n, s: ctx.enter_context(nc.sbuf_tensor(n, s, F32))
        w = sb("w_qkv", [P, KT, 3, P])
        qT, kT, v = sb("qT", [P, SEQ]), sb("kT", [P, SEQ]), sb("v", [P, T, VD])
        qk, sq = sb("qk_normed", [P, 2, 256]), sb("qk_squares", [P, 256])
        ss, rs = sb("qk_sumsq", [P, T, 4]), sb("qk_rstd", [P, T, 4])
        dist = sb("negdist", [P, 1920])
        pr = sb("probs", [P, 2, 2, SEQ])
        wt, wtT = sb("weights", [P, 2, SEQ]), sb("weightsT", [P, 2, SEQ])
        mx, den = sb("neg_max", [P, 2, 2]), sb("denoms", [P, T, 2])
        cf, rd = sb("coef", [P, 2]), sb("rdenom", [P, T])
        o, osq = sb("o", [P, T, VD]), sb("o_squares", [P, VD])
        oss, ors = sb("o_sumsq", [P, T]), sb("o_rstd", [P, T])
        nsl, qs = sb("neg_slope_h", [P, 1]), sb("qscale_h", [P, 1])
        dl, wl = g.sem("dist_loaded"), g.sem("w_qkv_loaded")
        pj, vr = g.sem("proj_ready"), g.sem("v_ready")
        sqr, ssr, rsr, nr = g.sem("qk_squares_ready"), g.sem("qk_sumsq_ready"), g.sem("qk_rstd_step"), g.sem("qk_normed_ready")
        tr, tq, tk = g.sem("qk_transposed"), g.sem("qT_ready"), g.sem("kT_ready")
        sr, ng, er = g.sem("scores_ready"), g.sem("neg_scores_ready"), g.sem("exp_ready")
        wr, wtr, wte = g.sem("weights_ready"), g.sem("weights_transposed"), g.sem("weightsT_ready")
        pv, oe, osr, ofs = g.sem("pv_ready"), g.sem("o_read"), g.sem("o_squares_ready"), g.sem("o_rstd_step")
        vs, fin, hd = g.sem("dve_attn_step"), g.sem("o_written"), g.sem("head_scalars_ready")
        seen, seen_p = g.sem("scores_wait_passed"), g.sem("sumsq_wait_passed")
        with nc.Block() as block:
            @block.sync
            def _(sp):
                sp.dma_start(dist[:], io["c_negdist"]).then_inc(dl, 16)

                def load(h):
                    for n in range(3):
                        sp.dma_start(w[:, :, n, :], w_in[:, :, bass.ds(h * P + n * HALF, P)]).then_inc(wl, 16)

                load(0)
                with sp.Fori(1, HEADS) as h:
                    sp.wait_ge(pj, h * T)
                    load(h)

            @block.tensor
            def _(pe):
                def head(h):
                    def transposes(t):
                        pe.wait_ge(nr, h * T + t + 1)
                        wait(pe, tq, h * T + t)
                        wait(pe, tk, h * T + t)
                        for n in range(2):
                            last = nc.tensor.transpose(g.ps[:, 7 - n, 0:P], qk[:, t % 2, n * P:(n + 1) * P], g.ident[:])
                        last.then_inc(tr, 1)

                    pe.wait_ge(wl, 48 * (h + 1))
                    wait(pe, ng, h * 2 * T)
                    wait(pe, oe, h * T)
                    for t in range(T):
                        if t >= 4:
                            pe.wait_ge(nr, h * T + t - 3)
                            pe.wait_ge(vr, h * T + t - 3)
                        for j in range(KT):
                            last = nc.tensor.matmul(g.ps[:, t % 4, 0:384], hT[:, j, t * P:(t + 1) * P],
                                                    w[:, j, :, :].rearrange("p a n -> p (a n)"), start=j == 0, stop=j == KT - 1)
                        last.then_inc(pj, 1)
                        if t >= 1:
                            transposes(t - 1)
                    transposes(T - 1)
                    pe.wait_ge(tq, h * T + T)
                    pe.wait_ge(tk, h * T + T)
                    pe.wait_ge(vr, h * T + T)
                    for u in range(T + 2):
                        if u < T:
                            for c in range(2):
                                if u > 0:
                                    pe.wait_ge(ng, h * 2 * T + 2 * (u - 1) + c + 1)
                                for half in range(2):
                                    last = nc.tensor.matmul(g.ps[:, 2 * c + half, :], qT[64 * c:64 * c + 64, u * P:(u + 1) * P],
                                                            kT[64 * c:64 * c + 64, half * HALF:(half + 1) * HALF], start=True, stop=True)
                                last.then_inc(sr, 1)
                        if 1 <= u <= T:
                            q = u - 1
                            pe.wait_ge(wr, h * T + q + 1)
                            wait(pe, wte, h * T + q)
                            for k in range(T):
                                last = nc.tensor.transpose(g.ps[:, 4 + k // 4, (k % 4) * P:(k % 4 + 1) * P], wt[:, q % 2, k * P:(k + 1) * P], g.ident[:])
                            last.then_inc(wtr, 1)
                        if u >= 2:
                            q = u - 2
                            pe.wait_ge(wte, h * T + q + 1)
                            wait(pe, oe, h * T + q)
                            for k in range(T):
                                last = nc.tensor.matmul(g.ps[:, 6, 0:VD], wtT[:, q % 2, k * P:(k + 1) * P], v[:, k, :], start=k == 0, stop=k == T - 1)
                            last.then_inc(pv, 1)

                head(0)
                with pe.Fori(1, HEADS) as h:
                    head(h)

            @block.scalar
            def _(act):
                def head(h):
                    wait(act, pv, h * T)
                    for t in range(T):
                        act.wait_ge(pj, h * T + t + 1)
                        wait(act, ssr, h * T + t)
                        nc.scalar.activation(sq[:], g.ps[:, t % 4, 0:256], ACT.Square).then_inc(sqr, 1)
                        nc.scalar.activation(v[:, t, :], g.ps[:, t % 4, 256:384], ACT.Copy).then_inc(vr, 1)
                        act.wait_ge(tr, h * T + t + 1)
                        nc.scalar.activation(kT[:, t * P:(t + 1) * P], g.ps[:, 6, 0:P], ACT.Copy,
                                             scale=g.vecs[:, ROW_KN:ROW_KN + 1]).then_inc(tk, 1)
                    for u in range(T + 2):
                        if u < T:
                            for c in range(2):
                                act.wait_ge(ng, h * 2 * T + 2 * u + c + 1)
                                p = pr[:, u % 2, c, :]
                                nc.scalar.activation(p, p, ACT.Exp, scale=-1.0, bias=mx[:, u % 2, c:c + 1],
                                                     accum_out=den[:, u, c:c + 1]).then_inc(er, 1)
                        if 1 <= u <= T:
                            q = u - 1
                            act.wait_ge(wtr, h * T + q + 1)
                            if q >= 2:
                                act.wait_ge(pv, h * T + q - 1)
                            nc.scalar.activation(wtT[:, q % 2, :], g.ps[:, 4:6, :].rearrange("p a n -> p (a n)"), ACT.Copy).then_inc(wte, 1)
                        if u >= 2:
                            q = u - 2
                            act.wait_ge(pv, h * T + q + 1)
                            wait(act, fin, h)
                            nc.scalar.activation(o[:, q, :], g.ps[:, 6, 0:VD], ACT.Copy, scale=rd[:, q:q + 1]).then_inc(oe, 1)
                            act.wait_ge(oe, h * T + q + 1)
                            wait(act, osr, h * T + q)
                            nc.scalar.activation(osq[:], o[:, q, :], ACT.Square, accum_out=oss[:, q:q + 1]).then_inc(osr, 1)

                head(0)
                with act.Fori(1, HEADS) as h:
                    head(h)

            @block.gpsimd
            def _(pool):
                def head(h):
                    for t in range(T):
                        pool.wait_ge(ssr, h * T + t + 1)
                        wait(pool, nr, h * T + t)
                        pool.sem_inc(seen_p, 1)
                        nc.gpsimd.tensor_scalar(rs[:, t, :], ss[:, t, :], 1.0 / QK, EPS, ALU.mult, ALU.add).then_inc(rsr, 1)
                        pool.wait_ge(rsr, h * 2 * T + 2 * t + 1)
                        tt(nc.gpsimd, rs[:, t, :], rs[:, t, :], g.mhalf[:, 0:4], ALU.pow).then_inc(rsr, 1)
                    pool.wait_ge(osr, h * T + T)
                    pool.sem_inc(seen_p, 1)
                    nc.gpsimd.tensor_scalar(ors[:], oss[:], 1.0 / VD, EPS, ALU.mult, ALU.add).then_inc(ofs, 1)
                    pool.wait_ge(ofs, 2 * h + 1)
                    tt(nc.gpsimd, ors[:], ors[:], g.mhalf[:, 0:T], ALU.pow).then_inc(ofs, 1)

                head(0)
                with pool.Fori(1, HEADS) as h:
                    head(h)

            @block.vector
            def _(dve):
                V = nc.vector
                step = Chain(dve, vs)
                dve.wait_ge(dl, 16)

                def head(h):
                    wait(dve, ng, h * 2 * T)
                    V.tensor_copy(nsl[:], g.negslope[:, bass.ds(h, 1)]).then_inc(hd, 1)
                    V.tensor_copy(qs[:], g.qscale[:, bass.ds(h, 1)]).then_inc(hd, 1)
                    dve.wait_ge(hd, 2 * h + 2)

                    def normed(t):
                        dve.wait_ge(rsr, h * 2 * T + 2 * t + 2)
                        dve.wait_ge(vr, h * T + t + 1)
                        if t >= 2:
                            dve.wait_ge(tr, h * T + t - 1)
                        tt(V, qk[:, t % 2, :].rearrange("p (a n) -> p a n", n=QK), g.ps[:, t % 4, 0:256].rearrange("p (a n) -> p a n", n=QK),
                           rs[:, t, :].unsqueeze(2).to_broadcast([P, 4, QK]), ALU.mult).then_inc(nr, 1)

                    def q_out(t):
                        dve.wait_ge(tr, h * T + t + 1)
                        V.tensor_scalar(qT[:, t * P:(t + 1) * P], g.ps[:, 7, 0:P], qs[:, 0:1], None, ALU.mult).then_inc(tq, 1)

                    for t in range(T):
                        dve.wait_ge(sqr, h * T + t + 1)
                        V.tensor_reduce(out=ss[:, t, :], in_=sq[:].rearrange("p (a n) -> p a n", n=QK), axis=AX, op=ALU.add).then_inc(ssr, 1)
                        normed(t)
                        q_out(t)
                    for u in range(T):
                        for c in range(2):
                            if u >= 2:
                                dve.wait_ge(wr, h * T + u - 1)
                            dve.wait_ge(sr, h * 2 * T + 2 * u + c + 1)
                            dve.sem_inc(seen, 1)
                            V.tensor_tensor_reduce(out=pr[:, u % 2, c, :], in0=g.ps[:, 2 * c:2 * c + 2, :].rearrange("p a n -> p (a n)"),
                                                   in1=dist[:, 896 - u * P:896 - u * P + SEQ], scale=nsl[:, 0:1], scalar=3.0e38,
                                                   op0=ALU.add, op1=ALU.min, accum_out=mx[:, u % 2, c:c + 1]).then_inc(ng, 1)
                        dve.wait_ge(er, h * 2 * T + 2 * u + 2)
                        base = h * 3 * T + 3 * u
                        V.reciprocal(cf[:], den[:, u, :]).then_inc(vs, 1)
                        dve.wait_ge(vs, base + 1)
                        V.tensor_copy(rd[:, u:u + 1], cf[:, 0:1]).then_inc(vs, 1)
                        V.scalar_tensor_tensor(out=cf[:, 1:2], in0=den[:, u, 0:1], scalar=g.neglam[:, 0:1], in1=cf[:, 1:2],
                                               op0=ALU.mult, op1=ALU.mult).then_inc(vs, 1)
                        dve.wait_ge(vs, base + 3)
                        if u >= 2:
                            dve.wait_ge(wtr, h * T + u - 1)
                        V.scalar_tensor_tensor(out=wt[:, u % 2, :], in0=pr[:, u % 2, 1, :], scalar=cf[:, 1:2], in1=pr[:, u % 2, 0, :],
                                               op0=ALU.mult, op1=ALU.add).then_inc(wr, 1)
                        dve.wait_ge(wr, h * T + u + 1)
                    dve.wait_ge(ofs, 2 * h + 2)
                    tt(V, mixed[:, :, bass.ds(h * VD, VD)], o[:], ors[:].unsqueeze(2).to_broadcast([P, T, VD]), ALU.mult).then_inc(fin, 1)

                head(0)
                with dve.Fori(1, HEADS) as h:
                    head(h)


def project_out(nc, g, tag, src, srcT, weight, scaled):
    with ExitStack() as ctx:
        w = ctx.enter_context(nc.sbuf_tensor(f"w_{tag}", [P, KT, D], F32))
        wl, tr = g.sem(f"w_loaded_{tag}"), g.sem(f"mix_transposed_{tag}")
        ea, ed = g.sem(f"mixT_low_{tag}"), g.sem(f"mixT_high_{tag}")
        pr, xa = g.sem(f"out_ready_{tag}"), g.sem(f"x_added_{tag}")
        wv = weight.rearrange("(j p) n -> p j n", p=P)
        with nc.Block() as block:
            @block.sync
            def _(sp):
                for j in range(KT):
                    sp.dma_start(w[:, j, :], wv[:, j, :]).then_inc(wl, 16)

            @block.tensor
            def _(pe):
                if src is not None:
                    for t in range(T):
                        wait(pe, ea, t - 1)
                        wait(pe, ed, 4 * (t - 1))
                        for j in range(KT):
                            last = nc.tensor.transpose(g.ps[:, 2 * (t % 2) + j // 4, (j % 4) * P:(j % 4 + 1) * P], src[:, t, j * P:(j + 1) * P], g.ident[:])
                        last.then_inc(tr, 1)
                    pe.wait_ge(ea, T)
                    pe.wait_ge(ed, 4 * T)
                pe.wait_ge(wl, 16 * KT)
                sv = srcT[:, :, :].rearrange("p j (i two) -> p j two i", two=2)
                for t in range(T):
                    wait(pe, xa, t - 1)
                    for half in range(2):
                        for j in range(KT):
                            last = nc.tensor.matmul(g.ps[:, 4 + 2 * (t % 2) + half, :], sv[:, j, t // 4, (t % 4) * P:(t % 4 + 1) * P],
                                                    w[:, j, half * HALF:(half + 1) * HALF], start=j == 0, stop=j == KT - 1)
                    last.then_inc(pr, 1)

            @block.scalar
            def _(act):
                if src is not None:
                    for t in range(T):
                        act.wait_ge(tr, t + 1)
                        nc.scalar.activation(srcT[:, 0:4, t * P:(t + 1) * P], g.ps[:, 2 * (t % 2), :].rearrange("p (j n) -> p j n", n=P), ACT.Copy,
                                             scale=scaled[:, ROW_SUBLN:ROW_SUBLN + 1]).then_inc(ea, 1)

            @block.vector
            def _(dve):
                if src is not None:
                    for t in range(T):
                        dve.wait_ge(tr, t + 1)
                        for j in range(4):
                            nc.vector.tensor_scalar(srcT[:, 4 + j, t * P:(t + 1) * P], g.ps[:, 2 * (t % 2) + 1, j * P:(j + 1) * P],
                                                    scaled[:, ROW_SSDN + j:ROW_SSDN + j + 1], None, ALU.mult).then_inc(ed, 1)
                for t in range(T):
                    dve.wait_ge(pr, t + 1)
                    tt(nc.vector, g.x[:, t, :], g.x[:, t, :], g.ps[:, 4 + 2 * (t % 2):6 + 2 * (t % 2), :].rearrange("p a n -> p (a n)"), ALU.add).then_inc(xa, 1)


def route(nc, g, layer, hT, h):
    io = g.io
    NL = GROUPS + EXPERTS
    with ExitStack() as ctx:
        sb = lambda n, s, d=F32: ctx.enter_context(nc.sbuf_tensor(f"{n}_r{layer}", s, d))
        rw, rb = sb("router_w", [P, KT, NL]), sb("router_b", [P, NL])
        gl, el = sb("group_logits", [P, T, 8]), sb("expert_logits", [P, T, EXPERTS])
        gm, em = sb("group_max", [P, T, 8]), sb("expert_max", [P, T, 8])
        gi, ei = sb("group_idx", [P, T, 8], U32), sb("expert_idx", [P, T, 8], U32)
        gf, ef = sb("group_idx_f", [P, T]), sb("expert_idx_f", [P, T, 2])
        m12 = sb("choice", [P, 2, T, EXPERTS])
        both, pre = sb("chosen", [P, T, EXPERTS]), sb("chosen_before", [P, T, EXPERTS])
        ge, gs, gp = sb("group_exp", [P, T, 4]), sb("group_sum", [P, T]), sb("group_p", [P, T])
        de, dn = sb("expert_exp", [P, T]), sb("expert_den", [P, T])
        cnt, cge = sb("counts", [P, EXPERTS]), sb("count_steps", [P, EXPERTS, 8])
        nb, inc, inc2 = sb("n_blocks", [P, EXPERTS]), sb("blocks_end", [P, EXPERTS]), sb("blocks_end2", [P, EXPERTS])
        rk, rt = sb("slot_of", [P, T, EXPERTS]), sb("slot_tmp", [P, T, EXPERTS])
        df = sb("slot_f", [P, 2, T])
        bt, bf = sb("block_cmp", [1, MAX_BLOCKS, EXPERTS]), sb("block_expert_f", [1, MAX_BLOCKS])
        npf = sb("n_pairs_f", [1, 2])
        cmp24 = sb("pair_cmp", [1, MAX_BLOCKS // 2])
        rl, lr = g.sem(f"router_loaded_{layer}"), g.sem(f"logits_ready_{layer}")
        vs, gd, ge_r = g.sem(f"dve_route_step_{layer}"), g.sem(f"softmax_in_{layer}"), g.sem(f"softmax_exp_{layer}")
        ch, rr, sd = g.sem(f"chosen_ready_{layer}"), g.sem(f"ranks_ready_{layer}"), g.sem(f"slots_ready_{layer}")
        sc = g.sem(f"scattered_{layer}")
        rgw = io["router_group_w"][layer].rearrange("(p j) g -> p j g", j=KT)
        rew = io["router_expert_w"][layer].rearrange("(p j) g e -> p j (g e)", j=KT)
        iota_e, grp_e, iota_b, j128 = (g.small[:, a:b] for a, b in ((0, 32), (32, 64), (64, 112), (112, 120)))
        with nc.Block() as block:
            @block.sync
            def _(sp):
                with nc.allow_non_contiguous_dma("router weights, rows of 4 and 32"):
                    sp.dma_start(rw[:, :, 0:GROUPS], rgw).then_inc(rl, 16)
                    sp.dma_start(rw[:, :, GROUPS:], rew).then_inc(rl, 16)
                    sp.dma_start(rb[:, 0:GROUPS], io["router_group_b"][layer].partition_broadcast(P)).then_inc(rl, 16)
                    sp.dma_start(rb[:, GROUPS:], io["router_expert_b"][layer].rearrange("g e -> (g e)").partition_broadcast(P)).then_inc(rl, 16)

            @block.tensor
            def _(pe):
                pe.wait_ge(rl, 64)
                for t in range(T):
                    for j in range(KT):
                        last = nc.tensor.matmul(g.ps[:, 0, t * NL:(t + 1) * NL], hT[:, j, t * P:(t + 1) * P], rw[:, j, :], start=j == 0, stop=j == KT - 1)
                last.then_inc(lr, 1)
                pe.wait_ge(ch, 1)
                for t in range(T):
                    nc.tensor.matmul(g.ps[:, 1, t * EXPERTS:(t + 1) * EXPERTS], g.masks[:, M_LT * P:(M_LT + 1) * P], both[:, t, :], start=True, stop=False)
                    nc.tensor.matmul(g.ps[:, 1, t * EXPERTS:(t + 1) * EXPERTS], g.masks[:, M_ONE * P:(M_ONE + 1) * P], pre[:, t, :], start=False, stop=True)
                nc.tensor.matmul(g.ps[:, 2, 0:EXPERTS], g.masks[:, M_ONE * P:(M_ONE + 1) * P], cnt[:], start=True, stop=True).then_inc(rr, 1)

            @block.scalar
            def _(act):
                act.wait_ge(gd, 1)
                nc.scalar.activation(ge[:], ge[:], ACT.Exp).then_inc(ge_r, 1)
                act.wait_ge(gd, 2)
                nc.scalar.activation(de[:], de[:], ACT.Exp).then_inc(ge_r, 1)

            @block.vector
            def _(dve):
                V = nc.vector
                step = Chain(dve, vs)
                bE = lambda v: v.unsqueeze(2).to_broadcast([P, T, EXPERTS])
                cE = lambda v: v.unsqueeze(1).to_broadcast([P, T, EXPERTS])
                step(V.memset(gl[:], -BIG))
                dve.wait_ge(rl, 64)
                dve.wait_ge(lr, 1)
                lg = g.ps[:, 0, 0:T * NL].rearrange("p (t n) -> p t n", n=NL)
                step(tt(V, gl[:, :, 0:GROUPS], lg[:, :, 0:GROUPS], rb[:, 0:GROUPS].unsqueeze(1).to_broadcast([P, T, GROUPS]), ALU.add))
                step(tt(V, el[:], lg[:, :, GROUPS:], cE(rb[:, GROUPS:]), ALU.add))
                for t in range(T):
                    step(V.max(gm[:, t, :], gl[:, t, :]))
                    step(V.max_index(gi[:, t, :], gm[:, t, :], gl[:, t, :]))
                tt(V, ge[:], gl[:, :, 0:GROUPS], gm[:, :, 0:1].to_broadcast([P, T, GROUPS]), ALU.subtract).then_inc(gd, 1)
                step(V.tensor_copy(gf[:], gi[:, :, 0]))
                step(tt(V, rt[:], cE(grp_e), bE(gf[:]), ALU.is_equal))
                step(V.tensor_scalar(rk[:], rt[:], BIG, -BIG, ALU.mult, ALU.add))
                step(tt(V, el[:], el[:], rk[:], ALU.add))
                for t in range(T):
                    step(V.max(em[:, t, :], el[:, t, :]))
                    step(V.max_index(ei[:, t, :], em[:, t, :], el[:, t, :]))
                tt(V, de[:], em[:, :, 1], em[:, :, 0], ALU.subtract).then_inc(gd, 1)
                step(V.tensor_copy(ef[:], ei[:, :, 0:2]))
                for k in range(2):
                    step(tt(V, m12[:, k], cE(iota_e), bE(ef[:, :, k]), ALU.is_equal))
                step(tt(V, both[:], m12[:, 0], m12[:, 1], ALU.add))
                step(V.memset(pre[:, 0, :], 0.0))
                for t in range(1, T):
                    step(tt(V, pre[:, t, :], pre[:, t - 1, :], both[:, t - 1, :], ALU.add))
                tt(V, cnt[:], pre[:, T - 1, :], both[:, T - 1, :], ALU.add).then_inc(ch, 1)
                dve.wait_ge(ge_r, 2)
                step(V.tensor_reduce(out=gs[:], in_=ge[:], axis=AX, op=ALU.add))
                step(V.tensor_scalar(dn[:], de[:], 1.0, None, ALU.add))
                step(tt(V, dn[:], dn[:], gs[:], ALU.mult))
                step(V.reciprocal(g.gates[:, 0, :], dn[:]))
                step(tt(V, g.gates[:, 1, :], g.gates[:, 0, :], de[:], ALU.mult))
                dve.wait_ge(rr, 1)
                step(V.tensor_copy(cnt[:], g.ps[:, 2, 0:EXPERTS]))
                step(tt(V, cge[:], cnt[:].unsqueeze(2).to_broadcast([P, EXPERTS, 8]), j128.unsqueeze(1).to_broadcast([P, EXPERTS, 8]), ALU.is_gt))
                step(V.tensor_reduce(out=nb[:], in_=cge[:], axis=AX, op=ALU.add))
                src, dst = nb, inc
                for s in (1, 2, 4, 8, 16):
                    step(V.tensor_copy(dst[:, 0:s], src[:, 0:s]))
                    step(tt(V, dst[:, s:], src[:, s:], src[:, 0:EXPERTS - s], ALU.add))
                    src, dst = dst, (inc2 if dst is inc else inc)
                end, start = src, dst
                step(tt(V, start[:], end[:], nb[:], ALU.subtract))
                step(V.tensor_scalar(start[:], start[:], float(P), None, ALU.mult))
                step(tt(V, rk[:], g.ps[:, 1, 0:T * EXPERTS].rearrange("p (t n) -> p t n", n=EXPERTS), cE(start[:]), ALU.add))
                for k in range(2):
                    step(tt(V, rt[:], rk[:], m12[:, k], ALU.mult))
                    step(V.tensor_reduce(out=df[:, k, :], in_=rt[:], axis=AX, op=ALU.add))
                V.tensor_copy(g.slot_i[:], df[:]).then_inc(sd, 1)
                step(tt(V, bt[:], end[0:1, :].unsqueeze(1).to_broadcast([1, MAX_BLOCKS, EXPERTS]),
                        iota_b[0:1, :].unsqueeze(2).to_broadcast([1, MAX_BLOCKS, EXPERTS]), ALU.is_le))
                step(V.tensor_reduce(out=bf[:], in_=bt[:], axis=AX, op=ALU.add))
                step(V.tensor_scalar(bf[:], bf[:], float(EXPERTS - 1), None, ALU.min))
                step(V.tensor_copy(g.block_expert[:], bf[:]))
                step(tt(V, cmp24[:], end[0:1, EXPERTS - 1:EXPERTS].to_broadcast([1, MAX_BLOCKS // 2]), iota_b[0:1, 0:MAX_BLOCKS:2], ALU.is_gt))
                step(V.tensor_reduce(out=npf[:, 0:1], in_=cmp24[:], axis=AX, op=ALU.add))
                step(V.tensor_scalar(g.last_pair[:], npf[:, 0:1], -1.0, None, ALU.add))

            @block.gpsimd
            def _(pool):
                pool.wait_ge(sd, 1)
                for t in range(T):
                    for k in range(2):
                        pool.indirect_dma_start(out=g.slots[:, :], out_offset=bass.IndirectOffsetOnAxis(ap=g.slot_i[:, k, t:t + 1], axis=0),
                                                in_=h[:, t, :], in_offset=None).then_inc(sc, 16)
                pool.wait_ge(sc, 16 * 2 * T)


def experts(nc, g, layer):
    io = g.io
    w1 = io["expert_w1"][layer].rearrange("e (p j) n -> e p j n", j=KT)
    w3 = io["expert_w3"][layer].rearrange("e (p j) n -> e p j n", j=KT)
    w2 = io["expert_w2"][layer].rearrange("e (p j) n -> e p (j n)", j=2)
    with ExitStack() as ctx:
        sb = lambda n, s: ctx.enter_context(nc.sbuf_tensor(f"{n}_e{layer}", s, F32))
        w13, w2s = sb("w13", [P, 2, 2, KT, HID]), sb("w2", [P, 2, 2, D])
        xb, xT = sb("x_block", [P, 2, D]), sb("xT_block", [P, 2, KT, P])
        sg, hid, hT = sb("silu", [P, 2, HID]), sb("hidden", [P, 2, HID]), sb("hiddenT", [P, 2, P])
        yb = sb("y_block", [P, 2, D])
        xl = [g.sem(f"x_block_loaded{s}_{layer}") for s in range(2)]
        w13l = [g.sem(f"w13_loaded{s}_{layer}") for s in range(2)]
        w2l = [g.sem(f"w2_loaded{s}_{layer}") for s in range(2)]
        yst = [g.sem(f"y_stored{s}_{layer}") for s in range(2)]
        xt, xea, xed = g.sem(f"xT_ready_{layer}"), g.sem(f"xT_low_read_{layer}"), g.sem(f"xT_high_read_{layer}")
        gu, sil, hr = g.sem(f"gate_up_ready_{layer}"), g.sem(f"silu_done_{layer}"), g.sem(f"hidden_ready_{layer}")
        ht, he, yr = g.sem(f"hidden_transposed_{layer}"), g.sem(f"hiddenT_ready_{layer}"), g.sem(f"y_ready_{layer}")
        yea, yed = g.sem(f"y_low_read_{layer}"), g.sem(f"y_high_read_{layer}")
        PAIRS = MAX_BLOCKS // 2

        def pairs(eng, step, finish=None):
            m = eng.value_load(g.last_pair[0:1, 0:1], min_val=0, max_val=PAIRS - 1)
            for i in range(2):
                step(i, 0)
                step(i, 1)
            with eng.Fori(2, PAIRS) as i:
                with eng.If(i <= m):
                    step(i, 0)
                    step(i, 1)
                with eng.Else():
                    eng.nop()
            if finish:
                finish(m)

        with nc.Block() as block:
            @block.sync
            def _(sp):
                def load_x(k, s):
                    sp.dma_start(xb[:, s, :], g.slots[bass.ds(k * P, P), :]).then_inc(xl[s], 16)

                load_x(0, 0)

                def step(i, s):
                    k = 2 * i + s
                    wait(sp, xt, k)
                    load_x(k + 1, 1 - s)
                    e = sp.value_load(g.block_expert[0:1, bass.ds(k, 1)], min_val=0, max_val=EXPERTS - 1)
                    wait(sp, gu, k - 1)
                    for n, w in enumerate((w1, w3)):
                        sp.dma_start(w13[:, s, n, :, :], w[bass.ds(e, 1), :, :, :].rearrange("e p j n -> (e p) j n")).then_inc(w13l[s], 16)

                pairs(sp, step)

            @block.gpsimd
            def _(pool):
                def store_y(i, s):
                    k = 2 * i + s
                    pool.wait_ge(yea, k + 1)
                    pool.wait_ge(yed, k + 1)
                    pool.dma_start(g.slots[bass.ds(k * P, P), :], yb[:, s, :]).then_inc(yst[s], 16)

                def step(i, s):
                    k = 2 * i + s
                    e = pool.value_load(g.block_expert[0:1, bass.ds(k, 1)], min_val=0, max_val=EXPERTS - 1)
                    wait(pool, yr, k - 1)
                    pool.dma_start(w2s[:, s, :, :].rearrange("p j n -> p (j n)"),
                                   w2[bass.ds(e, 1), :, :].rearrange("e p n -> (e p) n")).then_inc(w2l[s], 16)
                    if isinstance(k, int) and k == 0:
                        return
                    store_y(i - 1 + s, 1 - s)

                def finish(m):
                    store_y(m, 1)
                    for s in range(2):
                        pool.wait_ge(yst[s], 16 * (m + 1))

                pairs(pool, step, finish)

            @block.tensor
            def _(pe):
                def transpose_x(k, s, turn):
                    pe.wait_ge(xl[s], 16 * (turn + 1))
                    wait(pe, xea, k)
                    wait(pe, xed, k)
                    xv = xb[:, s, :].rearrange("p (q j) -> p j q", j=KT)
                    for j in range(KT):
                        last = nc.tensor.transpose(g.ps[:, 2 + j // 4, (j % 4) * P:(j % 4 + 1) * P], xv[:, j, :], g.ident[:])
                    last.then_inc(xt, 1)

                def transpose_hidden(k, s):
                    pe.wait_ge(hr, k + 1)
                    wait(pe, he, k)
                    hv = hid[:, s, :].rearrange("p (q j) -> p j q", j=2)
                    for j in range(2):
                        last = nc.tensor.transpose(g.ps[:, 4, j * P:(j + 1) * P], hv[:, j, :], g.ident[:])
                    last.then_inc(ht, 1)

                def down(k, s, turn):
                    pe.wait_ge(he, k + 1)
                    pe.wait_ge(w2l[s], 16 * (turn + 1))
                    wait(pe, yea, k)
                    wait(pe, yed, k)
                    for half in range(2):
                        for j in range(2):
                            last = nc.tensor.matmul(g.ps[:, 5 + half, :], hT[:, j, :], w2s[:, s, j, half * HALF:(half + 1) * HALF], start=j == 0, stop=j == 1)
                    last.then_inc(yr, 1)

                transpose_x(0, 0, 0)

                def step(i, s):
                    k = 2 * i + s
                    pe.wait_ge(w13l[s], 32 * (i + 1))
                    pe.wait_ge(xea, k + 1)
                    pe.wait_ge(xed, k + 1)
                    wait(pe, hr, k - 1)
                    for j in range(KT):
                        last = nc.tensor.matmul(g.ps[:, s, :], xT[:, s, j, :], w13[:, s, :, j, :], start=j == 0, stop=j == KT - 1)
                    last.then_inc(gu, 1)
                    first = isinstance(k, int) and k == 0
                    if not first:
                        transpose_hidden(k - 1, 1 - s)
                    transpose_x(k + 1, 1 - s, i + s)
                    if not first:
                        down(k - 1, 1 - s, i - 1 + s)

                def finish(m):
                    transpose_hidden(2 * m + 1, 1)
                    down(2 * m + 1, 1, m)

                pairs(pe, step, finish)

            @block.scalar
            def _(act):
                def copy_x(k, s):
                    act.wait_ge(xt, k + 1)
                    wait(act, gu, k - 1)
                    nc.scalar.activation(xT[:, s, 0:4, :].rearrange("p j n -> p (j n)"), g.ps[:, 2, :], ACT.Copy).then_inc(xea, 1)

                def copy_y(k, s, stored):
                    act.wait_ge(yr, k + 1)
                    wait(act, yst[s], stored)
                    nc.scalar.activation(yb[:, s, 0:HALF], g.ps[:, 5, :], ACT.Copy).then_inc(yea, 1)

                copy_x(0, 0)

                def step(i, s):
                    k = 2 * i + s
                    act.wait_ge(gu, k + 1)
                    wait(act, hr, k - 1)
                    nc.scalar.activation(sg[:, s, :], g.ps[:, s, 0:HID], ACT.Silu).then_inc(sil, 1)
                    copy_x(k + 1, 1 - s)
                    if not (isinstance(k, int) and k == 0):
                        copy_y(k - 1, 1 - s, 16 * (i - 1 + s))

                pairs(act, step, lambda m: copy_y(2 * m + 1, 1, 16 * m))

            @block.vector
            def _(dve):
                def copy_x(k, s):
                    dve.wait_ge(xt, k + 1)
                    wait(dve, gu, k - 1)
                    nc.vector.tensor_copy(xT[:, s, 4:8, :].rearrange("p j n -> p (j n)"), g.ps[:, 3, :]).then_inc(xed, 1)

                def copy_hidden(k):
                    dve.wait_ge(ht, k + 1)
                    wait(dve, yr, k)
                    nc.vector.tensor_copy(hT[:].rearrange("p j n -> p (j n)"), g.ps[:, 4, 0:2 * P]).then_inc(he, 1)

                def copy_y(k, s, stored):
                    dve.wait_ge(yr, k + 1)
                    wait(dve, yst[s], stored)
                    nc.vector.tensor_copy(yb[:, s, HALF:], g.ps[:, 6, :]).then_inc(yed, 1)

                copy_x(0, 0)

                def step(i, s):
                    k = 2 * i + s
                    first = isinstance(k, int) and k == 0
                    if not first:
                        copy_hidden(k - 1)
                    dve.wait_ge(sil, k + 1)
                    wait(dve, ht, k - 1)
                    tt(nc.vector, hid[:, s, :], sg[:, s, :], g.ps[:, s, HID:], ALU.mult).then_inc(hr, 1)
                    copy_x(k + 1, 1 - s)
                    if not first:
                        copy_y(k - 1, 1 - s, 16 * (i - 1 + s))

                def finish(m):
                    copy_hidden(2 * m + 1)
                    copy_y(2 * m + 1, 1, 16 * m)

                pairs(dve, step, finish)


def combine(nc, g, layer, last_layer):
    BUF = 4
    with ExitStack() as ctx:
        yg = ctx.enter_context(nc.sbuf_tensor(f"y_gathered_{layer}", [P, BUF, 2, D], F32))
        gt = [g.sem(f"y_gathered{s}_{layer}") for s in range(BUF)]
        vs, ad, out = g.sem(f"dve_combine_step_{layer}"), g.sem(f"combined_{layer}"), g.sem(f"out_stored_{layer}")
        with nc.Block() as block:
            @block.gpsimd
            def _(pool):
                for t in range(T):
                    wait(pool, ad, t - BUF + 1)
                    for k in range(2):
                        pool.indirect_dma_start(out=yg[:, t % BUF, k, :], out_offset=None, in_=g.slots[:, :],
                                                in_offset=bass.IndirectOffsetOnAxis(ap=g.slot_i[:, k, t:t + 1], axis=0)).then_inc(gt[t % BUF], 16)

            @block.vector
            def _(dve):
                step = Chain(dve, vs)
                for t in range(T):
                    dve.wait_ge(gt[t % BUF], 32 * (t // BUF + 1))
                    for k in range(2):
                        ins = nc.vector.scalar_tensor_tensor(out=g.x[:, t, :], in0=yg[:, t % BUF, k, :], scalar=g.gates[:, k, t:t + 1], in1=g.x[:, t, :],
                                                             op0=ALU.mult, op1=ALU.add)
                        if k == 0:
                            step(ins)
                    ins.then_inc(ad, 1)

            @block.sync
            def _(sp):
                if last_layer:
                    for t in range(T):
                        sp.wait_ge(ad, t + 1)
                        base = t // 4 + 2 * P * (t % 4)
                        sp.dma_start(g.io["out"][0, base:base + 2 * P - 1:2, :], g.x[:, t, :]).then_inc(out, 16)
                    sp.wait_ge(out, 16 * T)


def fourier(nc, g, hT, fT):
    io = g.io
    with ExitStack() as ctx:
        sb = lambda n, s: ctx.enter_context(nc.sbuf_tensor(n, s, F32))
        dch = sb("dft_channels", [P, 2, HALF])
        dsq = sb("dft_tokens", [P, 2, 2, 4, HALF])
        ab = sb("dft_stage1", [P, T, 2, D])
        ev = sb("dft_even", [P, 2, HALF])
        cl, sl = g.sem("dft_channels_loaded"), g.sem("dft_tokens_loaded")
        p1, r1 = g.sem("stage1_ready"), [g.sem("stage1_even_read"), g.sem("stage1_odd_read")]
        p2, er, fr = g.sem("stage2_ready"), g.sem("even_copied"), g.sem("fT_ready")
        with nc.Block() as block:
            @block.sync
            def _(sp):
                sp.dma_start(dch[:], io["c_dft_channels"].rearrange("(a p) n -> p a n", p=P)).then_inc(cl, 16)
                for par in range(2):
                    for cs in range(2):
                        sp.dma_start(dsq[:, par, cs, :, :], io["c_dft_tokens"][par, cs].rearrange("(a p) n -> p a n", p=P)).then_inc(sl, 16)

            @block.tensor
            def _(pe):
                pe.wait_ge(cl, 16)
                for u in range(T * 4):
                    t, gr = u // 4, u % 4
                    if u >= 4:
                        pe.wait_ge(r1[u % 2], (u - 4) // 2 + 1)
                    for a in range(2):
                        last = nc.tensor.matmul(g.ps[:, u % 4, :], hT[:, 2 * gr + a, t * P:(t + 1) * P], dch[:, a, :], start=a == 0, stop=a == 1)
                    last.then_inc(p1, 1)
                pe.wait_ge(sl, 64)
                for s in range(2):
                    pe.wait_ge(r1[s], T * 2)
                for c in range(KT):
                    wait(pe, fr, 2 * (c - 1))
                    for par in range(2):
                        for n in range(8):
                            t, cs = n // 2, n % 2
                            last = nc.tensor.matmul(g.ps[:, 4 + 2 * (c % 2) + par, :], ab[:, 4 * par + t, cs, c * P:(c + 1) * P], dsq[:, par, cs, t, :],
                                                    start=n == 0, stop=n == 7)
                    last.then_inc(p2, 1)

            @block.scalar
            def _(act):
                for u in range(0, T * 4, 2):
                    t, gr = u // 4, u % 4
                    act.wait_ge(p1, u + 1)
                    nc.scalar.activation(ab[:, t, :, gr * 256:(gr + 1) * 256], g.ps[:, u % 4, :].rearrange("p (a n) -> p a n", a=2), ACT.Copy).then_inc(r1[0], 1)
                for c in range(KT):
                    act.wait_ge(p2, c + 1)
                    wait(act, fr, 2 * (c - 1))
                    nc.scalar.activation(ev[:, c % 2, :], g.ps[:, 4 + 2 * (c % 2), :], ACT.Copy).then_inc(er, 1)

            @block.vector
            def _(dve):
                for u in range(1, T * 4, 2):
                    t, gr = u // 4, u % 4
                    dve.wait_ge(p1, u + 1)
                    nc.vector.tensor_copy(ab[:, t, :, gr * 256:(gr + 1) * 256], g.ps[:, u % 4, :].rearrange("p (a n) -> p a n", a=2)).then_inc(r1[1], 1)
                for c in range(KT):
                    dve.wait_ge(er, c + 1)
                    for n, op in enumerate((ALU.add, ALU.subtract)):
                        tt(nc.vector, fT[:, c, n * HALF:(n + 1) * HALF], ev[:, c % 2, :], g.ps[:, 5 + 2 * (c % 2), :], op).then_inc(fr, 1)


class Shared:
    pass


@contextmanager
def stage(nc):
    before = nc.snapshot_sems()
    yield
    nc.clear_and_free_semaphores(nc.allocated_since(before))
    nc.all_engine_barrier()


def build(nc, io):
    with ExitStack() as ctx:
        g = Shared()
        g.io = io
        g.sem = lambda name: nc.alloc_semaphore(name=name)
        sb = lambda n, s, d=F32: ctx.enter_context(nc.sbuf_tensor(n, s, d))
        g.slots = nc.dram_tensor("slots", (SLOT_BLOCKS * P, D), F32, kind="Internal").ap()
        g.ps = ctx.enter_context(nc.psum_tensor("ps", [P, 8, HALF], F32))
        g.x = sb("x_sb", [P, T, D])
        g.ident, g.masks, g.small = sb("ident", [P, P]), sb("masks", [P, 5 * P + 2]), sb("small", [P, 120])
        g.vecs, g.dtb, g.dskip = sb("vecs", [P, 44]), sb("dt_bias_a", [P, 32]), sb("dskip", [P, 8])
        g.neglam, g.qscale, g.negslope = sb("neg_lambda", [P, 1]), sb("qscale", [P, HEADS]), sb("neg_slopes", [P, HEADS])
        g.mhalf = sb("minus_half", [P, T])
        g.gates, g.slot_i = sb("gates", [P, 2, T]), sb("slot_i", [P, 2, T], I32)
        g.block_expert, g.last_pair = sb("block_expert", [1, MAX_BLOCKS], I32), sb("last_pair", [1, 1], I32)
        g.x_loaded, g.slots_cleared = g.sem("x_loaded"), g.sem("slots_cleared")

        with stage(nc):
            load_constants(nc, g)
        with ExitStack() as c0:
            sc = lambda n, s: c0.enter_context(nc.sbuf_tensor(n, s, F32))
            hT, mixed = sc("hT_mix0", [P, KT, SEQ]), sc("mixed", [P, T, D])
            with nc.sbuf_tensor("h_mix0", [P, 2, D], F32) as h:
                with stage(nc):
                    norm_transpose(nc, g, "mix0", io["norm_mix"][0], hT, h, order_natural, False, first=True)
            with ExitStack() as c1:
                s1 = lambda n, s: c1.enter_context(nc.sbuf_tensor(n, s, F32))
                xbcT, xs, draw = s1("xbcT", [P, XBC_T, SEQ + 4]), s1("xs", [P, T, 640]), s1("dt_raw", [P, T, 16])
                with stage(nc):
                    ssd_project(nc, g, hT, xbcT, xs, mixed, draw)
                with stage(nc):
                    ssd_scan(nc, g, xbcT, xs, mixed, draw)
            with stage(nc):
                attention(nc, g, hT, mixed)
            with stage(nc):
                project_out(nc, g, "out0", mixed, hT, io["w_out"][0], g.vecs)
        for layer in range(2):
            if layer == 1:
                with nc.sbuf_tensor("hT_mix1", [P, KT, SEQ], F32) as hT:
                    with nc.sbuf_tensor("h_mix1", [P, 2, D], F32) as h:
                        with stage(nc):
                            norm_transpose(nc, g, "mix1", io["norm_mix"][1], hT, h, order_tile, True)
                    with stage(nc):
                        fourier(nc, g, hT, hT)
                    with stage(nc):
                        project_out(nc, g, "out1", None, hT, io["w_fourier"][0], None)
            with nc.sbuf_tensor(f"hT_ffn{layer}", [P, KT, SEQ], F32) as hT, nc.sbuf_tensor(f"h_ffn{layer}", [P, T, D], F32) as h:
                with stage(nc):
                    norm_transpose(nc, g, f"ffn{layer}", io["norm_ffn"][layer], hT, h, order_tile, False)
                with stage(nc):
                    route(nc, g, layer, hT, h)
            with stage(nc):
                experts(nc, g, layer)
            with stage(nc):
                combine(nc, g, layer, layer == 1)


_INS = ['x', 'norm_mix', 'norm_ffn', 'w_in', 'q_norm', 'k_norm', 'lambda_q1', 'lambda_k1', 'lambda_q2', 'lambda_k2',
        'attn_subln', 'conv_w', 'conv_b', 'dt_bias', 'a_log', 'd_skip', 'ssd_norm', 'w_out', 'w_fourier',
        'router_group_w', 'router_group_b', 'router_expert_w', 'router_expert_b', 'expert_w1', 'expert_w3', 'expert_w2']


def shape_constants():
    import numpy as np
    k, n = np.arange(P)[:, None], np.arange(P)[None, :]
    masks = np.concatenate([k <= n, k > n, k >= n, k < n, np.ones((P, P), bool), k < 64, k >= 64], axis=1).astype(np.float32)
    small = np.concatenate([np.arange(32), np.arange(32) // PER_GROUP, np.arange(MAX_BLOCKS), np.arange(8) * P]).astype(np.float32)
    negdist = -np.abs(k + 896 - np.arange(1920)[None, :]).astype(np.float32)
    d = np.arange(256)
    ang = 2 * np.pi * ((d[:, None] * d[None, :]) % 256) / 256
    channels = (np.concatenate([np.cos(ang), np.sin(ang)], axis=1) / 512.0).astype(np.float32)
    tokens = []
    for par in range(2):
        ang = 2 * np.pi * (((2 * np.arange(512) + par)[:, None] * np.arange(512)[None, :]) % 1024) / 1024
        tokens.append(np.stack([np.cos(ang), -np.sin(ang)]))
    return {"c_ident": np.eye(P, dtype=np.float32), "c_masks": masks, "c_small": small, "c_negdist": negdist,
            "c_dft_channels": channels, "c_dft_tokens": np.stack(tokens).astype(np.float32)}


def kernel(**inputs):
    import numpy as _np
    import concourse.bacc as _bacc
    from concourse.bass_utils import run_bass_kernel_spmd as _run

    nc = _bacc.Bacc("TRN2", target_bir_lowering=False, num_devices=1)
    arrays, io = {}, {}
    for name, a in {**{n: inputs[n] for n in _INS}, **shape_constants()}.items():
        a = _np.ascontiguousarray(a)
        arrays[f"in_{name}"] = a
        io[name] = nc.dram_tensor(f"in_{name}", a.shape, F32, kind="ExternalInput").ap()
    io["out"] = nc.dram_tensor("out_0", (1, SEQ, D), F32, kind="ExternalOutput").ap()
    build(nc, io)
    r = _run(nc, [arrays], core_ids=[0])
    return r.results[0]["out_0"]
```

```python
from contextlib import ExitStack, contextmanager

import concourse.bass as bass
from concourse import mybir

F32 = mybir.dt.float32
F32R = mybir.dt.float32r
I32 = mybir.dt.int32
U32 = mybir.dt.uint32
ALU = mybir.AluOpType
ACT = mybir.ActivationFunctionType
AX = mybir.AxisListType.X

P = 128
D = 1024
SEQ = 1024
T = SEQ // P
KT = D // P
HALF = 512
HEADS = 4
QK = 64
VD = 128
SSD_H = 8
SSD_W = 512
XBC = 768
XBC_T = XBC // P
CONV = 5
COL_V, COL_Z, COL_XBC, COL_DT = 1024, 1536, 2048, 2816
EXPERTS = 32
GROUPS = 4
GROUPS_F = 4
PER_GROUP = EXPERTS // GROUPS
HID = 256
MAX_BLOCKS = EXPERTS + 2 * SEQ // P
SLOT_BLOCKS = MAX_BLOCKS + 3
BIG = 1.0e30
EPS = 1e-6
SLOPES = [2.0 ** (-8.0 * (h + 1) / HEADS) for h in range(HEADS)]
LAMBDA_INIT = 0.8 - 0.6
EMPTY = 1 << 20
ROW_CONVW, ROW_CONVB, ROW_SSDN, ROW_SUBLN, ROW_QN, ROW_KN, N_ROWS = 0, 30, 36, 40, 41, 42, 43
M_LE, M_GT, M_GE, M_LT, M_ONE = range(5)


class Shared:
    pass


def wait(eng, sem, value):
    if isinstance(value, int) and value <= 0:
        return
    eng.wait_ge(sem, value)


class Chain:

    def __init__(self, eng, sem):
        self.eng, self.sem, self.n = eng, sem, 0

    def __call__(self, ins):
        ins.then_inc(self.sem, 1)
        self.n = self.n + 1
        self.eng.wait_ge(self.sem, self.n)


def tt(e, out, a, b, op):
    return e.tensor_tensor(out=out, in0=a, in1=b, op=op)


def load_constants(nc, g):
    io = g.io
    with ExitStack() as ctx:
        rows = ctx.enter_context(nc.sbuf_tensor("rows", [P, P], F32))
        lam4 = ctx.enter_context(nc.sbuf_tensor("lam4", [P, 4, QK], F32))
        lamp = ctx.enter_context(nc.sbuf_tensor("lamp", [P, 2, QK], F32))
        lams = ctx.enter_context(nc.sbuf_tensor("lams", [P, 2], F32))
        cst, rowl = g.sem("constants_loaded"), g.sem("vector_rows_loaded")
        zs, rt = g.sem("minus_half_ready"), g.sem("rows_transposed")
        ds, ls, es = g.sem("dve_const_step"), g.sem("lambda_sums_ready"), g.sem("lambda_exps_ready")
        n_cst = 9
        with nc.Block() as block:
            @block.sync
            def _(sp):
                sp.dma_start(g.ident[:], io["c_ident"]).then_inc(cst, 16)
                sp.dma_start(g.masks[:], io["c_masks"]).then_inc(cst, 16)
                sp.dma_start(g.small[:], io["c_small"].partition_broadcast(P)).then_inc(cst, 16)
                sp.dma_start(g.ids[:], io["c_ids"]).then_inc(cst, 16)
                for t in range(T):
                    sp.dma_start(g.x[:, t, :], io["x"][t * P:(t + 1) * P, :]).then_inc(g.x_loaded, 16)

            @block.scalar
            def _(act):
                act.dma_start(rows[0:30, :], io["conv_w"][0].rearrange("k (c p) -> (k c) p", p=P)).then_inc(rowl, 16)
                act.dma_start(rows[30:36, :], io["conv_b"][0].rearrange("(c p) -> c p", p=P)).then_inc(rowl, 16)
                act.dma_start(rows[36:40, :], io["ssd_norm"][0].rearrange("(c p) -> c p", p=P)).then_inc(rowl, 16)
                act.dma_start(rows[40:41, :], io["attn_subln"]).then_inc(rowl, 16)
                for c in range(2):
                    act.dma_start(rows[41:42, c * QK:(c + 1) * QK], io["q_norm"]).then_inc(rowl, 16)
                    act.dma_start(rows[42:43, c * QK:(c + 1) * QK], io["k_norm"]).then_inc(rowl, 16)
                act.dma_start(g.dtb[:, 0:16], io["dt_bias"][0].rearrange("a h -> (a h)").partition_broadcast(P)).then_inc(cst, 16)
                act.dma_start(g.dtb[:, 16:32], io["a_log"][0].rearrange("a h -> (a h)").partition_broadcast(P)).then_inc(cst, 16)
                act.dma_start(g.dskip[:], io["d_skip"][0].partition_broadcast(P)).then_inc(cst, 16)
                for n, name in enumerate(("lambda_q1", "lambda_k1", "lambda_q2", "lambda_k2")):
                    if n < 2:
                        act.dma_start(lam4[:, n, :], io[name][0].partition_broadcast(P)).then_inc(cst, 16)
                    else:
                        act.dma_start(lam4[:, n, :], io[name][0].partition_broadcast(P)).then_inc(rowl, 16)
                act.wait_ge(ls, 1)
                nc.scalar.activation(lams[:], lams[:], ACT.Exp).then_inc(es, 1)
                act.wait_ge(cst, 16 * n_cst)
                nc.scalar.activation(g.dtb[:, 16:32], g.dtb[:, 16:32], ACT.Exp).then_inc(es, 1)

            @block.gpsimd
            def _(pool):
                nc.gpsimd.memset(g.mhalf[:], -0.5).then_inc(zs, 1)
                pool.wait_ge(zs, 1)

            @block.tensor
            def _(pe):
                pe.wait_ge(rowl, 16 * 10)
                pe.wait_ge(cst, 16 * n_cst)
                nc.tensor.transpose(g.ps[:, 0, 0:N_ROWS], rows[0:N_ROWS, :], g.ident[0:N_ROWS, 0:N_ROWS]).then_inc(rt, 1)

            @block.vector
            def _(dve):
                step = Chain(dve, ds)
                dve.wait_ge(rowl, 16 * 10)
                dve.wait_ge(cst, 16 * n_cst)
                step(tt(nc.vector, lamp[:, 0, :], lam4[:, 0, :], lam4[:, 1, :], ALU.mult))
                step(tt(nc.vector, lamp[:, 1, :], lam4[:, 2, :], lam4[:, 3, :], ALU.mult))
                nc.vector.tensor_reduce(out=lams[:], in_=lamp[:], axis=AX, op=ALU.add).then_inc(ls, 1)
                dve.wait_ge(es, 2)
                step(tt(nc.vector, g.neglam[:], lams[:, 1:2], lams[:, 0:1], ALU.subtract))
                step(nc.vector.tensor_scalar(g.neglam[:], g.neglam[:], -LAMBDA_INIT, None, ALU.add))
                step(nc.vector.tensor_scalar(g.dtb[:, 16:32], g.dtb[:, 16:32], -1.0, None, ALU.mult))
                dve.wait_ge(rt, 1)
                step(nc.vector.tensor_copy(g.vecs[:, 0:N_ROWS], g.ps[:, 0, 0:N_ROWS]))
                for h in range(HEADS):
                    step(nc.vector.tensor_scalar(g.qscale[:, h:h + 1], g.vecs[:, ROW_QN:ROW_QN + 1],
                                                 QK ** -0.5 / SLOPES[h], None, ALU.mult))
                    step(nc.vector.memset(g.negslope[:, h:h + 1], -SLOPES[h]))
                step(nc.vector.tensor_scalar(g.vecs[:, ROW_SUBLN:ROW_SUBLN + 1], g.vecs[:, ROW_SUBLN:ROW_SUBLN + 1],
                                             1.0 - LAMBDA_INIT, None, ALU.mult))


def norm_transpose(nc, g, tag, gain, hT, h, order, blocked, first=False, stored=None, weights=None):
    slots = h.shape[1]
    with ExitStack() as ctx:
        sb = lambda n, s: ctx.enter_context(nc.sbuf_tensor(f"{n}_{tag}", s, F32))
        gb, junk, ss, rs = sb("gain_b", [P, D]), sb("squares", [P, D]), sb("sumsq", [P, T]), sb("rstd", [P, T])
        gl, ssr, rsr = g.sem(f"gain_loaded_{tag}"), g.sem(f"sumsq_ready_{tag}"), g.sem(f"rstd_step_{tag}")
        hr, tr = g.sem(f"h_ready_{tag}"), g.sem(f"h_transposed_{tag}")
        ea, ed = g.sem(f"hT_low_ready_{tag}"), g.sem(f"hT_high_ready_{tag}")
        with nc.Block() as block:
            @block.sync
            def _(sp):
                sp.dma_start(gb[:], gain.partition_broadcast(P)).then_inc(gl, 16)
                if weights is not None:
                    for s in range(2):
                        for n in range(2):
                            load_w13(sp, weights, n, s, s)
                    load_w2(sp, weights, 0, 0)
                if stored is not None:
                    for t in range(T):
                        sp.wait_ge(hr, t + 1)
                        sp.dma_start(g.h_rows[t * P:(t + 1) * P, :], h[:, t, :]).then_inc(stored, 16)

            @block.scalar
            def _(act):
                def squares(t):
                    if first:
                        act.wait_ge(g.x_loaded, 16 * T)
                    wait(act, ssr, t)
                    nc.scalar.activation(junk[:], g.x[:, t, :], ACT.Square, accum_out=ss[:, t:t + 1]).then_inc(ssr, 1)

                squares(0)
                squares(1)
                for t in range(T):
                    if t + 2 < T:
                        squares(t + 2)
                    act.wait_ge(tr, t + 1)
                    for dst, src in order(t):
                        last = nc.scalar.activation(hT[:, 0:4, dst], g.ps[:, 2 * (t % 2), :].rearrange("p (j n) -> p j n", n=P)[:, :, src], ACT.Copy)
                    last.then_inc(ea, 1)

            @block.gpsimd
            def _(pool):
                for t in range(T):
                    pool.wait_ge(ssr, t + 1)
                    nc.gpsimd.tensor_scalar(rs[:, t:t + 1], ss[:, t:t + 1], 1.0 / D, EPS, ALU.mult, ALU.add).then_inc(rsr, 1)
                    pool.wait_ge(rsr, 2 * t + 1)
                    tt(nc.gpsimd, rs[:, t:t + 1], rs[:, t:t + 1], g.mhalf[:, 0:1], ALU.pow).then_inc(rsr, 1)

            @block.vector
            def _(dve):
                dve.wait_ge(gl, 16)
                if first:
                    dve.wait_ge(g.x_loaded, 16 * T)

                def normed(t):
                    dve.wait_ge(rsr, 2 * t + 2)
                    if slots < T:
                        wait(dve, tr, t - slots + 1)
                    nc.vector.scalar_tensor_tensor(out=h[:, t % slots, :], in0=g.x[:, t, :], scalar=rs[:, t:t + 1], in1=gb[:],
                                                   op0=ALU.mult, op1=ALU.mult).then_inc(hr, 1)

                normed(0)
                for t in range(T):
                    if t + 1 < T:
                        normed(t + 1)
                    dve.wait_ge(tr, t + 1)
                    for dst, src in order(t):
                        last = nc.vector.tensor_copy(hT[:, 4:8, dst], g.ps[:, 2 * (t % 2) + 1, :].rearrange("p (j n) -> p j n", n=P)[:, :, src])
                    last.then_inc(ed, 1)

            @block.tensor
            def _(pe):
                for t in range(T):
                    pe.wait_ge(hr, t + 1)
                    wait(pe, ea, t - 1)
                    wait(pe, ed, t - 1)
                    hv = h[:, t % slots, :]
                    for j in range(KT):
                        src = hv[:, j * P:(j + 1) * P] if blocked else hv.rearrange("p (q j) -> p j q", j=KT)[:, j, :]
                        last = nc.tensor.transpose(g.ps[:, 2 * (t % 2) + j // 4, (j % 4) * P:(j % 4 + 1) * P], src, g.ident[:])
                    last.then_inc(tr, 1)


def order_mirrored(t):
    if t < 4:
        return [(slice(t * P, (t + 1) * P), slice(0, P))]
    a = (11 - t) * P + 1
    if t > 4:
        return [(slice(a, a + P), slice(None, None, -1))]
    return [(slice(a, a + P - 1), slice(P - 1, 0, -1)), (slice(HALF, HALF + 1), slice(0, 1))]


def order_same(t):
    return [(slice(t * P, (t + 1) * P), slice(0, P))]


def ssd_project(nc, g, hT, xbcT, xs, mixed, draw):
    io = g.io
    w_in = io["w_in"][0].rearrange("(p j) n -> p j n", j=KT)
    with ExitStack() as ctx:
        sb = lambda n, s: ctx.enter_context(nc.sbuf_tensor(n, s, F32))
        wx, wz, wd = sb("w_xbc", [P, KT, XBC]), sb("w_z", [P, KT, HALF]), sb("w_dt", [P, KT, 16])
        acc = sb("conv_acc", [P, 2, SEQ])
        wl, pr, ev = g.sem("w_xbc_loaded"), g.sem("ssd_unit_ready"), g.sem("ssd_unit_read")
        wzl, pads = g.sem("w_z_loaded"), g.sem("conv_pads_ready")
        cs, cv, sl, xt, xe = g.sem("conv_step"), g.sem("conv_ready"), g.sem("silu_ready"), g.sem("x_transposed"), g.sem("x_by_token_ready")
        NX = 2 * XBC_T
        with nc.Block() as block:
            @block.sync
            def _(sp):
                sp.dma_start(wx[:], w_in[:, :, COL_XBC:COL_XBC + XBC]).then_inc(wl, 16)
                sp.dma_start(wz[:], w_in[:, :, COL_Z:COL_Z + HALF]).then_inc(wzl, 16)
                sp.dma_start(wd[:], w_in[:, :, COL_DT:COL_DT + 16]).then_inc(wzl, 16)

            @block.gpsimd
            def _(pool):
                nc.gpsimd.memset(xbcT[:, :, 0:2], 0.0).then_inc(pads, 1)
                nc.gpsimd.memset(xbcT[:, :, SEQ + 2:SEQ + 4], 0.0).then_inc(pads, 1)

            @block.tensor
            def _(pe):
                pe.wait_ge(wl, 16)
                for u in range(NX):
                    ct, half = u // 2, u % 2
                    wait(pe, ev, u - 3)
                    for j in range(KT):
                        last = nc.tensor.matmul(g.ps[:, u % 4, :], wx[:, j, ct * P:(ct + 1) * P],
                                                hT[:, j, half * HALF:(half + 1) * HALF], start=j == 0, stop=j == KT - 1)
                    last.then_inc(pr, 1)
                pe.wait_ge(wzl, 32)
                for t in range(T):
                    u = NX + t
                    wait(pe, ev, u - 3)
                    for j in range(KT):
                        last = nc.tensor.matmul(g.ps[:, u % 4, :], hT[:, j, t * P:(t + 1) * P], wz[:, j, :], start=j == 0, stop=j == KT - 1)
                    last.then_inc(pr, 1)
                u = NX + T
                pe.wait_ge(ev, u - 3)
                for t in range(T):
                    for j in range(KT):
                        last = nc.tensor.matmul(g.ps[:, u % 4, t * 16:(t + 1) * 16], hT[:, j, t * P:(t + 1) * P], wd[:, j, :],
                                                start=j == 0, stop=j == KT - 1)
                last.then_inc(pr, 1)
                for c in range(T):
                    pe.wait_ge(sl, 5)
                    wait(pe, xe, c - 1)
                    for ct in range(5):
                        last = nc.tensor.transpose(g.ps[:, 4 + 2 * (c % 2) + ct // 4, (ct % 4) * P:(ct % 4 + 1) * P],
                                                   xbcT[:, ct, c * P:(c + 1) * P], g.ident[:])
                    last.then_inc(xt, 1)

            @block.scalar
            def _(act):
                for u in range(NX):
                    ct, half = u // 2, u % 2
                    act.wait_ge(pr, u + 1)
                    nc.scalar.activation(xbcT[:, ct, 2 + half * HALF:2 + (half + 1) * HALF], g.ps[:, u % 4, :], ACT.Copy).then_inc(ev, 1)
                done = 0
                for t in range(T):
                    u = NX + t
                    act.wait_ge(pr, u + 1)
                    nc.scalar.activation(mixed[:, t, SSD_W:], g.ps[:, u % 4, :], ACT.Silu).then_inc(ev, 1)
                    if t >= 2 and done < XBC_T:
                        act.wait_ge(cv, done + 1)
                        nc.scalar.activation(xbcT[:, done, 0:SEQ], acc[:, done % 2, :], ACT.Silu).then_inc(sl, 1)
                        done += 1
                act.wait_ge(pr, NX + T + 1)
                nc.scalar.activation(draw[:], g.ps[:, (NX + T) % 4, 0:P].rearrange("p (t n) -> p t n", n=16), ACT.Copy).then_inc(ev, 1)
                assert done == XBC_T
                for c in range(T):
                    act.wait_ge(xt, c + 1)
                    nc.scalar.activation(xs[:, c, 0:640], g.ps[:, 4 + 2 * (c % 2):6 + 2 * (c % 2), :].rearrange("p a n -> p (a n)")[:, 0:640],
                                         ACT.Copy).then_inc(xe, 1)

            @block.vector
            def _(dve):
                step = Chain(dve, cs)
                dve.wait_ge(pads, 2)
                for ct in range(XBC_T):
                    dve.wait_ge(ev, 2 * ct + 2)
                    wait(dve, sl, ct - 1)
                    a = acc[:, ct % 2, :]
                    w = lambda k: g.vecs[:, ROW_CONVW + k * XBC_T + ct:ROW_CONVW + k * XBC_T + ct + 1]
                    step(nc.vector.tensor_scalar(a, xbcT[:, ct, 0:SEQ], w(0), g.vecs[:, ROW_CONVB + ct:ROW_CONVB + ct + 1], ALU.mult, ALU.add))
                    for k in range(1, CONV):
                        ins = nc.vector.scalar_tensor_tensor(out=a, in0=xbcT[:, ct, k:k + SEQ], scalar=w(k), in1=a, op0=ALU.mult, op1=ALU.add)
                        if k < CONV - 1:
                            step(ins)
                    ins.then_inc(cv, 1)
                    dve.wait_ge(cv, ct + 1)


def ssd_scan(nc, g, xbcT, xs, mixed, draw):
    NC = T
    with ExitStack() as ctx:
        sb = lambda n, s: ctx.enter_context(nc.sbuf_tensor(n, s, F32))
        dt, a = sb("dt", [P, NC, 16]), sb("dta", [P, NC, 16])
        r1, r2 = sb("dt_pos", [P, NC, 16]), sb("dt_abs", [P, NC, 16])
        ex = sb("decays", [P, 384])
        bz = sb("b_by_group", [P, 2, SEQ])
        half_mask = lambda gr: g.masks[:, 5 * P + gr:5 * P + gr + 1]
        am = sb("a_masked", [P, 2, SSD_H, P])
        lm = sb("l_mat", [P, 2, SSD_H, P])
        cb = sb("cb_masked", [P, 2, 2, P])
        xd = sb("x_dt", [P, 2, SSD_W])
        xw = sb("x_decayed", [P, 2, SSD_W])
        st = sb("state", [P, 2, SSD_W])
        off = sb("y_off", [P, SSD_W])
        y = sb("y", [P, NC, SSD_W])
        ss, rs = sb("ssd_sumsq", [P, NC]), sb("ssd_rstd", [P, NC])
        dtm = [g.sem(f"softplus_{n}") for n in ("in", "exp", "ln")]
        ar, cum, exr = g.sem("dta_ready"), g.sem("cumsums_ready"), g.sem("decays_ready")
        vs, psd = g.sem("dve_ssd_step"), g.sem("pool_ssd_step")
        amr, seg, lr, mr = g.sem("a_masked_ready"), g.sem("segsum_ready"), g.sem("l_exp_ready"), g.sem("m_ready")
        cbr, yd, ydr = g.sem("cb_ready"), g.sem("y_diag_ready"), g.sem("y_diag_added")
        xdr, xwr, inc, inr = g.sem("x_dt_ready"), g.sem("x_decayed_ready"), g.sem("state_inc_ready"), g.sem("state_updated")
        yo, yor, cbu = g.sem("y_off_ready"), g.sem("y_off_added"), g.sem("cb_read")
        yg, sq, fin = g.sem("y_gated"), g.sem("ssd_squares_ready"), g.sem("ssd_rstd_step")
        y0 = g.sem("y_skip_ready")
        bzr = g.sem("b_by_group_ready")
        mask = lambda m: g.masks[:, m * P:(m + 1) * P]
        bh = lambda v: v.unsqueeze(2).to_broadcast([P, SSD_H, 64])
        hv = lambda v: v.rearrange("p (h n) -> p h n", h=SSD_H)
        dirs = lambda i: (i, NC - 1 - i)
        with nc.Block() as block:
            @block.scalar
            def _(act):
                act.wait_ge(dtm[0], 1)
                nc.scalar.activation(r2[:], r2[:], ACT.Exp, scale=-1.0).then_inc(dtm[1], 1)
                act.wait_ge(dtm[1], 1)
                nc.scalar.activation(r2[:], r2[:], ACT.Ln, bias=1.0).then_inc(dtm[2], 1)
                act.wait_ge(cum, 1)
                nc.scalar.activation(ex[:], g.ps[:, 7, 0:384], ACT.Exp).then_inc(exr, 1)
                for i in range(NC):
                    for d in range(2):
                        act.wait_ge(seg, 2 * i + d + 1)
                        wait(act, yd, i)
                        nc.scalar.activation(lm[:, d].rearrange("p h n -> p (h n)"), g.ps[:, 2 * d:2 * d + 2, :].rearrange("p a n -> p (a n)"),
                                             ACT.Exp).then_inc(lr, 1)
                for c in range(NC):
                    act.wait_ge(yg, c + 1)
                    wait(act, sq, c)
                    nc.scalar.activation(off[:], y[:, c, :], ACT.Square, accum_out=ss[:, c:c + 1]).then_inc(sq, 1)

            @block.tensor
            def _(pe):
                pe.wait_ge(ar, 1)
                for n, (m, d) in enumerate(((M_LE, 0), (M_GE, 1), (M_GT, 0), (M_LT, 1))):
                    nc.tensor.matmul(g.ps[:, 7, 64 * n:64 * n + 64], mask(m), a[:, :, 8 * d:8 * d + 8], start=True, stop=True)
                nc.tensor.matmul(g.ps[:, 7, 256:384], mask(M_ONE), a[:].rearrange("p c n -> p (c n)"), start=True, stop=True).then_inc(cum, 1)

                def segsums(i):
                    for d in range(2):
                        pe.wait_ge(amr, 2 * i + d + 1)
                        wait(pe, lr, 2 * i + d - 1)
                        for half in range(2):
                            last = nc.tensor.matmul(g.ps[:, 2 * d + half, :], mask((M_GT, M_LT)[d]),
                                                    am[:, d].rearrange("p h n -> p (h n)")[:, half * HALF:(half + 1) * HALF], start=True, stop=True)
                        last.then_inc(seg, 1)

                segsums(0)
                pe.wait_ge(bzr, 2)
                for i in range(NC):
                    wait(pe, cbu, 2 * i)
                    for gr in range(2):
                        last = nc.tensor.matmul(g.ps[:, 4, gr * P:(gr + 1) * P], bz[:, gr, i * P:(i + 1) * P],
                                                xbcT[:, 5, i * P:(i + 1) * P], start=True, stop=True)
                    last.then_inc(cbr, 1)
                    for d in range(2):
                        c = dirs(i)[d]
                        if i < NC - 1:
                            pe.wait_ge(xwr, 2 * i + d + 1)
                            wait(pe, inr, 2 * i + d)
                            if i == 0 and d == 0:
                                pe.wait_ge(exr, 1)
                            nc.tensor.matmul(g.ps[:, 7, :], xs[:, c, SSD_W:SSD_W + P], xw[:, d, :], start=True, stop=True).then_inc(inc, 1)
                        if i > 0:
                            pe.wait_ge(inr, 2 * (i - 1) + d + 1)
                            wait(pe, yor, 2 * (i - 1) + d)
                            nc.tensor.matmul(g.ps[:, 6, :], xbcT[:, 5, c * P:(c + 1) * P], st[:, d, :], start=True, stop=True).then_inc(yo, 1)
                    if i + 1 < NC:
                        segsums(i + 1)
                    pe.wait_ge(mr, 2 * i + 2)
                    pe.wait_ge(xdr, 2 * i + 2)
                    wait(pe, ydr, i)
                    for h in range(SSD_H):
                        for d in range(2):
                            last = nc.tensor.matmul(g.ps[:, 5, h * 64:h * 64 + 64], lm[:, d, h, :], xd[:, d, h * 64:h * 64 + 64],
                                                    start=d == 0, stop=d == 1)
                    last.then_inc(yd, 1)

            @block.gpsimd
            def _(pool):
                pool.wait_ge(ar, 1)

                def masked(i):
                    for d in range(2):
                        wait(pool, seg, 2 * (i - 1) + d + 1)
                        tt(nc.gpsimd, am[:, d], mask((M_LE, M_GE)[d]).unsqueeze(1).to_broadcast([P, SSD_H, P]),
                           a[:, i, 8 * d:8 * d + 8].unsqueeze(2).to_broadcast([P, SSD_H, P]), ALU.mult).then_inc(amr, 1)

                masked(0)
                for i in range(NC):
                    for d in range(2):
                        wait(pool, yd, i)
                        tt(nc.gpsimd, hv(xd[:, d, :]), hv(xs[:, i, 0:SSD_W]), bh(dt[:, i, 8 * d:8 * d + 8]), ALU.mult).then_inc(xdr, 1)
                    if i + 1 < NC:
                        masked(i + 1)
                for c in range(NC):
                    pool.wait_ge(sq, c + 1)
                    nc.gpsimd.tensor_scalar(rs[:, c:c + 1], ss[:, c:c + 1], 1.0 / SSD_W, EPS, ALU.mult, ALU.add).then_inc(fin, 1)
                    pool.wait_ge(fin, 2 * c + 1)
                    tt(nc.gpsimd, rs[:, c:c + 1], rs[:, c:c + 1], g.mhalf[:, 0:1], ALU.pow).then_inc(fin, 1)

            @block.vector
            def _(dve):
                step = Chain(dve, vs)
                V = nc.vector
                b3 = lambda v: v.unsqueeze(1).to_broadcast([P, NC, 16])
                step(tt(V, r1[:], draw[:], b3(g.dtb[:, 0:16]), ALU.add))
                V.scalar_tensor_tensor(out=r2[:], in0=r1[:], scalar=-1.0, in1=r1[:], op0=ALU.mult, op1=ALU.max).then_inc(dtm[0], 1)
                dve.wait_ge(dtm[0], 1)
                step(V.tensor_scalar(r1[:], r1[:], 0.0, None, ALU.max))
                step(V.memset(st[:], 0.0))
                dve.wait_ge(dtm[2], 1)
                step(tt(V, dt[:], r1[:], r2[:], ALU.add))
                tt(V, a[:], dt[:], b3(g.dtb[:, 16:32]), ALU.mult).then_inc(ar, 1)
                for gr in range(2):
                    V.tensor_scalar(bz[:, gr, :], xbcT[:, 4, 0:SEQ], half_mask(gr), None, ALU.mult).then_inc(bzr, 1)
                for c in range(NC):
                    step(tt(V, hv(y[:, c, :]), hv(xs[:, c, 0:SSD_W]), bh(g.dskip[:]), ALU.mult))
                dve.wait_ge(ar, 1)
                dve.wait_ge(exr, 1)
                e4 = ex[:, 0:256].rearrange("p (q c h) -> p q c h", q=4, h=SSD_H)
                e5 = ex[:, 256:384].rearrange("p (c q) -> p c q", q=16)
                for d in range(2):
                    step(tt(V, e4[:, 2 + d], e4[:, 2 + d], dt[:, :, 8 * d:8 * d + 8], ALU.mult))
                for i in range(NC):
                    if i < NC - 1:
                        for d in range(2):
                            c = dirs(i)[d]
                            wait(dve, inc, 2 * (i - 1) + d + 1)
                            tt(V, hv(xw[:, d, :]), hv(xs[:, c, 0:SSD_W]), bh(e4[:, 2 + d, c]), ALU.mult).then_inc(xwr, 1)
                    dve.wait_ge(cbr, i + 1)
                    wait(dve, mr, 2 * i)
                    for d in range(2):
                        tt(V, cb[:, d], g.ps[:, 4, 0:256].rearrange("p (g n) -> p g n", g=2),
                           mask((M_LE, M_GE)[d]).unsqueeze(1).to_broadcast([P, 2, P]), ALU.mult).then_inc(cbu, 1)
                    dve.wait_ge(cbu, 2 * i + 2)
                    for d in range(2):
                        c = dirs(i)[d]
                        if i > 0:
                            dve.wait_ge(yo, 2 * (i - 1) + d + 1)
                            step(tt(V, hv(off[:]), hv(g.ps[:, 6, :]), bh(e4[:, d, c]), ALU.mult))
                            tt(V, y[:, c, :], y[:, c, :], off[:], ALU.add).then_inc(yor, 1)
                            dve.wait_ge(yor, 2 * (i - 1) + d + 1)
                        if i < NC - 1:
                            step(tt(V, hv(st[:, d, :]), hv(st[:, d, :]), bh(e5[:, c, 8 * d:8 * d + 8]), ALU.mult))
                            dve.wait_ge(inc, 2 * i + d + 1)
                            for gr in range(2):
                                cols = slice(256 * gr, 256 * gr + 256)
                                ins = V.scalar_tensor_tensor(out=st[:, d, cols], in0=g.ps[:, 7, cols], scalar=half_mask(gr), in1=st[:, d, cols],
                                                             op0=ALU.mult, op1=ALU.add)
                            ins.then_inc(inr, 1)
                    for d in range(2):
                        dve.wait_ge(lr, 2 * i + d + 1)
                        for gr in range(2):
                            ins = tt(V, lm[:, d, 4 * gr:4 * gr + 4, :], lm[:, d, 4 * gr:4 * gr + 4, :],
                                     cb[:, d, gr, :].unsqueeze(1).to_broadcast([P, 4, P]), ALU.mult)
                        ins.then_inc(mr, 1)
                    dve.wait_ge(yd, i + 1)
                    tt(V, y[:, i, :], y[:, i, :], g.ps[:, 5, :], ALU.add).then_inc(ydr, 1)
                    dve.wait_ge(ydr, i + 1)
                for c in range(NC):
                    tt(V, y[:, c, :], y[:, c, :], mixed[:, c, SSD_W:], ALU.mult).then_inc(yg, 1)
                for c in range(NC):
                    dve.wait_ge(yg, NC)
                    dve.wait_ge(fin, 2 * c + 2)
                    step(V.tensor_scalar(mixed[:, c, SSD_W:], y[:, c, :], rs[:, c:c + 1], None, ALU.mult))


def attention(nc, g, hT, mixed):
    io = g.io
    w_in = io["w_in"][0].rearrange("(p j) n -> p j n", j=KT)
    with ExitStack() as ctx:
        sb = lambda n, s: ctx.enter_context(nc.sbuf_tensor(n, s, F32))
        w = sb("w_qkv", [P, KT, 3, P])
        qT, kT, v = sb("qT", [P, SEQ]), sb("kT", [P, SEQ]), sb("v", [P, T, VD])
        qk, sq = sb("qk_normed", [P, 2, 256]), sb("qk_squares", [P, 256])
        ss, rs = sb("qk_sumsq", [P, T, 4]), sb("qk_rstd", [P, T, 4])
        dist = sb("negdist", [P, 1920])
        pr = sb("probs", [P, 2, 2, SEQ])
        wt, wtT = sb("weights", [P, 2, SEQ]), sb("weightsT", [P, 2, SEQ])
        mx, den = sb("neg_max", [P, 2, 2]), sb("denoms", [P, T, 2])
        cf, rd = sb("coef", [P, 2]), sb("rdenom", [P, T])
        o, osq = sb("o", [P, T, VD]), sb("o_squares", [P, VD])
        oss, ors = sb("o_sumsq", [P, T]), sb("o_rstd", [P, T])
        nsl, qs = sb("neg_slope_h", [P, 1]), sb("qscale_h", [P, 1])
        dl, wl = g.sem("dist_loaded"), g.sem("w_qkv_loaded")
        pj, vr = g.sem("proj_ready"), g.sem("v_ready")
        sqr, ssr, rsr, nr = g.sem("qk_squares_ready"), g.sem("qk_sumsq_ready"), g.sem("qk_rstd_step"), g.sem("qk_normed_ready")
        tr, tq, tk = g.sem("qk_transposed"), g.sem("qT_ready"), g.sem("kT_ready")
        sr, ng, er = g.sem("scores_ready"), g.sem("neg_scores_ready"), g.sem("exp_ready")
        wr, wtr, wte = g.sem("weights_ready"), g.sem("weights_transposed"), g.sem("weightsT_ready")
        pv, oe, osr, ofs = g.sem("pv_ready"), g.sem("o_read"), g.sem("o_squares_ready"), g.sem("o_rstd_step")
        vs, fin, hd = g.sem("dve_attn_step"), g.sem("o_written"), g.sem("head_scalars_ready")
        seen, seen_p = g.sem("scores_wait_passed"), g.sem("sumsq_wait_passed")
        with nc.Block() as block:
            @block.sync
            def _(sp):
                sp.dma_start(dist[:], io["c_negdist"]).then_inc(dl, 16)

                def load(h):
                    for n in range(3):
                        sp.dma_start(w[:, :, n, :], w_in[:, :, bass.ds(h * P + n * HALF, P)]).then_inc(wl, 16)

                load(0)
                with sp.Fori(1, HEADS) as h:
                    sp.wait_ge(pj, h * T)
                    load(h)

            @block.tensor
            def _(pe):
                def head(h):
                    def transposes(t):
                        pe.wait_ge(nr, h * T + t + 1)
                        wait(pe, tq, h * T + t)
                        wait(pe, tk, h * T + t)
                        for n in range(2):
                            last = nc.tensor.transpose(g.ps[:, 7 - n, 0:P], qk[:, t % 2, n * P:(n + 1) * P], g.ident[:])
                        last.then_inc(tr, 1)

                    pe.wait_ge(wl, 48 * (h + 1))
                    wait(pe, ng, h * 2 * T)
                    wait(pe, oe, h * T)
                    for t in range(T):
                        if t >= 4:
                            pe.wait_ge(nr, h * T + t - 3)
                            pe.wait_ge(vr, h * T + t - 3)
                        for j in range(KT):
                            last = nc.tensor.matmul(g.ps[:, t % 4, 0:384], hT[:, j, t * P:(t + 1) * P],
                                                    w[:, j, :, :].rearrange("p a n -> p (a n)"), start=j == 0, stop=j == KT - 1)
                        last.then_inc(pj, 1)
                        if t >= 1:
                            transposes(t - 1)
                    transposes(T - 1)
                    pe.wait_ge(tq, h * T + T)
                    pe.wait_ge(tk, h * T + T)
                    pe.wait_ge(vr, h * T + T)
                    for u in range(T + 2):
                        if u < T:
                            for c in range(2):
                                if u > 0:
                                    pe.wait_ge(ng, h * 2 * T + 2 * (u - 1) + c + 1)
                                for half in range(2):
                                    last = nc.tensor.matmul(g.ps[:, 2 * c + half, :], qT[64 * c:64 * c + 64, u * P:(u + 1) * P],
                                                            kT[64 * c:64 * c + 64, half * HALF:(half + 1) * HALF], start=True, stop=True)
                                last.then_inc(sr, 1)
                        if 1 <= u <= T:
                            q = u - 1
                            pe.wait_ge(wr, h * T + q + 1)
                            wait(pe, wte, h * T + q)
                            for k in range(T):
                                last = nc.tensor.transpose(g.ps[:, 4 + k // 4, (k % 4) * P:(k % 4 + 1) * P], wt[:, q % 2, k * P:(k + 1) * P], g.ident[:])
                            last.then_inc(wtr, 1)
                        if u >= 2:
                            q = u - 2
                            pe.wait_ge(wte, h * T + q + 1)
                            wait(pe, oe, h * T + q)
                            for k in range(T):
                                last = nc.tensor.matmul(g.ps[:, 6, 0:VD], wtT[:, q % 2, k * P:(k + 1) * P], v[:, k, :], start=k == 0, stop=k == T - 1)
                            last.then_inc(pv, 1)

                head(0)
                with pe.Fori(1, HEADS) as h:
                    head(h)

            @block.scalar
            def _(act):
                def head(h):
                    wait(act, pv, h * T)
                    for t in range(T):
                        act.wait_ge(pj, h * T + t + 1)
                        wait(act, ssr, h * T + t)
                        nc.scalar.activation(sq[:], g.ps[:, t % 4, 0:256], ACT.Square).then_inc(sqr, 1)
                        nc.scalar.activation(v[:, t, :], g.ps[:, t % 4, 256:384], ACT.Copy).then_inc(vr, 1)
                        act.wait_ge(tr, h * T + t + 1)
                        nc.scalar.activation(kT[:, t * P:(t + 1) * P], g.ps[:, 6, 0:P], ACT.Copy,
                                             scale=g.vecs[:, ROW_KN:ROW_KN + 1]).then_inc(tk, 1)
                    for u in range(T + 2):
                        if u < T:
                            for c in range(2):
                                act.wait_ge(ng, h * 2 * T + 2 * u + c + 1)
                                p = pr[:, u % 2, c, :]
                                nc.scalar.activation(p, p, ACT.Exp, scale=-1.0, bias=mx[:, u % 2, c:c + 1],
                                                     accum_out=den[:, u, c:c + 1]).then_inc(er, 1)
                        if 1 <= u <= T:
                            q = u - 1
                            act.wait_ge(wtr, h * T + q + 1)
                            if q >= 2:
                                act.wait_ge(pv, h * T + q - 1)
                            nc.scalar.activation(wtT[:, q % 2, :], g.ps[:, 4:6, :].rearrange("p a n -> p (a n)"), ACT.Copy).then_inc(wte, 1)
                        if u >= 2:
                            q = u - 2
                            act.wait_ge(pv, h * T + q + 1)
                            wait(act, fin, h)
                            nc.scalar.activation(o[:, q, :], g.ps[:, 6, 0:VD], ACT.Copy, scale=rd[:, q:q + 1]).then_inc(oe, 1)
                            act.wait_ge(oe, h * T + q + 1)
                            wait(act, osr, h * T + q)
                            nc.scalar.activation(osq[:], o[:, q, :], ACT.Square, accum_out=oss[:, q:q + 1]).then_inc(osr, 1)

                head(0)
                with act.Fori(1, HEADS) as h:
                    head(h)

            @block.gpsimd
            def _(pool):
                def head(h):
                    for t in range(T):
                        pool.wait_ge(ssr, h * T + t + 1)
                        wait(pool, nr, h * T + t)
                        pool.sem_inc(seen_p, 1)
                        nc.gpsimd.tensor_scalar(rs[:, t, :], ss[:, t, :], 1.0 / QK, EPS, ALU.mult, ALU.add).then_inc(rsr, 1)
                        pool.wait_ge(rsr, h * 2 * T + 2 * t + 1)
                        tt(nc.gpsimd, rs[:, t, :], rs[:, t, :], g.mhalf[:, 0:4], ALU.pow).then_inc(rsr, 1)
                    pool.wait_ge(osr, h * T + T)
                    pool.sem_inc(seen_p, 1)
                    nc.gpsimd.tensor_scalar(ors[:], oss[:], 1.0 / VD, EPS, ALU.mult, ALU.add).then_inc(ofs, 1)
                    pool.wait_ge(ofs, 2 * h + 1)
                    tt(nc.gpsimd, ors[:], ors[:], g.mhalf[:, 0:T], ALU.pow).then_inc(ofs, 1)

                head(0)
                with pool.Fori(1, HEADS) as h:
                    head(h)

            @block.vector
            def _(dve):
                V = nc.vector
                step = Chain(dve, vs)
                dve.wait_ge(dl, 16)

                def head(h):
                    wait(dve, ng, h * 2 * T)
                    V.tensor_copy(nsl[:], g.negslope[:, bass.ds(h, 1)]).then_inc(hd, 1)
                    V.tensor_copy(qs[:], g.qscale[:, bass.ds(h, 1)]).then_inc(hd, 1)
                    dve.wait_ge(hd, 2 * h + 2)

                    def normed(t):
                        dve.wait_ge(rsr, h * 2 * T + 2 * t + 2)
                        dve.wait_ge(vr, h * T + t + 1)
                        if t >= 2:
                            dve.wait_ge(tr, h * T + t - 1)
                        tt(V, qk[:, t % 2, :].rearrange("p (a n) -> p a n", n=QK), g.ps[:, t % 4, 0:256].rearrange("p (a n) -> p a n", n=QK),
                           rs[:, t, :].unsqueeze(2).to_broadcast([P, 4, QK]), ALU.mult).then_inc(nr, 1)

                    def q_out(t):
                        dve.wait_ge(tr, h * T + t + 1)
                        V.tensor_scalar(qT[:, t * P:(t + 1) * P], g.ps[:, 7, 0:P], qs[:, 0:1], None, ALU.mult).then_inc(tq, 1)

                    for t in range(T):
                        dve.wait_ge(sqr, h * T + t + 1)
                        V.tensor_reduce(out=ss[:, t, :], in_=sq[:].rearrange("p (a n) -> p a n", n=QK), axis=AX, op=ALU.add).then_inc(ssr, 1)
                        normed(t)
                        q_out(t)
                    for u in range(T):
                        for c in range(2):
                            if u >= 2:
                                dve.wait_ge(wr, h * T + u - 1)
                            dve.wait_ge(sr, h * 2 * T + 2 * u + c + 1)
                            dve.sem_inc(seen, 1)
                            V.tensor_tensor_reduce(out=pr[:, u % 2, c, :], in0=g.ps[:, 2 * c:2 * c + 2, :].rearrange("p a n -> p (a n)"),
                                                   in1=dist[:, 896 - u * P:896 - u * P + SEQ], scale=nsl[:, 0:1], scalar=3.0e38,
                                                   op0=ALU.add, op1=ALU.min, accum_out=mx[:, u % 2, c:c + 1]).then_inc(ng, 1)
                        dve.wait_ge(er, h * 2 * T + 2 * u + 2)
                        base = h * 3 * T + 3 * u
                        V.reciprocal(cf[:], den[:, u, :]).then_inc(vs, 1)
                        dve.wait_ge(vs, base + 1)
                        V.tensor_copy(rd[:, u:u + 1], cf[:, 0:1]).then_inc(vs, 1)
                        V.scalar_tensor_tensor(out=cf[:, 1:2], in0=den[:, u, 0:1], scalar=g.neglam[:, 0:1], in1=cf[:, 1:2],
                                               op0=ALU.mult, op1=ALU.mult).then_inc(vs, 1)
                        dve.wait_ge(vs, base + 3)
                        if u >= 2:
                            dve.wait_ge(wtr, h * T + u - 1)
                        V.scalar_tensor_tensor(out=wt[:, u % 2, :], in0=pr[:, u % 2, 1, :], scalar=cf[:, 1:2], in1=pr[:, u % 2, 0, :],
                                               op0=ALU.mult, op1=ALU.add).then_inc(wr, 1)
                        dve.wait_ge(wr, h * T + u + 1)
                    dve.wait_ge(ofs, 2 * h + 2)
                    tt(V, mixed[:, :, bass.ds(h * VD, VD)], o[:], ors[:].unsqueeze(2).to_broadcast([P, T, VD]), ALU.mult).then_inc(fin, 1)

                head(0)
                with dve.Fori(1, HEADS) as h:
                    head(h)


def project_out(nc, g, tag, src, srcT, weight, scaled):
    with ExitStack() as ctx:
        w = ctx.enter_context(nc.sbuf_tensor(f"w_{tag}", [P, KT, D], F32))
        wl, tr = g.sem(f"w_loaded_{tag}"), g.sem(f"mix_transposed_{tag}")
        ea, ed = g.sem(f"mixT_low_{tag}"), g.sem(f"mixT_high_{tag}")
        pr, xa = g.sem(f"out_ready_{tag}"), g.sem(f"x_added_{tag}")
        wv = weight.rearrange("(j p) n -> p j n", p=P)
        with nc.Block() as block:
            @block.sync
            def _(sp):
                for j in range(KT):
                    sp.dma_start(w[:, j, :], wv[:, j, :]).then_inc(wl, 16)

            @block.tensor
            def _(pe):
                if src is not None:
                    for t in range(T):
                        wait(pe, ea, t - 1)
                        wait(pe, ed, 4 * (t - 1))
                        for j in range(KT):
                            last = nc.tensor.transpose(g.ps[:, 2 * (t % 2) + j // 4, (j % 4) * P:(j % 4 + 1) * P], src[:, t, j * P:(j + 1) * P], g.ident[:])
                        last.then_inc(tr, 1)
                    pe.wait_ge(ea, T)
                    pe.wait_ge(ed, 4 * T)
                pe.wait_ge(wl, 16 * KT)
                for t in range(T):
                    wait(pe, xa, t - 1)
                    for half in range(2):
                        for j in range(KT):
                            last = nc.tensor.matmul(g.ps[:, 4 + 2 * (t % 2) + half, :], srcT[:, j, t * P:(t + 1) * P],
                                                    w[:, j, half * HALF:(half + 1) * HALF], start=j == 0, stop=j == KT - 1)
                    last.then_inc(pr, 1)

            @block.scalar
            def _(act):
                if src is not None:
                    for t in range(T):
                        act.wait_ge(tr, t + 1)
                        for dst, cut in order_mirrored(t):
                            last = nc.scalar.activation(srcT[:, 0:4, dst], g.ps[:, 2 * (t % 2), :].rearrange("p (j n) -> p j n", n=P)[:, :, cut], ACT.Copy,
                                                        scale=scaled[:, ROW_SUBLN:ROW_SUBLN + 1])
                        last.then_inc(ea, 1)

            @block.vector
            def _(dve):
                if src is not None:
                    for t in range(T):
                        dve.wait_ge(tr, t + 1)
                        for j in range(4):
                            for dst, cut in order_mirrored(t):
                                last = nc.vector.tensor_scalar(srcT[:, 4 + j, dst], g.ps[:, 2 * (t % 2) + 1, j * P:(j + 1) * P][:, cut],
                                                               scaled[:, ROW_SSDN + j:ROW_SSDN + j + 1], None, ALU.mult)
                            last.then_inc(ed, 1)
                for t in range(T):
                    dve.wait_ge(pr, t + 1)
                    tt(nc.vector, g.x[:, t, :], g.x[:, t, :], g.ps[:, 4 + 2 * (t % 2):6 + 2 * (t % 2), :].rearrange("p a n -> p (a n)"), ALU.add).then_inc(xa, 1)


def route(nc, g, layer, hT):
    io = g.io
    NL = GROUPS + EXPERTS
    with ExitStack() as ctx:
        sb = lambda n, s, d=F32: ctx.enter_context(nc.sbuf_tensor(f"{n}_r{layer}", s, d))
        rw, rb = sb("router_w", [P, KT, NL]), sb("router_b", [P, NL])
        gl, el = sb("group_logits", [P, T, 8]), sb("expert_logits", [P, T, EXPERTS])
        gm, em = sb("group_max", [P, T, 8]), sb("expert_max", [P, T, 8])
        gi, ei = sb("group_idx", [P, T, 8], U32), sb("expert_idx", [P, T, 8], U32)
        gf, ef = sb("group_idx_f", [P, T]), sb("expert_idx_f", [P, T, 2])
        m12 = sb("choice", [P, 2, T, EXPERTS])
        both, pre = sb("chosen", [P, T, EXPERTS]), sb("chosen_before", [P, T, EXPERTS])
        ge, gs, gp = sb("group_exp", [P, T, 4]), sb("group_sum", [P, T]), sb("group_p", [P, T])
        de, dn = sb("expert_exp", [P, T]), sb("expert_den", [P, T])
        cnt, cge = sb("counts", [P, EXPERTS]), sb("count_steps", [P, EXPERTS, 8])
        nb, inc, inc2 = sb("n_blocks", [P, EXPERTS]), sb("blocks_end", [P, EXPERTS]), sb("blocks_end2", [P, EXPERTS])
        rk, rt = sb("slot_of", [P, T, EXPERTS]), sb("slot_tmp", [P, T, EXPERTS])
        df, si, sf = sb("slot_f", [P, 2, T]), sb("slot_parts", [P, 2, 2 * T], I32), sb("slot_parts_f", [P, 2, 2 * T])
        hq, hb = sb("onehot_place", [P, 2 * T, P]), sb("onehot_block", [P, 2 * T, SLOT_BLOCKS])
        pad, tab = sb("slot_empty", [P, SLOT_BLOCKS]), sb("slot_choice", [P, SLOT_BLOCKS])
        EXTRA = MAX_BLOCKS - EXPERTS
        bt, bf = sb("block_cmp", [1, EXTRA, EXPERTS]), sb("block_expert_f", [1, EXTRA])
        npf = sb("n_pairs_f", [1, 2])
        pair_cmp = sb("pair_cmp", [1, EXTRA // 2])
        rl, lr = g.sem(f"router_loaded_{layer}"), g.sem(f"logits_ready_{layer}")
        vs, gd, ge_r = g.sem(f"dve_route_step_{layer}"), g.sem(f"softmax_in_{layer}"), g.sem(f"softmax_exp_{layer}")
        ch, rr = g.sem(f"chosen_ready_{layer}"), g.sem(f"ranks_ready_{layer}")
        ohr, tbr = g.sem(f"onehots_ready_{layer}"), g.sem(f"slot_choices_ready_{layer}")
        rgw = io["router_group_w"][layer].rearrange("(p j) g -> p j g", j=KT)
        rew = io["router_expert_w"][layer].rearrange("(p j) g e -> p j (g e)", j=KT)
        cuts = [0, 32, 64, 72, 72 + SLOT_BLOCKS, 72 + SLOT_BLOCKS + P, 72 + SLOT_BLOCKS + P + EXPERTS]
        iota_e, grp_e, j128, iota_b, iota_p, first_slot = (g.small[:, a:b] for a, b in zip(cuts, cuts[1:]))
        with nc.Block() as block:
            @block.sync
            def _(sp):
                with nc.allow_non_contiguous_dma("router weights, rows of 4 and 32"):
                    sp.dma_start(rw[:, :, 0:GROUPS], rgw).then_inc(rl, 16)
                    sp.dma_start(rw[:, :, GROUPS:], rew).then_inc(rl, 16)
                    sp.dma_start(rb[:, 0:GROUPS], io["router_group_b"][layer].partition_broadcast(P)).then_inc(rl, 16)
                    sp.dma_start(rb[:, GROUPS:], io["router_expert_b"][layer].rearrange("g e -> (g e)").partition_broadcast(P)).then_inc(rl, 16)
                sp.wait_ge(g.h_stored[layer], 16 * T)

            @block.tensor
            def _(pe):
                pe.wait_ge(rl, 64)
                for t in range(T):
                    for j in range(KT):
                        last = nc.tensor.matmul(g.ps[:, 0, t * NL:(t + 1) * NL], hT[:, j, t * P:(t + 1) * P], rw[:, j, :], start=j == 0, stop=j == KT - 1)
                last.then_inc(lr, 1)
                pe.wait_ge(ch, 1)
                for t in range(T):
                    nc.tensor.matmul(g.ps[:, 1, t * EXPERTS:(t + 1) * EXPERTS], g.masks[:, M_LT * P:(M_LT + 1) * P], both[:, t, :], start=True, stop=False)
                    nc.tensor.matmul(g.ps[:, 1, t * EXPERTS:(t + 1) * EXPERTS], g.masks[:, M_ONE * P:(M_ONE + 1) * P], pre[:, t, :], start=False, stop=True)
                nc.tensor.matmul(g.ps[:, 2, 0:EXPERTS], g.masks[:, M_ONE * P:(M_ONE + 1) * P], cnt[:], start=True, stop=True).then_inc(rr, 1)
                pe.wait_ge(ohr, 1)
                for m in range(2 * T):
                    last = nc.tensor.matmul(g.ps[:, 3, 0:SLOT_BLOCKS], hq[:, m, :], hb[:, m, :], start=m == 0, stop=m == 2 * T - 1)
                last.then_inc(tbr, 1)

            @block.scalar
            def _(act):
                act.wait_ge(gd, 1)
                nc.scalar.activation(ge[:], ge[:], ACT.Exp).then_inc(ge_r, 1)
                act.wait_ge(gd, 2)
                nc.scalar.activation(de[:], de[:], ACT.Exp).then_inc(ge_r, 1)

            @block.vector
            def _(dve):
                V = nc.vector
                step = Chain(dve, vs)
                bE = lambda v: v.unsqueeze(2).to_broadcast([P, T, EXPERTS])
                cE = lambda v: v.unsqueeze(1).to_broadcast([P, T, EXPERTS])
                step(V.memset(gl[:], -BIG))
                dve.wait_ge(rl, 64)
                dve.wait_ge(lr, 1)
                lg = g.ps[:, 0, 0:T * NL].rearrange("p (t n) -> p t n", n=NL)
                step(tt(V, gl[:, :, 0:GROUPS], lg[:, :, 0:GROUPS], rb[:, 0:GROUPS].unsqueeze(1).to_broadcast([P, T, GROUPS]), ALU.add))
                step(tt(V, el[:], lg[:, :, GROUPS:], cE(rb[:, GROUPS:]), ALU.add))
                for t in range(T):
                    step(V.max(gm[:, t, :], gl[:, t, :]))
                    step(V.max_index(gi[:, t, :], gm[:, t, :], gl[:, t, :]))
                tt(V, ge[:], gl[:, :, 0:GROUPS], gm[:, :, 0:1].to_broadcast([P, T, GROUPS]), ALU.subtract).then_inc(gd, 1)
                step(V.tensor_copy(gf[:], gi[:, :, 0]))
                step(tt(V, rt[:], cE(grp_e), bE(gf[:]), ALU.is_equal))
                step(V.tensor_scalar(rk[:], rt[:], BIG, -BIG, ALU.mult, ALU.add))
                step(tt(V, el[:], el[:], rk[:], ALU.add))
                for t in range(T):
                    step(V.max(em[:, t, :], el[:, t, :]))
                    step(V.max_index(ei[:, t, :], em[:, t, :], el[:, t, :]))
                tt(V, de[:], em[:, :, 1], em[:, :, 0], ALU.subtract).then_inc(gd, 1)
                step(V.tensor_copy(ef[:], ei[:, :, 0:2]))
                for k in range(2):
                    step(tt(V, m12[:, k], cE(iota_e), bE(ef[:, :, k]), ALU.is_equal))
                step(tt(V, both[:], m12[:, 0], m12[:, 1], ALU.add))
                step(V.memset(pre[:, 0, :], 0.0))
                for t in range(1, T):
                    step(tt(V, pre[:, t, :], pre[:, t - 1, :], both[:, t - 1, :], ALU.add))
                tt(V, cnt[:], pre[:, T - 1, :], both[:, T - 1, :], ALU.add).then_inc(ch, 1)
                dve.wait_ge(ge_r, 2)
                step(V.tensor_reduce(out=gs[:], in_=ge[:], axis=AX, op=ALU.add))
                step(V.tensor_scalar(dn[:], de[:], 1.0, None, ALU.add))
                step(tt(V, dn[:], dn[:], gs[:], ALU.mult))
                step(V.reciprocal(g.gates[:, 0, :], dn[:]))
                step(tt(V, g.gates[:, 1, :], g.gates[:, 0, :], de[:], ALU.mult))
                dve.wait_ge(rr, 1)
                step(V.tensor_copy(cnt[:], g.ps[:, 2, 0:EXPERTS]))
                step(tt(V, cge[:], cnt[:].unsqueeze(2).to_broadcast([P, EXPERTS, 8]), j128.unsqueeze(1).to_broadcast([P, EXPERTS, 8]), ALU.is_gt))
                step(V.tensor_reduce(out=nb[:], in_=cge[:], axis=AX, op=ALU.add))
                src, dst = nb, inc
                for s in (1, 2, 4, 8, 16):
                    step(V.tensor_copy(dst[:, 0:s], src[:, 0:s]))
                    step(tt(V, dst[:, s:], src[:, s:], src[:, 0:EXPERTS - s], ALU.add))
                    src, dst = dst, (inc2 if dst is inc else inc)
                end, jump = src, dst
                step(tt(V, jump[:], end[:], nb[:], ALU.subtract))
                step(V.tensor_scalar(jump[:], jump[:], float(P), float(P * (EXPERTS - 1)), ALU.mult, ALU.add))
                step(tt(V, jump[:], jump[:], first_slot, ALU.subtract))
                ranks = g.ps[:, 1, 0:T * EXPERTS].rearrange("p (t n) -> p t n", n=EXPERTS)
                step(V.tensor_scalar(rt[:], ranks, float(P), None, ALU.is_ge))
                step(tt(V, rt[:], rt[:], cE(jump[:]), ALU.mult))
                step(tt(V, rk[:], ranks, cE(first_slot), ALU.add))
                step(tt(V, rk[:], rk[:], rt[:], ALU.add))
                for k in range(2):
                    step(tt(V, rt[:], rk[:], m12[:, k], ALU.mult))
                    step(V.tensor_reduce(out=df[:, k, :], in_=rt[:], axis=AX, op=ALU.add))
                M = 2 * T
                step(V.tensor_copy(si[:, 0, :], df[:].rearrange("p k t -> p (k t)")))
                step(V.tensor_scalar(si[:, 1, :], si[:, 0, :], P - 1, None, ALU.bitwise_and))
                step(V.tensor_scalar(si[:, 0, :], si[:, 0, :], P.bit_length() - 1, None, ALU.arith_shift_right))
                step(V.tensor_copy(sf[:], si[:]))
                step(tt(V, hq[:], iota_p.unsqueeze(1).to_broadcast([P, M, P]), sf[:, 1, :].unsqueeze(2).to_broadcast([P, M, P]), ALU.is_equal))
                step(tt(V, hb[:], iota_b.unsqueeze(1).to_broadcast([P, M, SLOT_BLOCKS]), sf[:, 0, :].unsqueeze(2).to_broadcast([P, M, SLOT_BLOCKS]), ALU.is_equal))
                tt(V, hb[:], hb[:], g.ids[:].unsqueeze(2).to_broadcast([P, M, SLOT_BLOCKS]), ALU.mult).then_inc(ohr, 1)
                step(tt(V, bt[:], end[0:1, :].unsqueeze(1).to_broadcast([1, EXTRA, EXPERTS]),
                        iota_b[0:1, 0:EXTRA].unsqueeze(2).to_broadcast([1, EXTRA, EXPERTS]), ALU.is_le))
                step(V.tensor_reduce(out=bf[:], in_=bt[:], axis=AX, op=ALU.add))
                step(V.tensor_scalar(bf[:], bf[:], float(EXPERTS - 1), None, ALU.min))
                step(V.tensor_copy(g.block_expert[:, EXPERTS:MAX_BLOCKS], bf[:]))
                step(V.tensor_copy(g.block_expert[:, 0:EXPERTS], iota_e[0:1, :]))
                step(tt(V, pair_cmp[:], end[0:1, EXPERTS - 1:EXPERTS].to_broadcast([1, EXTRA // 2]), iota_b[0:1, 0:EXTRA:2], ALU.is_gt))
                step(V.tensor_reduce(out=npf[:, 0:1], in_=pair_cmp[:], axis=AX, op=ALU.add))
                step(V.tensor_scalar(g.last_pair[:], npf[:, 0:1], float(EXPERTS // 2 - 1), None, ALU.add))
                dve.wait_ge(tbr, 1)
                step(V.tensor_scalar(pad[:], g.ps[:, 3, 0:SLOT_BLOCKS], 0.0, float(EMPTY), ALU.is_equal, ALU.mult))
                step(V.scalar_tensor_tensor(out=tab[:], in0=g.ps[:, 3, 0:SLOT_BLOCKS], scalar=-1.0, in1=pad[:], op0=ALU.add, op1=ALU.add))
                step(V.tensor_copy(g.slot_y[:], tab[:]))
                step(V.tensor_scalar(g.slot_x[:], g.slot_y[:], 1, None, ALU.arith_shift_right))


def expert_weights(nc, g, layer):
    e = Shared()
    io = g.io
    e.w13 = [io[f"expert_w{n}"][layer].rearrange("e (p j) n -> e p j n", j=KT) for n in (1, 3)]
    e.w2 = io["expert_w2"][layer].rearrange("e (p j) n -> e p (j n)", j=2)
    e.w13l = [[g.sem(f"w{n}_loaded{s}_{layer}") for n in (1, 3)] for s in range(2)]
    e.w2l = [g.sem(f"w2_loaded{s}_{layer}") for s in range(2)]
    return e


def load_w13(sp, e, n, expert, s):
    sp.dma_start(e.raw[:, s, n, :, :], e.w13[n][bass.ds(expert, 1), :, :, :].rearrange("e p j n -> (e p) j n")).then_inc(e.w13l[s][n], 16)


def load_w2(sp, e, expert, s):
    sp.dma_start(e.w2s[:, s, :, :].rearrange("p j n -> p (j n)"), e.w2[bass.ds(expert, 1), :, :].rearrange("e p n -> (e p) n")).then_inc(e.w2l[s], 16)


def experts(nc, g, layer, e):
    with ExitStack() as ctx:
        sb = lambda n, s, d=F32: ctx.enter_context(nc.sbuf_tensor(f"{n}_e{layer}", s, d))
        raw, w2s, w13l, w2l = e.raw, e.w2s, e.w13l, e.w2l
        wh, wl = sb("w13_hi", [P, 2, 2, KT, HID], F32R), sb("w13_lo", [P, 2, 2, KT, HID], F32R)
        xb = sb("x_block", [P, 2, D])
        xh, xlo = sb("xT_hi", [P, 2, KT, P], F32R), sb("xT_lo", [P, 2, KT, P], F32R)
        sg, hid, hT = sb("silu", [P, 2, HID]), sb("hidden", [P, 2, HID]), sb("hiddenT", [P, 2, P])
        yb = sb("y_block", [P, 2, D])
        ix, iy = sb("gather_rows", [P, 2], I32), sb("scatter_rows", [P, 2], I32)
        xl = [g.sem(f"x_block_loaded{s}_{layer}") for s in range(2)]
        yst = [g.sem(f"y_stored{s}_{layer}") for s in range(2)]
        xt, xhr, xlr = g.sem(f"x_transposed_{layer}"), g.sem(f"xT_hi_ready_{layer}"), g.sem(f"xT_lo_ready_{layer}")
        whr, wlr = g.sem(f"w13_hi_ready_{layer}"), g.sem(f"w13_lo_ready_{layer}")
        gu, sil, hr = g.sem(f"gate_up_ready_{layer}"), g.sem(f"silu_done_{layer}"), g.sem(f"hidden_ready_{layer}")
        ht, he, yr = g.sem(f"hidden_transposed_{layer}"), g.sem(f"hiddenT_ready_{layer}"), g.sem(f"y_ready_{layer}")
        yea, yed = g.sem(f"y_low_read_{layer}"), g.sem(f"y_high_read_{layer}")
        ixr, iyr, x0 = g.sem(f"gather_rows_ready_{layer}"), g.sem(f"scatter_rows_ready_{layer}"), g.sem(f"x_block_cleared_{layer}")
        seen = g.sem(f"pool_wait_passed_{layer}")
        FIRST, PAIRS = EXPERTS // 2, MAX_BLOCKS // 2

        def pairs(eng, step, finish=None):
            for i in range(2):
                step(i, 0, None)
                step(i, 1, None)
            with eng.Fori(2, FIRST - 1) as i:
                step(i, 0, None)
                step(i, 1, None)
            m = eng.value_load(g.last_pair[0:1, 0:1], min_val=FIRST - 1, max_val=PAIRS - 1)
            with eng.Fori(FIRST - 1, PAIRS) as i:
                with eng.If(i <= m):
                    step(i, 0, m)
                    step(i, 1, m)
                with eng.Else():
                    eng.nop()
            if finish:
                finish(m)

        def for_next(eng, i, m, f):
            if m is None:
                f()
                return
            with eng.If(i < m):
                f()
            with eng.Else():
                eng.nop()

        with nc.Block() as block:
            @block.sync
            def _(sp):
                def expert_of(k, m):
                    if m is None:
                        return k
                    return sp.value_load(g.block_expert[0:1, bass.ds(k, 1)], min_val=0, max_val=EXPERTS - 1)

                def w13(k, s, m):
                    x = expert_of(k, m)
                    for n in range(2):
                        wait(sp, wlr, 2 * (k - 2) + n + 1)
                        load_w13(sp, e, n, x, s)

                def down_w(k, s, m):
                    x = expert_of(k, m)
                    wait(sp, yr, k - 1)
                    load_w2(sp, e, x, s)

                def step(i, s, m):
                    k = 2 * i + s
                    if s == 0:
                        for_next(sp, i, m, lambda: w13(k + 2, s, m))
                        down_w(k + 1, 1 - s, m)
                    else:
                        for_next(sp, i, m, lambda: (w13(k + 2, s, m), down_w(k + 1, 1 - s, m)))

                pairs(sp, step)

            @block.gpsimd
            def _(pool):
                def gather_x(k, s, turn):
                    wait(pool, xl[s], 16 * turn)
                    pool.sem_inc(seen, 1)
                    nc.gpsimd.tensor_copy(ix[:, s:s + 1], g.slot_x[:, bass.ds(k, 1)]).then_inc(ixr, 1)
                    wait(pool, xt, k - 1)
                    pool.wait_ge(ixr, k + 1)
                    pool.sem_inc(seen, 1)
                    pool.indirect_dma_start(out=xb[:, s, :], out_offset=None, in_=g.h_rows[:, :],
                                            in_offset=bass.IndirectOffsetOnAxis(ap=ix[:, s:s + 1], axis=0),
                                            bounds_check=SEQ - 1, oob_is_err=False).then_inc(xl[s], 16)

                def scatter_y(k, s, turn):
                    wait(pool, yst[s], 16 * turn)
                    pool.sem_inc(seen, 1)
                    nc.gpsimd.tensor_copy(iy[:, s:s + 1], g.slot_y[:, bass.ds(k, 1)]).then_inc(iyr, 1)
                    pool.wait_ge(yea, k + 1)
                    pool.wait_ge(yed, k + 1)
                    pool.wait_ge(iyr, k + 1)
                    pool.sem_inc(seen, 1)
                    pool.indirect_dma_start(out=g.y_rows[:, :], out_offset=bass.IndirectOffsetOnAxis(ap=iy[:, s:s + 1], axis=0),
                                            in_=yb[:, s, :], in_offset=None,
                                            bounds_check=2 * SEQ - 1, oob_is_err=False).then_inc(yst[s], 16)

                nc.gpsimd.memset(xb[:], 0.0).then_inc(x0, 1)
                pool.wait_ge(x0, 1)
                pool.wait_ge(g.h_stored[layer], 16 * T)
                gather_x(0, 0, 0)
                gather_x(1, 1, 0)
                gather_x(2, 0, 1)

                def step(i, s, m):
                    k = 2 * i + s
                    gather_x(k + 3, 1 - s, i + 1 + s)
                    if not (isinstance(k, int) and k == 0):
                        scatter_y(k - 1, 1 - s, i - 1 + s)

                def finish(m):
                    scatter_y(2 * m + 1, 1, m)
                    for s in range(2):
                        pool.wait_ge(yst[s], 16 * (m + 1))
                        pool.sem_inc(seen, 1)
                        pool.wait_ge(xl[s], 16 * (m + 3 - s))
                        pool.sem_inc(seen, 1)

                pairs(pool, step, finish)

            @block.tensor
            def _(pe):
                def transpose_x(k, s, turn):
                    pe.wait_ge(xl[s], 16 * (turn + 1))
                    wait(pe, xhr, 2 * k)
                    wait(pe, xlr, 2 * k)
                    xv = xb[:, s, :].rearrange("p (q j) -> p j q", j=KT)
                    for j in range(KT):
                        last = nc.tensor.transpose(g.ps[:, 2 + j // 4, (j % 4) * P:(j % 4 + 1) * P], xv[:, j, :], g.ident[:])
                    last.then_inc(xt, 1)

                def transpose_hidden(k, s):
                    pe.wait_ge(hr, k + 1)
                    wait(pe, he, k)
                    hv = hid[:, s, :].rearrange("p (q j) -> p j q", j=2)
                    for j in range(2):
                        last = nc.tensor.transpose(g.ps[:, 4, j * P:(j + 1) * P], hv[:, j, :], g.ident[:])
                    last.then_inc(ht, 1)

                def down(k, s, turn):
                    pe.wait_ge(he, k + 1)
                    pe.wait_ge(w2l[s], 16 * (turn + 1))
                    wait(pe, yea, k)
                    wait(pe, yed, k)
                    for half in range(2):
                        for j in range(2):
                            last = nc.tensor.matmul(g.ps[:, 5 + half, :], hT[:, j, :], w2s[:, s, j, half * HALF:(half + 1) * HALF], start=j == 0, stop=j == 1)
                    last.then_inc(yr, 1)

                pe.wait_ge(x0, 1)
                transpose_x(0, 0, 0)

                def step(i, s, m):
                    k = 2 * i + s
                    first = isinstance(k, int) and k == 0
                    if not first:
                        transpose_hidden(k - 1, 1 - s)
                    transpose_x(k + 1, 1 - s, i + s)
                    pe.wait_ge(whr, 2 * k + 2)
                    pe.wait_ge(wlr, 2 * k + 2)
                    pe.wait_ge(xhr, 2 * k + 2)
                    pe.wait_ge(xlr, 2 * k + 2)
                    wait(pe, hr, k - 1)
                    for j in range(KT):
                        for n, (a, b) in enumerate(((xh, wh), (xh, wl), (xlo, wh))):
                            last = nc.tensor.matmul(g.ps[:, s, :], a[:, s, j, :], b[:, s, :, j, :], start=j == 0 and n == 0, stop=j == KT - 1 and n == 2)
                    last.then_inc(gu, 1)
                    if not first:
                        down(k - 1, 1 - s, i - 1 + s)

                def finish(m):
                    transpose_hidden(2 * m + 1, 1)
                    down(2 * m + 1, 1, m)

                pairs(pe, step, finish)

            @block.scalar
            def _(act):
                def split_w(k, s, turn):
                    wait(act, gu, k - 1)
                    for n in range(2):
                        act.wait_ge(w13l[s][n], 16 * (turn + 1))
                        nc.scalar.activation(wh[:, s, n, :, :], raw[:, s, n, :, :], ACT.Copy).then_inc(whr, 1)

                def split_x(k, s):
                    act.wait_ge(xt, k + 1)
                    wait(act, gu, k - 1)
                    for b in range(2):
                        nc.scalar.activation(xh[:, s, 4 * b:4 * b + 4, :].rearrange("p j n -> p (j n)"), g.ps[:, 2 + b, :], ACT.Copy).then_inc(xhr, 1)

                def copy_y(k, s, stored):
                    act.wait_ge(yr, k + 1)
                    wait(act, yst[s], stored)
                    nc.scalar.activation(yb[:, s, 0:HALF], g.ps[:, 5, :], ACT.Copy).then_inc(yea, 1)

                split_w(0, 0, 0)
                split_x(0, 0)

                def step(i, s, m):
                    k = 2 * i + s
                    split_x(k + 1, 1 - s)
                    if s == 0:
                        split_w(k + 1, 1 - s, i + s)
                    else:
                        for_next(act, i, m, lambda: split_w(k + 1, 1 - s, i + s))
                    act.wait_ge(gu, k + 1)
                    wait(act, hr, k - 1)
                    nc.scalar.activation(sg[:, s, :], g.ps[:, s, 0:HID], ACT.Silu).then_inc(sil, 1)
                    if not (isinstance(k, int) and k == 0):
                        copy_y(k - 1, 1 - s, 16 * (i - 1 + s))

                pairs(act, step, lambda m: copy_y(2 * m + 1, 1, 16 * m))

            @block.vector
            def _(dve):
                def split_w(k, s):
                    for n in range(2):
                        dve.wait_ge(whr, 2 * k + n + 1)
                        tt(nc.vector, wl[:, s, n, :, :], raw[:, s, n, :, :], wh[:, s, n, :, :].bitcast(F32), ALU.subtract).then_inc(wlr, 1)

                def split_x(k, s):
                    for b in range(2):
                        dve.wait_ge(xhr, 2 * k + b + 1)
                        tt(nc.vector, xlo[:, s, 4 * b:4 * b + 4, :].rearrange("p j n -> p (j n)"), g.ps[:, 2 + b, :],
                           xh[:, s, 4 * b:4 * b + 4, :].rearrange("p j n -> p (j n)").bitcast(F32), ALU.subtract).then_inc(xlr, 1)

                def copy_hidden(k):
                    dve.wait_ge(ht, k + 1)
                    wait(dve, yr, k)
                    nc.vector.tensor_copy(hT[:].rearrange("p j n -> p (j n)"), g.ps[:, 4, 0:2 * P]).then_inc(he, 1)

                def copy_y(k, s, stored):
                    dve.wait_ge(yr, k + 1)
                    wait(dve, yst[s], stored)
                    nc.vector.tensor_copy(yb[:, s, HALF:], g.ps[:, 6, :]).then_inc(yed, 1)

                split_w(0, 0)
                split_x(0, 0)

                def step(i, s, m):
                    k = 2 * i + s
                    first = isinstance(k, int) and k == 0
                    if not first:
                        copy_hidden(k - 1)
                    split_x(k + 1, 1 - s)
                    if s == 0:
                        split_w(k + 1, 1 - s)
                    else:
                        for_next(dve, i, m, lambda: split_w(k + 1, 1 - s))
                    dve.wait_ge(sil, k + 1)
                    wait(dve, ht, k - 1)
                    tt(nc.vector, hid[:, s, :], sg[:, s, :], g.ps[:, s, HID:], ALU.mult).then_inc(hr, 1)
                    if not first:
                        copy_y(k - 1, 1 - s, 16 * (i - 1 + s))

                def finish(m):
                    copy_hidden(2 * m + 1)
                    copy_y(2 * m + 1, 1, 16 * m)

                pairs(dve, step, finish)


def combine(nc, g, layer, last_layer):
    BUF = 4
    with ExitStack() as ctx:
        yg = ctx.enter_context(nc.sbuf_tensor(f"y_by_token_{layer}", [P, BUF, 2, D], F32))
        gt = [g.sem(f"y_by_token_loaded{s}_{layer}") for s in range(BUF)]
        vs, ad, out = g.sem(f"dve_combine_step_{layer}"), g.sem(f"combined_{layer}"), g.sem(f"out_stored_{layer}")
        yv = g.y_rows.rearrange("(t p k) n -> t p k n", p=P, k=2)
        with nc.Block() as block:
            @block.scalar
            def _(act):
                for t in range(T):
                    wait(act, ad, t - BUF + 1)
                    act.dma_start(yg[:, t % BUF, :, :], yv[t]).then_inc(gt[t % BUF], 16)

            @block.vector
            def _(dve):
                step = Chain(dve, vs)
                for t in range(T):
                    dve.wait_ge(gt[t % BUF], 16 * (t // BUF + 1))
                    for k in range(2):
                        ins = nc.vector.scalar_tensor_tensor(out=g.x[:, t, :], in0=yg[:, t % BUF, k, :], scalar=g.gates[:, k, t:t + 1], in1=g.x[:, t, :],
                                                             op0=ALU.mult, op1=ALU.add)
                        if k == 0:
                            step(ins)
                    ins.then_inc(ad, 1)

            @block.sync
            def _(sp):
                if last_layer:
                    for t in range(T):
                        sp.wait_ge(ad, t + 1)
                        sp.dma_start(g.io["out"][t * P:(t + 1) * P, :], g.x[:, t, :]).then_inc(out, 16)
                    sp.wait_ge(out, 16 * T)


def fourier(nc, g, hT):
    io = g.io
    NG = GROUPS_F
    with ExitStack() as ctx:
        sb = lambda n, s: ctx.enter_context(nc.sbuf_tensor(n, s, F32))
        diff = sb("h_minus_mirror", [P, KT, HALF])
        dch = sb("dft_channels", [P, 2, 2 * P])
        ct, st, alt = sb("cos_tokens", [P, 4, HALF + 1]), sb("sin_tokens", [P, 4, HALF]), sb("alternating", [1, HALF + 1])
        ab = sb("channel_dft", [P, 4, NG, 2 * P])
        a5 = sb("channel_dft_512", [1, NG, P + 1])
        pt, qt, pz = sb("cos_part", [P, NG, HALF]), sb("sin_part", [P, NG, HALF]), sb("cos_part_mirror0", [P, NG, P])
        pn, pnz = sb("cos_part_128", [NG, HALF]), sb("cos_part_128_mirror0", [NG, P])
        wd, wm, wp, wn = sb("w_direct", [P, NG, D]), sb("w_mirror", [P, NG, D]), sb("w_plus", [P, NG, D]), sb("w_128", [NG, D])
        cl, tl, wl = g.sem("dft_channels_loaded"), g.sem("dft_tokens_loaded"), g.sem("w_fourier_loaded")
        fd, fo = g.sem("difference_ready"), g.sem("folded")
        p1, r1, a5p, a5r = g.sem("channel_dft_ready"), g.sem("channel_dft_read"), g.sem("dft_512_ready"), g.sem("dft_512_read")
        p2, pr_, qr, p5, zc = g.sem("token_dft_ready"), g.sem("cos_part_read"), g.sem("sin_part_read"), g.sem("cos_512_ready"), g.sem("mirror0_ready")
        wpr, wmr = g.sem("w_plus_ready"), g.sem("w_minus_ready")
        xr, yr, zr, xs, ya = g.sem("x_part_ready"), g.sem("y_part_ready"), g.sem("z_part_ready"), g.sem("x_part_added"), g.sem("y_part_added")
        cols = lambda t: slice(t * P, (t + 1) * P)
        with nc.Block() as block:
            @block.sync
            def _(sp):
                sp.dma_start(dch[:], io["c_dft_channels"].rearrange("(a p) n -> p a n", p=P)).then_inc(cl, 16)
                sp.dma_start(ct[:], io["c_cos_tokens"].rearrange("(a p) n -> p a n", p=P)).then_inc(tl, 16)
                sp.dma_start(alt[:], io["c_alternating"]).then_inc(tl, 16)
                sp.dma_start(st[:], io["c_sin_tokens"].rearrange("(a p) n -> p a n", p=P)).then_inc(tl, 16)
                sp.dma_start(wd[:], io["w_fourier_direct"].rearrange("g p n -> p g n")).then_inc(wl, 16)
                sp.dma_start(wm[:], io["w_fourier_mirror"].rearrange("g p n -> p g n")).then_inc(wl, 16)
                sp.dma_start(wn[:], io["w_fourier_128"]).then_inc(wl, 16)

            @block.gpsimd
            def _(pool):
                pool.wait_ge(wl, 48)
                for gr in range(NG):
                    tt(nc.gpsimd, wp[:, gr, :], wd[:, gr, :], wm[:, gr, :], ALU.add).then_inc(wpr, 1)
                for gr in range(NG):
                    pool.wait_ge(wpr, gr + 1)
                    tt(nc.gpsimd, wd[:, gr, :], wd[:, gr, :], wm[:, gr, :], ALU.subtract).then_inc(wmr, 1)

            @block.tensor
            def _(pe):
                pe.wait_ge(cl, 16)
                for t in range(4):
                    pe.wait_ge(fo, t + 1)
                    for pair in range(2):
                        u = 2 * t + pair
                        wait(pe, r1, u - 3)
                        for gr in (2 * pair, 2 * pair + 1):
                            o = (gr % 2) * 2 * P
                            for a in range(2):
                                nc.tensor.matmul(g.ps[:, u % 4, o:o + P + 1], hT[:, 2 * gr + a, cols(t)], dch[:, a, 0:P + 1], start=a == 0, stop=a == 1)
                            for a in range(2):
                                last = nc.tensor.matmul(g.ps[:, u % 4, o + P + 1:o + 2 * P], diff[:, 2 * gr + a, cols(t)], dch[:, a, P + 1:], start=a == 0, stop=a == 1)
                        last.then_inc(p1, 1)
                for gr in range(NG):
                    for a in range(2):
                        nc.tensor.matmul(g.ps[0:1, 4, cols(gr)], hT[:, 2 * gr + a, HALF:HALF + 1], dch[:, a, 0:P], start=a == 0, stop=a == 1)
                    for a in range(2):
                        last = nc.tensor.matmul(g.ps[0:1, 5, gr:gr + 1], hT[:, 2 * gr + a, HALF:HALF + 1], dch[:, a, P:P + 1], start=a == 0, stop=a == 1)
                last.then_inc(a5p, 1)
                pe.wait_ge(tl, 48)
                pe.wait_ge(r1, 8)

                def cosines(out, weights, last_row, part):
                    for t in range(4):
                        nc.tensor.matmul(out, weights(t), ct[:, t, part], start=t == 0, stop=False)
                    return nc.tensor.matmul(out, last_row, alt[:, part], start=False, stop=True)

                for v in range(2 * NG):
                    gr = v // 2
                    if v >= 4:
                        pe.wait_ge((pr_, qr)[v % 2], (v - 4) // 2 + 1)
                    if v % 2 == 0:
                        wait(pe, a5r, 2)
                        last = cosines(g.ps[:, v % 4, :], lambda t: ab[:, t, gr, 0:P], a5[:, gr, 0:P], slice(0, HALF))
                    else:
                        for t in range(4):
                            last = nc.tensor.matmul(g.ps[:, v % 4, :], ab[:, t, gr, P:], st[:, t, :], start=t == 0, stop=t == 3)
                    last.then_inc(p2, 1)
                pe.wait_ge(pr_, 3)
                last = cosines(g.ps[0:NG, 0, :], lambda t: ab[:, t, :, P], a5[:, :, P], slice(0, HALF))
                last.then_inc(p2, 1)
                for gr in range(NG):
                    cosines(g.ps[:, 6, gr:gr + 1], lambda t: ab[:, t, gr, 0:P], a5[:, gr, 0:P], slice(HALF, HALF + 1))
                last = cosines(g.ps[0:NG, 6, NG:NG + 1], lambda t: ab[:, t, :, P], a5[:, :, P], slice(HALF, HALF + 1))
                last.then_inc(p5, 1)
                pe.wait_ge(wpr, NG)
                pe.wait_ge(wmr, NG)
                pe.wait_ge(pr_, NG + 1)
                pe.wait_ge(qr, NG)
                pe.wait_ge(zc, 4)

                def x_part(bank, main, special):
                    for half in range(2):
                        n = slice(half * HALF, (half + 1) * HALF)
                        for gr in range(NG):
                            nc.tensor.matmul(g.ps[:, bank + half, :], main[:, gr, :], wp[:, gr, n], start=gr == 0, stop=False)
                        last = nc.tensor.matmul(g.ps[:, bank + half, :], special, wn[:, n], start=False, stop=True)
                    return last

                for t in range(4):
                    bank = 4 * (t % 2)
                    wait(pe, xs, t - 1)
                    x_part(bank, pt[:, :, cols(t)], pn[:, cols(t)]).then_inc(xr, 1)
                    wait(pe, ya, t - 1)
                    for half in range(2):
                        for gr in range(NG):
                            last = nc.tensor.matmul(g.ps[:, bank + 2 + half, :], qt[:, gr, cols(t)], wd[:, gr, half * HALF:(half + 1) * HALF], start=gr == 0, stop=gr == NG - 1)
                    last.then_inc(yr, 1)
                pe.wait_ge(xs, 3)
                x_part(0, pz[:], pnz[:]).then_inc(zr, 1)

            @block.scalar
            def _(act):
                for u in range(8):
                    t, pair = u // 2, u % 2
                    act.wait_ge(p1, u + 1)
                    nc.scalar.activation(ab[:, t, 2 * pair:2 * pair + 2, :].rearrange("p g n -> p (g n)"), g.ps[:, u % 4, :], ACT.Copy).then_inc(r1, 1)
                act.wait_ge(a5p, 1)
                nc.scalar.activation(a5[:, :, 0:P], g.ps[0:1, 4, :].rearrange("p (g n) -> p g n", g=NG), ACT.Copy).then_inc(a5r, 1)
                nc.scalar.activation(a5[:, :, P], g.ps[0:1, 5, 0:NG], ACT.Copy).then_inc(a5r, 1)
                for gr in range(NG):
                    act.wait_ge(p2, 2 * gr + 1)
                    nc.scalar.activation(pt[:, gr, :], g.ps[:, 2 * gr % 4, :], ACT.Copy).then_inc(pr_, 1)
                act.wait_ge(p2, 2 * NG + 1)
                nc.scalar.activation(pn[:], g.ps[0:NG, 0, :], ACT.Copy).then_inc(pr_, 1)
                act.wait_ge(pr_, NG + 1)
                nc.scalar.activation(pz[:, :, 1:], pt[:, :, 1:P], ACT.Copy).then_inc(zc, 1)
                nc.scalar.activation(pnz[:, 1:], pn[:, 1:P], ACT.Copy).then_inc(zc, 1)
                act.wait_ge(p5, 1)
                nc.scalar.activation(pz[:, :, 0], g.ps[:, 6, 0:NG], ACT.Copy).then_inc(zc, 1)
                nc.scalar.activation(pnz[:, 0:1], g.ps[0:NG, 6, NG:NG + 1], ACT.Copy).then_inc(zc, 1)

            @block.vector
            def _(dve):
                V = nc.vector
                for t in range(4):
                    tt(V, diff[:, :, cols(t)], hT[:, :, cols(t)], hT[:, :, cols(4 + t)], ALU.subtract).then_inc(fd, 1)
                    dve.wait_ge(fd, t + 1)
                    a = t * P + (1 if t == 0 else 0)
                    tt(V, hT[:, :, a:(t + 1) * P], hT[:, :, a:(t + 1) * P], hT[:, :, HALF + a:HALF + (t + 1) * P], ALU.add).then_inc(fo, 1)
                for gr in range(NG):
                    dve.wait_ge(p2, 2 * gr + 2)
                    V.tensor_copy(qt[:, gr, :], g.ps[:, (2 * gr + 1) % 4, :]).then_inc(qr, 1)
                flat = lambda b: g.ps[:, b:b + 2, :].rearrange("p a n -> p (a n)")
                for t in range(4):
                    bank = 4 * (t % 2)
                    dve.wait_ge(xr, t + 1)
                    ins = tt(V, g.x[:, t, :], g.x[:, t, :], flat(bank), ALU.add)
                    if t > 0:
                        ins = tt(V, g.x[:, 4 + t, :], g.x[:, 4 + t, :], flat(bank), ALU.add)
                    ins.then_inc(xs, 1)
                    dve.wait_ge(xs, t + 1)
                    dve.wait_ge(yr, t + 1)
                    tt(V, g.x[:, t, :], g.x[:, t, :], flat(bank + 2), ALU.subtract)
                    tt(V, g.x[:, 4 + t, :], g.x[:, 4 + t, :], flat(bank + 2), ALU.add).then_inc(ya, 1)
                dve.wait_ge(ya, 4)
                dve.wait_ge(zr, 1)
                tt(V, g.x[:, 4, :], g.x[:, 4, :], flat(0), ALU.add).then_inc(xs, 1)


@contextmanager
def stage(nc):
    before = nc.snapshot_sems()
    yield
    nc.clear_and_free_semaphores(nc.allocated_since(before))
    nc.all_engine_barrier()


def build(nc, io):
    with ExitStack() as ctx:
        g = Shared()
        g.io = io
        g.sem = lambda name: nc.alloc_semaphore(name=name)
        sb = lambda n, s, d=F32: ctx.enter_context(nc.sbuf_tensor(n, s, d))
        g.h_rows = nc.dram_tensor("h_rows", (SEQ, D), F32, kind="Internal").ap()
        g.y_rows = nc.dram_tensor("y_rows", (2 * SEQ, D), F32, kind="Internal").ap()
        g.ps = ctx.enter_context(nc.psum_tensor("ps", [P, 8, HALF], F32))
        g.x = sb("x_sb", [P, T, D])
        g.ident, g.masks, g.small = sb("ident", [P, P]), sb("masks", [P, 5 * P + 2]), sb("small", [P, 72 + SLOT_BLOCKS + P + EXPERTS])
        g.ids = sb("choice_ids", [P, 2 * T])
        g.vecs, g.dtb, g.dskip = sb("vecs", [P, 44]), sb("dt_bias_a", [P, 32]), sb("dskip", [P, 8])
        g.neglam, g.qscale, g.negslope = sb("neg_lambda", [P, 1]), sb("qscale", [P, HEADS]), sb("neg_slopes", [P, HEADS])
        g.mhalf = sb("minus_half", [P, T])
        g.gates = sb("gates", [P, 2, T])
        g.slot_y, g.slot_x = sb("slot_y", [P, SLOT_BLOCKS], I32), sb("slot_x", [P, SLOT_BLOCKS], I32)
        g.block_expert, g.last_pair = sb("block_expert", [1, MAX_BLOCKS + 2], I32), sb("last_pair", [1, 1], I32)
        g.x_loaded, g.h_stored = g.sem("x_loaded"), [g.sem(f"h_stored_{n}") for n in range(2)]

        with stage(nc):
            load_constants(nc, g)
        with ExitStack() as c0:
            sc = lambda n, s: c0.enter_context(nc.sbuf_tensor(n, s, F32))
            hT, mixed = sc("hT_mix0", [P, KT, SEQ]), sc("mixed", [P, T, D])
            with nc.sbuf_tensor("h_mix0", [P, 2, D], F32) as h:
                with stage(nc):
                    norm_transpose(nc, g, "mix0", io["norm_mix"][0], hT, h, order_mirrored, False, first=True)
            with ExitStack() as c1:
                s1 = lambda n, s: c1.enter_context(nc.sbuf_tensor(n, s, F32))
                xbcT, xs, draw = s1("xbcT", [P, XBC_T, SEQ + 4]), s1("xs", [P, T, 640]), s1("dt_raw", [P, T, 16])
                with stage(nc):
                    ssd_project(nc, g, hT, xbcT, xs, mixed, draw)
                with stage(nc):
                    ssd_scan(nc, g, xbcT, xs, mixed, draw)
            with stage(nc):
                attention(nc, g, hT, mixed)
            with stage(nc):
                project_out(nc, g, "out0", mixed, hT, io["w_out"][0], g.vecs)
        for layer in range(2):
            if layer == 1:
                with nc.sbuf_tensor("hT_mix1", [P, KT, SEQ], F32) as hT:
                    with nc.sbuf_tensor("h_mix1", [P, 2, D], F32) as h:
                        with stage(nc):
                            norm_transpose(nc, g, "mix1", io["norm_mix"][1], hT, h, order_same, True)
                    with stage(nc):
                        fourier(nc, g, hT)
            with stage(nc), ExitStack() as c2:
                e = expert_weights(nc, g, layer)
                se = lambda n, s: c2.enter_context(nc.sbuf_tensor(f"{n}_{layer}", s, F32))
                e.raw, e.w2s = se("w13_raw", [P, 2, 2, KT, HID]), se("w2", [P, 2, 2, D])
                with nc.sbuf_tensor(f"hT_ffn{layer}", [P, KT, SEQ], F32) as hT, nc.sbuf_tensor(f"h_ffn{layer}", [P, T, D], F32) as h:
                    with stage(nc):
                        norm_transpose(nc, g, f"ffn{layer}", io["norm_ffn"][layer], hT, h, order_same, False, stored=g.h_stored[layer], weights=e)
                    with stage(nc):
                        route(nc, g, layer, hT)
                with stage(nc):
                    experts(nc, g, layer, e)
            with stage(nc):
                combine(nc, g, layer, layer == 1)


_INS = ['x', 'norm_mix', 'norm_ffn', 'w_in', 'q_norm', 'k_norm', 'lambda_q1', 'lambda_k1', 'lambda_q2', 'lambda_k2',
        'attn_subln', 'conv_w', 'conv_b', 'dt_bias', 'a_log', 'd_skip', 'ssd_norm', 'w_out', 'w_fourier',
        'router_group_w', 'router_group_b', 'router_expert_w', 'router_expert_b', 'expert_w1', 'expert_w3', 'expert_w2']


def shape_constants():
    import numpy as np
    k, n = np.arange(P)[:, None], np.arange(P)[None, :]
    masks = np.concatenate([k <= n, k > n, k >= n, k < n, np.ones((P, P), bool), k < 64, k >= 64], axis=1).astype(np.float32)
    small = np.concatenate([np.arange(32), np.arange(32) // PER_GROUP, np.arange(1, 9) * P, np.arange(SLOT_BLOCKS), np.arange(P), np.arange(32) * P]).astype(np.float32)
    negdist = -np.abs(k + 896 - np.arange(1920)[None, :]).astype(np.float32)
    ids = (2 * (k[:, :, None] + P * np.arange(T)[None, None, :]) + np.arange(2)[None, :, None] + 1).astype(np.float32)
    ids = ids.reshape(P, 2 * T)
    d, n, s = np.arange(2 * P), np.arange(HALF), np.arange(HALF + 1)
    turn = lambda a, b, size: 2 * np.pi * ((a[:, None] * b[None, :]) % size) / size
    ang = turn(d, d[:P + 1], 2 * P)
    channels = np.concatenate([np.cos(ang), np.sin(ang[:, 1:P])], axis=1) / np.sqrt(SEQ * 2.0 * P)
    channels[:, 0] /= 2
    cos_tokens, sin_tokens = np.cos(turn(n, s, SEQ)), np.sin(turn(n, s[:HALF], SEQ))
    return {"c_ident": np.eye(P, dtype=np.float32), "c_masks": masks, "c_small": small, "c_ids": ids, "c_negdist": negdist,
            "c_dft_channels": channels.astype(np.float32), "c_cos_tokens": cos_tokens.astype(np.float32),
            "c_sin_tokens": sin_tokens.astype(np.float32), "c_alternating": (1.0 - 2.0 * (s % 2))[None].astype(np.float32)}


def kernel(**inputs):
    import numpy as _np
    import concourse.bacc as _bacc
    from concourse.bass_utils import run_bass_kernel_spmd as _run

    nc = _bacc.Bacc("TRN2", target_bir_lowering=False, num_devices=1)
    arrays, io = {}, {}
    token = _np.concatenate([_np.arange(HALF), [HALF], SEQ - _np.arange(1, HALF)])
    ins = {n: inputs[n] for n in _INS}
    ins["x"] = ins["x"][0][token]
    wf = ins.pop("w_fourier")[0].reshape(GROUPS_F, 2 * P, D)
    ins["w_fourier_direct"], ins["w_fourier_mirror"], ins["w_fourier_128"] = wf[:, :P], wf[:, -_np.arange(P)], wf[:, P]
    for name, a in {**ins, **shape_constants()}.items():
        a = _np.ascontiguousarray(a)
        arrays[f"in_{name}"] = a
        io[name] = nc.dram_tensor(f"in_{name}", a.shape, F32, kind="ExternalInput").ap()
    io["out"] = nc.dram_tensor("out_0", (SEQ, D), F32, kind="ExternalOutput").ap()
    build(nc, io)
    r = _run(nc, [arrays], core_ids=[0])
    out = _np.empty_like(r.results[0]["out_0"])
    out[token] = r.results[0]["out_0"]
    return out[None]
```

```python
from contextlib import ExitStack, contextmanager

import concourse.bass as bass
from concourse import mybir

F32 = mybir.dt.float32
F32R = mybir.dt.float32r
I32 = mybir.dt.int32
U32 = mybir.dt.uint32
ALU = mybir.AluOpType
ACT = mybir.ActivationFunctionType
AX = mybir.AxisListType.X

P = 128
D = 1024
SEQ = 1024
T = SEQ // P
KT = D // P
HALF = 512
HEADS = 4
QK = 64
VD = 128
SSD_H = 8
SSD_W = 512
XBC = 768
XBC_T = XBC // P
CONV = 5
COL_V, COL_Z, COL_XBC, COL_DT = 1024, 1536, 2048, 2816
EXPERTS = 32
GROUPS = 4
GROUPS_F = 4
PER_GROUP = EXPERTS // GROUPS
LOGITS = GROUPS + EXPERTS
HID = 256
MAX_BLOCKS = EXPERTS + 2 * SEQ // P
SLOT_BLOCKS = MAX_BLOCKS + 4
BIG = 1.0e30
EPS = 1e-6
SLOPES = [2.0 ** (-8.0 * (h + 1) / HEADS) for h in range(HEADS)]
LAMBDA_INIT = 0.8 - 0.6
EMPTY = 1 << 20
ROW_CONVW, ROW_CONVB, ROW_SSDN, ROW_SUBLN, ROW_QN, ROW_KN, N_ROWS = 0, 30, 36, 40, 41, 42, 43
M_LE, M_GT, M_GE, M_LT, M_ONE = range(5)


class Shared:
    pass


def wait(eng, sem, value):
    if isinstance(value, int) and value <= 0:
        return
    eng.wait_ge(sem, value)


class Chain:

    def __init__(self, eng, sem):
        self.eng, self.sem, self.n = eng, sem, 0

    def __call__(self, ins):
        ins.then_inc(self.sem, 1)
        self.n = self.n + 1
        self.eng.wait_ge(self.sem, self.n)


def tt(e, out, a, b, op):
    return e.tensor_tensor(out=out, in0=a, in1=b, op=op)


class Constants:

    def __init__(self, nc, g, ctx):
        self.g = g
        self.rows = ctx.enter_context(nc.sbuf_tensor("rows", [P, P], F32))
        self.lam4 = ctx.enter_context(nc.sbuf_tensor("lam4", [P, 4, QK], F32))
        self.loaded, self.n = g.sem("constants_loaded"), 0

    def load(self, sp):
        g, io, rows = self.g, self.g.io, self.rows
        pairs = [(g.masks[:], io["c_masks"]), (g.small[:], io["c_small"].partition_broadcast(P)), (g.ids[:], io["c_ids"]),
                 (rows[0:30, :], io["conv_w"][0].rearrange("k (c p) -> (k c) p", p=P)),
                 (rows[30:36, :], io["conv_b"][0].rearrange("(c p) -> c p", p=P)),
                 (rows[36:40, :], io["ssd_norm"][0].rearrange("(c p) -> c p", p=P)),
                 (rows[40:41, :], io["attn_subln"]),
                 (g.dtb[:, 0:16], io["dt_bias"][0].rearrange("a h -> (a h)").partition_broadcast(P)),
                 (g.dtb[:, 16:32], io["a_log"][0].rearrange("a h -> (a h)").partition_broadcast(P)),
                 (g.dskip[:], io["d_skip"][0].partition_broadcast(P))]
        for c in range(2):
            pairs += [(rows[41:42, c * QK:(c + 1) * QK], io["q_norm"]), (rows[42:43, c * QK:(c + 1) * QK], io["k_norm"])]
        for n, name in enumerate(("lambda_q1", "lambda_k1", "lambda_q2", "lambda_k2")):
            pairs.append((self.lam4[:, n, :], io[name][0].partition_broadcast(P)))
        for dst, src in pairs:
            sp.dma_start(dst, src).then_inc(self.loaded, 16)
        self.n = len(pairs)


def prepare_constants(nc, g, c):
    rows, lam4, loaded = c.rows, c.lam4, 16 * c.n
    with ExitStack() as ctx:
        lamp = ctx.enter_context(nc.sbuf_tensor("lamp", [P, 2, QK], F32))
        lams = ctx.enter_context(nc.sbuf_tensor("lams", [P, 2], F32))
        rt = g.sem("rows_transposed")
        ds, ls, es = g.sem("dve_const_step"), g.sem("lambda_sums_ready"), g.sem("lambda_exps_ready")
        with nc.Block() as block:
            @block.scalar
            def _(act):
                act.wait_ge(ls, 1)
                nc.scalar.activation(lams[:], lams[:], ACT.Exp).then_inc(es, 1)
                act.wait_ge(c.loaded, loaded)
                nc.scalar.activation(g.dtb[:, 16:32], g.dtb[:, 16:32], ACT.Exp).then_inc(es, 1)

            @block.tensor
            def _(pe):
                pe.wait_ge(c.loaded, loaded)
                nc.tensor.transpose(g.ps[:, 0, 0:N_ROWS], rows[0:N_ROWS, :], g.ident[0:N_ROWS, 0:N_ROWS]).then_inc(rt, 1)

            @block.vector
            def _(dve):
                step = Chain(dve, ds)
                dve.wait_ge(c.loaded, loaded)
                step(tt(nc.vector, lamp[:, 0, :], lam4[:, 0, :], lam4[:, 1, :], ALU.mult))
                step(tt(nc.vector, lamp[:, 1, :], lam4[:, 2, :], lam4[:, 3, :], ALU.mult))
                nc.vector.tensor_reduce(out=lams[:], in_=lamp[:], axis=AX, op=ALU.add).then_inc(ls, 1)
                dve.wait_ge(es, 2)
                step(tt(nc.vector, g.neglam[:], lams[:, 1:2], lams[:, 0:1], ALU.subtract))
                step(nc.vector.tensor_scalar(g.neglam[:], g.neglam[:], -LAMBDA_INIT, None, ALU.add))
                step(nc.vector.tensor_scalar(g.dtb[:, 16:32], g.dtb[:, 16:32], -1.0, None, ALU.mult))
                dve.wait_ge(rt, 1)
                step(nc.vector.tensor_copy(g.vecs[:, 0:N_ROWS], g.ps[:, 0, 0:N_ROWS]))
                for h in range(HEADS):
                    step(nc.vector.tensor_scalar(g.qscale[:, h:h + 1], g.vecs[:, ROW_QN:ROW_QN + 1],
                                                 QK ** -0.5 / SLOPES[h], None, ALU.mult))
                    step(nc.vector.memset(g.negslope[:, h:h + 1], -SLOPES[h]))
                step(nc.vector.tensor_scalar(g.vecs[:, ROW_SUBLN:ROW_SUBLN + 1], g.vecs[:, ROW_SUBLN:ROW_SUBLN + 1],
                                             1.0 - LAMBDA_INIT, None, ALU.mult))


def norm_transpose(nc, g, tag, gain, hT, h, order, blocked, x=None, start=None, low=None, stored=None, weights=None, router=None):
    slots = h.shape[1]
    io = g.io
    first = x is not None
    x = x if first else g.x
    with ExitStack() as ctx:
        sb = lambda n, s: ctx.enter_context(nc.sbuf_tensor(f"{n}_{tag}", s, F32))
        gb, junk, ss, rs = sb("gain_b", [P, D]), sb("squares", [P, D]), sb("sumsq", [P, T]), sb("rstd", [P, T])
        gl, ssr, rsr = g.sem(f"gain_loaded_{tag}"), g.sem(f"sumsq_ready_{tag}"), g.sem(f"rstd_step_{tag}")
        hr, tr = g.sem(f"h_ready_{tag}"), g.sem(f"h_transposed_{tag}")
        if first:
            xl = [g.sem(f"x_loaded{t}_{tag}") for t in range(T)]
            idl, mhr = g.sem("identity_loaded"), g.sem("minus_half_ready")
        if router is not None:
            rw, lt = sb("router_w", [P, KT, LOGITS]), sb("logits_T", [LOGITS, 2, 2 * P])
            lt_used = g.sem(f"logits_transposed_{tag}")
            rl, lp, lc = g.sem(f"router_loaded_{tag}"), g.sem(f"logits_T_ready_{tag}"), g.sem(f"logits_T_copied_{tag}")
            rgw = io["router_group_w"][router].rearrange("(p j) g -> p j g", j=KT)
            rew = io["router_expert_w"][router].rearrange("(p j) g e -> p j (g e)", j=KT)
        by_feature = lambda t: g.ps[:, 2 * (t % 2):2 * (t % 2) + 2, :].rearrange("p a (j n) -> p (a j) n", n=P)
        ea, ed = g.sem(f"hT_low_ready_{tag}"), g.sem(f"hT_high_ready_{tag}")
        with nc.Block() as block:
            @block.sync
            def _(sp):
                if first:
                    sp.dma_start(x[:, 0, :], io["x"][0:P, :]).then_inc(xl[0], 16)
                    sp.dma_start(g.ident[:], io["c_ident"]).then_inc(idl, 16)
                sp.dma_start(gb[:], gain.partition_broadcast(P)).then_inc(gl, 16)
                if first:
                    for t in range(1, T):
                        sp.dma_start(x[:, t, :], io["x"][t * P:(t + 1) * P, :]).then_inc(xl[t], 16)
                    constants, w = start
                    constants.load(sp)
                    w.load(sp, 0)
                if router is not None:
                    with nc.allow_non_contiguous_dma("router weights, rows of 4 and 32"):
                        sp.dma_start(rw[:, :, 0:GROUPS], rgw).then_inc(rl, 16)
                        sp.dma_start(rw[:, :, GROUPS:], rew).then_inc(rl, 16)
                if weights is not None:
                    for s in range(2):
                        for n in range(2):
                            load_w13(sp, weights, n, s, s)
                    load_w2(sp, weights, 0, 0)
                if stored is not None:
                    for t in range(T):
                        sp.wait_ge(hr, t + 1)
                        sp.dma_start(g.h_rows[t * P:(t + 1) * P, :], h[:, t, :]).then_inc(stored, 16)

            @block.scalar
            def _(act):
                def squares(t):
                    if first:
                        act.wait_ge(xl[t], 16)
                    wait(act, ssr, t)
                    nc.scalar.activation(junk[:], x[:, t, :], ACT.Square, accum_out=ss[:, t:t + 1]).then_inc(ssr, 1)

                def copy_logits(q):
                    act.wait_ge(lp, q + 1)
                    wait(act, lt_used, q - 1)
                    nc.scalar.activation(lt[:, q % 2, :], g.ps[0:LOGITS, 4 + q % 2, 0:2 * P], ACT.Copy).then_inc(lc, 1)

                squares(0)
                squares(1)
                for t in range(T):
                    if t + 2 < T:
                        squares(t + 2)
                    act.wait_ge(tr, t + 1)
                    for dst, src in order(t):
                        if low is not None:
                            last = nc.scalar.activation(hT[:, :, dst], by_feature(t)[:, :, src], ACT.Copy)
                        else:
                            last = nc.scalar.activation(hT[:, 0:4, dst], by_feature(t)[:, 0:4, src], ACT.Copy)
                    last.then_inc(ea, 1)
                    if router is not None and t % 2 == 1 and t > 1:
                        copy_logits(t // 2 - 1)
                if router is not None:
                    copy_logits(T // 2 - 1)

            @block.gpsimd
            def _(pool):
                if first:
                    nc.gpsimd.memset(g.mhalf[:], -0.5).then_inc(mhr, 1)
                    pool.wait_ge(mhr, 1)
                for t in range(T):
                    pool.wait_ge(ssr, t + 1)
                    nc.gpsimd.tensor_scalar(rs[:, t:t + 1], ss[:, t:t + 1], 1.0 / D, EPS, ALU.mult, ALU.add).then_inc(rsr, 1)
                    pool.wait_ge(rsr, 2 * t + 1)
                    tt(nc.gpsimd, rs[:, t:t + 1], rs[:, t:t + 1], g.mhalf[:, 0:1], ALU.pow).then_inc(rsr, 1)

            @block.vector
            def _(dve):
                dve.wait_ge(gl, 16)

                def normed(t):
                    dve.wait_ge(rsr, 2 * t + 2)
                    if first:
                        dve.wait_ge(xl[t], 16)
                    if slots < T:
                        wait(dve, tr, t - slots + 1)
                    nc.vector.scalar_tensor_tensor(out=h[:, t % slots, :], in0=x[:, t, :], scalar=rs[:, t:t + 1], in1=gb[:],
                                                   op0=ALU.mult, op1=ALU.mult).then_inc(hr, 1)

                normed(0)
                for t in range(T):
                    if t + 1 < T:
                        normed(t + 1)
                    dve.wait_ge(tr, t + 1)
                    if low is not None:
                        dve.wait_ge(ea, t + 1)
                    for dst, src in order(t):
                        if low is not None:
                            last = tt(nc.vector, low[:, :, dst], by_feature(t)[:, :, src], hT[:, :, dst].bitcast(F32), ALU.subtract)
                        else:
                            last = nc.vector.tensor_copy(hT[:, 4:8, dst], by_feature(t)[:, 4:8, src])
                    last.then_inc(ed, 1)

            @block.tensor
            def _(pe):
                def logits(q):
                    pe.wait_ge(rl, 32)
                    pe.wait_ge(ea, 2 * q + 2)
                    pe.wait_ge(ed, 2 * q + 2)
                    wait(pe, lc, q - 1)
                    for j in range(KT):
                        last = nc.tensor.matmul(g.ps[0:LOGITS, 4 + q % 2, 0:2 * P], rw[:, j, :], hT[:, j, 2 * q * P:(2 * q + 2) * P], start=j == 0, stop=j == KT - 1)
                    last.then_inc(lp, 1)

                def by_token(q):
                    pe.wait_ge(lc, q + 1)
                    for t in (2 * q, 2 * q + 1):
                        last = nc.tensor.transpose(g.ps[:, 6, t * LOGITS:(t + 1) * LOGITS], lt[:, q % 2, (t % 2) * P:(t % 2 + 1) * P], g.ident[0:LOGITS, 0:LOGITS])
                    last.then_inc(lt_used, 1)

                if first:
                    pe.wait_ge(idl, 16)
                for t in range(T):
                    pe.wait_ge(hr, t + 1)
                    wait(pe, ea, t - 1)
                    wait(pe, ed, t - 1)
                    hv = h[:, t % slots, :]
                    for j in range(KT):
                        src = hv[:, j * P:(j + 1) * P] if blocked else hv.rearrange("p (q j) -> p j q", j=KT)[:, j, :]
                        last = nc.tensor.transpose(g.ps[:, 2 * (t % 2) + j // 4, (j % 4) * P:(j % 4 + 1) * P], src, g.ident[:])
                    last.then_inc(tr, 1)
                    if router is not None and t % 2 == 0 and t > 0:
                        logits(t // 2 - 1)
                    if router is not None and t % 2 == 1 and t > 1:
                        by_token(t // 2 - 1)
                if router is not None:
                    logits(T // 2 - 1)
                    by_token(T // 2 - 1)


def order_mirrored(t):
    if t < 4:
        return [(slice(t * P, (t + 1) * P), slice(0, P))]
    a = (11 - t) * P + 1
    if t > 4:
        return [(slice(a, a + P), slice(None, None, -1))]
    return [(slice(a, a + P - 1), slice(P - 1, 0, -1)), (slice(HALF, HALF + 1), slice(0, 1))]


def order_same(t):
    return [(slice(t * P, (t + 1) * P), slice(0, P))]


class InputWeights:
    W = 2 * P + 16
    N = 5

    def __init__(self, nc, g, ctx):
        self.w_in = g.io["w_in"][0].rearrange("(p j) n -> p j n", j=KT)
        self.raw = ctx.enter_context(nc.sbuf_tensor("w_ssd_raw", [P, KT, self.W], F32))
        self.loaded = g.sem("w_ssd_loaded")
        self.cols = [COL_XBC + n * 2 * P for n in range(3)] + [COL_Z + n * 2 * P for n in range(2)]

    def width(self, k):
        return self.W if k == self.N - 1 else 2 * P

    def load(self, sp, k):
        sp.dma_start(self.raw[:, :, 0:2 * P], self.w_in[:, :, self.cols[k]:self.cols[k] + 2 * P]).then_inc(self.loaded, 16)
        if k == self.N - 1:
            sp.dma_start(self.raw[:, :, 2 * P:], self.w_in[:, :, COL_DT:COL_DT + 16]).then_inc(self.loaded, 16)

    def wait_loaded(self, eng, k):
        eng.wait_ge(self.loaded, 16 * (k + 1 + (k == self.N - 1)))


def ssd_project(nc, g, w, hT, low, xbcT, xs, mixed, draw):
    with ExitStack() as ctx:
        hi, lo = (ctx.enter_context(nc.sbuf_tensor(f"w_ssd_{n}", [P, 2, KT, w.W], F32R)) for n in ("hi", "lo"))
        acc = ctx.enter_context(nc.sbuf_tensor("conv_acc", [P, 2, SEQ], F32))
        pr, ev, pads = g.sem("ssd_unit_ready"), g.sem("ssd_unit_read"), g.sem("conv_pads_ready")
        whr, wlr = g.sem("w_ssd_hi_ready"), g.sem("w_ssd_lo_ready")
        cs, cv, sl, xt, xe = g.sem("conv_step"), g.sem("conv_ready"), g.sem("silu_ready"), g.sem("x_transposed"), g.sem("x_by_token_ready")
        NX = 2 * XBC_T
        with nc.Block() as block:
            @block.sync
            def _(sp):
                for k in range(1, w.N):
                    sp.wait_ge(wlr, k)
                    w.load(sp, k)

            @block.gpsimd
            def _(pool):
                nc.gpsimd.memset(xbcT[:, :, 0:2], 0.0).then_inc(pads, 1)
                nc.gpsimd.memset(xbcT[:, :, SEQ + 2:SEQ + 4], 0.0).then_inc(pads, 1)

            @block.tensor
            def _(pe):
                def unit(u, k, weights, moving, n):
                    pe.wait_ge(wlr, k + 1)
                    wait(pe, ev, u - 3)
                    for j in range(KT):
                        for m, (a, b) in enumerate(((0, 0), (0, 1), (1, 0))):
                            last = nc.tensor.matmul(g.ps[:, u % 4, 0:n], weights[a](j), moving[b](j), start=j == 0 and m == 0, stop=j == KT - 1 and m == 2)
                    last.then_inc(pr, 1)

                for u in range(NX):
                    ct, half = u // 2, u % 2
                    k, c = ct // 2, ct % 2
                    unit(u, k, [lambda j, v=v: v[:, k % 2, j, c * P:(c + 1) * P] for v in (hi, lo)],
                         [lambda j, v=v: v[:, j, half * HALF:(half + 1) * HALF] for v in (hT, low)], HALF)
                for k in (3, 4):
                    for t in range(T):
                        unit(NX + T * (k - 3) + t, k, [lambda j, v=v: v[:, j, t * P:(t + 1) * P] for v in (hT, low)],
                             [lambda j, v=v: v[:, k % 2, j, 0:w.width(k)] for v in (hi, lo)], w.width(k))
                    if k == 3:
                        for c in range(T):
                            pe.wait_ge(sl, 5)
                            wait(pe, xe, c - 1)
                            for ct in range(5):
                                last = nc.tensor.transpose(g.ps[:, 4 + 2 * (c % 2) + ct // 4, (ct % 4) * P:(ct % 4 + 1) * P],
                                                           xbcT[:, ct, c * P:(c + 1) * P], g.ident[:])
                            last.then_inc(xt, 1)

            @block.scalar
            def _(act):
                def split_w(k):
                    w.wait_loaded(act, k)
                    wait(act, pr, 4 * (k - 1))
                    nc.scalar.activation(hi[:, k % 2, :, 0:w.width(k)], w.raw[:, :, 0:w.width(k)], ACT.Copy).then_inc(whr, 1)

                def silu(ct):
                    act.wait_ge(cv, ct + 1)
                    nc.scalar.activation(xbcT[:, ct, 0:SEQ], acc[:, ct % 2, :], ACT.Silu).then_inc(sl, 1)

                split_w(0)
                split_w(1)
                for u in range(NX):
                    ct, half = u // 2, u % 2
                    act.wait_ge(pr, u + 1)
                    nc.scalar.activation(xbcT[:, ct, 2 + half * HALF:2 + (half + 1) * HALF], g.ps[:, u % 4, :], ACT.Copy).then_inc(ev, 1)
                    if half == 1 and ct > 0:
                        silu(ct - 1)
                    if u % 4 == 3:
                        split_w(u // 4 + 2)
                for n in range(2 * T):
                    u, t = NX + n, n % T
                    act.wait_ge(pr, u + 1)
                    z = SSD_W + (n // T) * 2 * P
                    ins = nc.scalar.activation(mixed[:, t, z:z + 2 * P], g.ps[:, u % 4, 0:2 * P], ACT.Silu)
                    if n >= T:
                        ins = nc.scalar.activation(draw[:, t, :], g.ps[:, u % 4, 2 * P:w.W], ACT.Copy)
                    ins.then_inc(ev, 1)
                    if n == 2:
                        silu(XBC_T - 1)
                    if n == T - 1:
                        for c in range(T):
                            act.wait_ge(xt, c + 1)
                            nc.scalar.activation(xs[:, c, 0:640], g.ps[:, 4 + 2 * (c % 2):6 + 2 * (c % 2), :].rearrange("p a n -> p (a n)")[:, 0:640],
                                                 ACT.Copy).then_inc(xe, 1)

            @block.vector
            def _(dve):
                step = Chain(dve, cs)

                def split_w(k):
                    wait(dve, pr, 4 * (k - 1))
                    dve.wait_ge(whr, k + 1)
                    cut = slice(0, w.width(k))
                    tt(nc.vector, lo[:, k % 2, :, cut], w.raw[:, :, cut], hi[:, k % 2, :, cut].bitcast(F32), ALU.subtract).then_inc(wlr, 1)

                split_w(0)
                split_w(1)
                dve.wait_ge(pads, 2)
                for ct in range(XBC_T):
                    dve.wait_ge(ev, 2 * ct + 2)
                    wait(dve, sl, ct - 1)
                    a = acc[:, ct % 2, :]
                    v = lambda k: g.vecs[:, ROW_CONVW + k * XBC_T + ct:ROW_CONVW + k * XBC_T + ct + 1]
                    step(nc.vector.tensor_scalar(a, xbcT[:, ct, 0:SEQ], v(0), g.vecs[:, ROW_CONVB + ct:ROW_CONVB + ct + 1], ALU.mult, ALU.add))
                    for k in range(1, CONV):
                        ins = nc.vector.scalar_tensor_tensor(out=a, in0=xbcT[:, ct, k:k + SEQ], scalar=v(k), in1=a, op0=ALU.mult, op1=ALU.add)
                        if k < CONV - 1:
                            step(ins)
                    ins.then_inc(cv, 1)
                    dve.wait_ge(cv, ct + 1)
                    if ct % 2 == 1:
                        split_w(ct // 2 + 2)


def ssd_scan(nc, g, xbcT, xs, mixed, draw):
    NC = T
    with ExitStack() as ctx:
        sb = lambda n, s: ctx.enter_context(nc.sbuf_tensor(n, s, F32))
        dt, a = sb("dt", [P, NC, 16]), sb("dta", [P, NC, 16])
        r1, r2 = sb("dt_pos", [P, NC, 16]), sb("dt_abs", [P, NC, 16])
        ex = sb("decays", [P, 384])
        half_mask = lambda gr: g.masks[:, 5 * P + gr:5 * P + gr + 1]
        am = ctx.enter_context(nc.sbuf_tensor("a_masked", [P, 2, 2, SSD_H, P], F32R))
        ahl = sb("dta_parts", [P, 2, NC, 16])
        a_hi = ctx.enter_context(nc.sbuf_tensor("dta_hi", [P, NC, 16], F32R))
        masks_r = ctx.enter_context(nc.sbuf_tensor("masks_r", [P, 2, P], F32R))
        lm = sb("l_mat", [P, 2, 2, SSD_H, P])
        cb = sb("cb_masked", [P, 2, 2, P])
        xd = sb("x_dt", [P, 2, SSD_W])
        xw = sb("x_decayed", [P, 2, SSD_W])
        st = sb("state", [P, 2, SSD_W])
        off = sb("y_off", [P, SSD_W])
        y = mixed[:, :, 0:SSD_W]
        junk = sb("y_squares", [P, SSD_W])
        ss, rs = sb("ssd_sumsq", [P, NC]), sb("ssd_rstd", [P, NC])
        dtm = [g.sem(f"softplus_{n}") for n in ("in", "exp", "ln")]
        ar, cum, exr, wdr = g.sem("dta_ready"), g.sem("cumsums_ready"), g.sem("decays_ready"), g.sem("state_weights_ready")
        vs, apr, mkr = g.sem("dve_ssd_step"), g.sem("dta_parts_ready"), g.sem("masks_r_ready")
        amr, seg, lr, mr = g.sem("a_masked_ready"), g.sem("segsum_ready"), g.sem("l_exp_ready"), g.sem("m_ready")
        cbr, yd, ydr = g.sem("cb_ready"), g.sem("y_diag_ready"), g.sem("y_diag_added")
        xdr, xwr, inc, inr = g.sem("x_dt_ready"), g.sem("x_decayed_ready"), g.sem("state_inc_ready"), g.sem("state_updated")
        yo, yor, cbu = g.sem("y_off_ready"), g.sem("y_off_added"), g.sem("cb_read")
        yg, sq, fin = g.sem("y_gated"), g.sem("ssd_squares_ready"), g.sem("ssd_rstd_step")
        mask = lambda m: g.masks[:, m * P:(m + 1) * P]
        bh = lambda v: v.unsqueeze(2).to_broadcast([P, SSD_H, 64])
        hv = lambda v: v.rearrange("p (h n) -> p h n", h=SSD_H)
        dirs = lambda i: (i, NC - 1 - i)
        done_order = [c for i in range(NC // 2, NC) for c in dirs(i)]
        with nc.Block() as block:
            @block.scalar
            def _(act):
                act.wait_ge(dtm[0], 1)
                nc.scalar.activation(r2[:], r2[:], ACT.Exp, scale=-1.0).then_inc(dtm[1], 1)
                act.wait_ge(dtm[1], 1)
                nc.scalar.activation(r2[:], r2[:], ACT.Ln, bias=1.0).then_inc(dtm[2], 1)
                act.wait_ge(cum, 1)
                nc.scalar.activation(ex[:], g.ps[:, 7, 0:384], ACT.Exp).then_inc(exr, 1)
                e4 = ex[:, 0:256].rearrange("p (q c h) -> p q c h", q=4, h=SSD_H)

                def decayed(i):
                    for d in range(2):
                        c = dirs(i)[d]
                        wait(act, inc, 2 * (i - 1) + d + 1)
                        for h in range(SSD_H):
                            cols = slice(64 * h, 64 * h + 64)
                            last = nc.scalar.activation(xw[:, d, cols], xs[:, c, cols], ACT.Copy, scale=e4[:, 2 + d, c, h:h + 1])
                        last.then_inc(xwr, 1)

                act.wait_ge(wdr, 2)
                decayed(0)
                for i in range(NC):
                    if 0 < i < NC - 1:
                        decayed(i)
                    act.wait_ge(seg, i + 1)
                    wait(act, yd, i - 1)
                    nc.scalar.activation(lm[:, i % 2, 0].rearrange("p h n -> p (h n)"), g.ps[:, 0:2, :].rearrange("p a n -> p (a n)"),
                                         ACT.Exp).then_inc(lr, 1)
                for n, c in enumerate(done_order):
                    act.wait_ge(yg, n + 1)
                    wait(act, sq, n)
                    nc.scalar.activation(junk[:], y[:, c, :], ACT.Square, accum_out=ss[:, c:c + 1]).then_inc(sq, 1)
                act.wait_ge(fin, 2)
                for c in range(0, NC, 2):
                    nc.scalar.activation(mixed[:, c, SSD_W:], y[:, c, :], ACT.Copy, scale=rs[:, c:c + 1])

            @block.tensor
            def _(pe):
                pe.wait_ge(ar, 1)
                for n, (m, d) in enumerate(((M_LE, 0), (M_GE, 1), (M_GT, 0), (M_LT, 1))):
                    nc.tensor.matmul(g.ps[:, 7, 64 * n:64 * n + 64], mask(m), a[:, :, 8 * d:8 * d + 8], start=True, stop=True)
                nc.tensor.matmul(g.ps[:, 7, 256:384], mask(M_ONE), a[:].rearrange("p c n -> p (c n)"), start=True, stop=True).then_inc(cum, 1)

                def segsums(i):
                    pe.wait_ge(amr, 4 * i + 4)
                    wait(pe, lr, i)
                    for half in range(2):
                        for n, (d, part) in enumerate(((0, 0), (0, 1), (1, 0), (1, 1))):
                            last = nc.tensor.matmul(g.ps[:, half, :], masks_r[:, d, :],
                                                    am[:, part, d].rearrange("p h n -> p (h n)")[:, half * HALF:(half + 1) * HALF], start=n == 0, stop=n == 3)
                    last.then_inc(seg, 1)

                def cb_products(i):
                    wait(pe, cbu, 2 * i)
                    for gr in range(2):
                        rows = slice(64 * gr, 64 * gr + 64)
                        nc.tensor.matmul(g.ps[:, 2, gr * P:(gr + 1) * P], xbcT[rows, 4, i * P:(i + 1) * P],
                                         xbcT[rows, 5, i * P:(i + 1) * P], start=True, stop=True).then_inc(cbr, 1)
                        if gr == 0:
                            pe.wait_ge(cbr, 2 * i + 1)

                cb_products(0)
                pe.wait_ge(mkr, 1)
                segsums(0)
                for i in range(NC):
                    if i + 1 < NC:
                        cb_products(i + 1)
                    if i > 0:
                        for d in range(2):
                            c = dirs(i)[d]
                            pe.wait_ge(inr, 2 * (i - 1) + d + 1)
                            wait(pe, yor, 2 * (i - 2) + d + 1)
                            nc.tensor.matmul(g.ps[:, (6, 4)[d], :], xbcT[:, 5, c * P:(c + 1) * P], st[:, d, :], start=True, stop=True).then_inc(yo, 1)
                    if i < NC - 1:
                        for d in range(2):
                            c = dirs(i)[d]
                            pe.wait_ge(xwr, 2 * i + d + 1)
                            wait(pe, inr, 2 * (i - 1) + d + 1)
                            if i == 0 and d == 0:
                                pe.wait_ge(exr, 1)
                            nc.tensor.matmul(g.ps[:, (7, 3)[d], :], xs[:, c, SSD_W:SSD_W + P], xw[:, d, :], start=True, stop=True).then_inc(inc, 1)
                    if i + 1 < NC:
                        segsums(i + 1)
                    pe.wait_ge(mr, i + 1)
                    pe.wait_ge(xdr, 2 * i + 2)
                    wait(pe, ydr, i)
                    for h in range(SSD_H):
                        for d in range(2):
                            last = nc.tensor.matmul(g.ps[:, 5, h * 64:h * 64 + 64], lm[:, i % 2, d, h, :], xd[:, d, h * 64:h * 64 + 64],
                                                    start=d == 0, stop=d == 1)
                    last.then_inc(yd, 1)

            @block.gpsimd
            def _(pool):
                pool.wait_ge(apr, 2)

                def masked(i):
                    wait(pool, seg, i)
                    for part in range(2):
                        for d in range(2):
                            tt(nc.gpsimd, am[:, part, d], mask((M_LE, M_GE)[d]).unsqueeze(1).to_broadcast([P, SSD_H, P]),
                               ahl[:, part, i, 8 * d:8 * d + 8].unsqueeze(2).to_broadcast([P, SSD_H, P]), ALU.mult).then_inc(amr, 1)

                def gated(n):
                    c = done_order[n]
                    pool.wait_ge(ydr, c + 1)
                    pool.wait_ge(yor, max(2 * c - 1 if c > 0 else 0, 2 * (NC - 1 - c) if c < NC - 1 else 0))
                    tt(nc.gpsimd, y[:, c, :], y[:, c, :], mixed[:, c, SSD_W:], ALU.mult).then_inc(yg, 1)

                masked(0)
                masked(1)
                for i in range(NC):
                    for d in range(2):
                        wait(pool, yd, i)
                        tt(nc.gpsimd, hv(xd[:, d, :]), hv(xs[:, i, 0:SSD_W]), bh(dt[:, i, 8 * d:8 * d + 8]), ALU.mult).then_inc(xdr, 1)
                    if i + 2 < NC:
                        masked(i + 2)
                    if i > NC // 2 + 1:
                        for n in range(2):
                            gated(2 * (i - NC // 2 - 2) + n)
                for n in range(2 * (NC // 2 - 2), NC):
                    gated(n)
                pool.wait_ge(sq, NC)
                nc.gpsimd.tensor_scalar(rs[:], ss[:], 1.0 / SSD_W, EPS, ALU.mult, ALU.add).then_inc(fin, 1)
                pool.wait_ge(fin, 1)
                tt(nc.gpsimd, rs[:], rs[:], g.mhalf[:, 0:NC], ALU.pow).then_inc(fin, 1)

            @block.vector
            def _(dve):
                step = Chain(dve, vs)
                V = nc.vector
                b3 = lambda v: v.unsqueeze(1).to_broadcast([P, NC, 16])
                step(tt(V, r1[:], draw[:], b3(g.dtb[:, 0:16]), ALU.add))
                V.scalar_tensor_tensor(out=r2[:], in0=r1[:], scalar=-1.0, in1=r1[:], op0=ALU.mult, op1=ALU.max).then_inc(dtm[0], 1)
                dve.wait_ge(dtm[0], 1)
                step(V.tensor_scalar(r1[:], r1[:], 0.0, None, ALU.max))
                dve.wait_ge(dtm[2], 1)
                step(tt(V, dt[:], r1[:], r2[:], ALU.add))
                tt(V, a[:], dt[:], b3(g.dtb[:, 16:32]), ALU.mult).then_inc(ar, 1)
                dve.wait_ge(ar, 1)
                step(V.tensor_copy(a_hi[:], a[:]))
                V.tensor_copy(ahl[:, 0], a_hi[:].bitcast(F32)).then_inc(apr, 1)
                tt(V, ahl[:, 1], a[:], a_hi[:].bitcast(F32), ALU.subtract).then_inc(apr, 1)
                for d in range(2):
                    ins = V.tensor_copy(masks_r[:, d, :], mask((M_GT, M_LT)[d]))
                ins.then_inc(mkr, 1)

                def start_sum(c):
                    return tt(V, hv(y[:, c, :]), hv(xs[:, c, 0:SSD_W]), bh(g.dskip[:]), ALU.mult)

                def mask_cb(i):
                    dve.wait_ge(cbr, 2 * i + 2)
                    wait(dve, mr, i)
                    for d in range(2):
                        tt(V, cb[:, d], g.ps[:, 2, 0:2 * P].rearrange("p (g n) -> p g n", g=2), mask((M_LE, M_GE)[d]).unsqueeze(1).to_broadcast([P, 2, P]), ALU.mult).then_inc(cbu, 1)

                def add_diagonal(i):
                    dve.wait_ge(yd, i + 1)
                    wait(dve, yor, 2 * i)
                    tt(V, y[:, i, :], y[:, i, :], g.ps[:, 5, :], ALU.add).then_inc(ydr, 1)
                    dve.wait_ge(ydr, i + 1)

                start_sum(0)
                step(start_sum(NC - 1))
                e4 = ex[:, 0:256].rearrange("p (q c h) -> p q c h", q=4, h=SSD_H)
                e5 = ex[:, 256:384].rearrange("p (c q) -> p c q", q=16)
                dve.wait_ge(exr, 1)
                dve.wait_ge(ar, 1)
                for d in range(2):
                    tt(V, e4[:, 2 + d], e4[:, 2 + d], dt[:, :, 8 * d:8 * d + 8], ALU.mult).then_inc(wdr, 1)
                mask_cb(0)
                for i in range(NC):
                    dve.wait_ge(lr, i + 1)
                    dve.wait_ge(cbu, 2 * i + 2)
                    for d in (1, 0):
                        for gr in range(2):
                            ins = tt(V, lm[:, i % 2, d, 4 * gr:4 * gr + 4, :], lm[:, i % 2, 0, 4 * gr:4 * gr + 4, :],
                                     cb[:, d, gr, :].unsqueeze(1).to_broadcast([P, 4, P]), ALU.mult)
                        if d == 1:
                            step(ins)
                    ins.then_inc(mr, 1)
                    if i > 0:
                        add_diagonal(i - 1)
                    for d in range(2):
                        c = dirs(i)[d]
                        n = 2 * (i - 1) + d
                        if i > 0:
                            dve.wait_ge(yo, n + 1)
                            wait(dve, yor, n)
                            ins = tt(V, hv(off[:]), hv(g.ps[:, (6, 4)[d], :]), bh(e4[:, d, c]), ALU.mult)
                            if i < NC - 1:
                                ins = tt(V, hv(st[:, d, :]), hv(st[:, d, :]), bh(e5[:, c, 8 * d:8 * d + 8]), ALU.mult)
                            step(ins)
                            tt(V, y[:, c, :], y[:, c, :], off[:], ALU.add).then_inc(yor, 1)
                        if i < NC - 1:
                            dve.wait_ge(inc, 2 * i + d + 1)
                            for gr in range(2):
                                cols = slice(256 * gr, 256 * gr + 256)
                                if i == 0:
                                    ins = V.tensor_scalar(st[:, d, cols], g.ps[:, (7, 3)[d], cols], half_mask(gr), None, ALU.mult)
                                else:
                                    ins = V.scalar_tensor_tensor(out=st[:, d, cols], in0=g.ps[:, (7, 3)[d], cols], scalar=half_mask(gr), in1=st[:, d, cols],
                                                                 op0=ALU.mult, op1=ALU.add)
                            ins.then_inc(inr, 1)
                    if i + 1 < NC:
                        mask_cb(i + 1)
                    if i < NC // 2 - 1:
                        start_sum(i + 1)
                        step(start_sum(NC - 2 - i))
                add_diagonal(NC - 1)
                dve.wait_ge(fin, 2)
                for c in range(1, NC, 2):
                    V.tensor_scalar(mixed[:, c, SSD_W:], y[:, c, :], rs[:, c:c + 1], None, ALU.mult)


def attention(nc, g, hT, low, mixed):
    io = g.io
    w_in = io["w_in"][0].rearrange("(p j) n -> p j n", j=KT)
    with ExitStack() as ctx:
        sb = lambda n, s: ctx.enter_context(nc.sbuf_tensor(n, s, F32))
        w = sb("w_qkv_raw", [P, KT, P])
        w_hi, w_lo = (ctx.enter_context(nc.sbuf_tensor(f"w_qkv_{n}", [P, KT, 3, P], F32R)) for n in ("hi", "lo"))
        sbr = lambda n, s: ctx.enter_context(nc.sbuf_tensor(n, s, F32R))
        qs2, kh, kl, v = sbr("q_hi_over_lo", [P, 2, SEQ]), sbr("k_hi_twice", [P, 2, SEQ]), sbr("k_lo_twice", [P, 2, SEQ]), sb("v", [P, T, VD])
        qk, sq = sb("qk_normed", [P, 2, 4, 2, QK]), sb("qk_squares", [P, 256])
        ss, rs = sb("qk_sumsq", [P, T, 4]), sb("qk_rstd", [P, T, 4])
        dist = sb("negdist", [P, 1920])
        pr = sb("probs", [P, 2, 2, SEQ])
        first_w = lambda n: pr[:, n // 2, n % 2, :].rearrange("p (j n) -> p j n", j=KT)
        wt, wtT = sb("weights", [P, 2, SEQ]), sb("weightsT", [P, 2, SEQ])
        mx, den = sb("neg_max", [P, 2, 2]), sb("denoms", [P, T, 2])
        cf, rd = sb("coef", [P, 2]), sb("rdenom", [P, T])
        o, osq = sb("o", [P, T, VD]), sb("o_squares", [P, VD])
        oss, ors = sb("o_sumsq", [P, T]), sb("o_rstd", [P, T])
        nsl, qs = sb("neg_slope_h", [P, 1]), sb("qscale_h", [P, 1])
        dl, wl = g.sem("dist_loaded"), g.sem("w_qkv_loaded")
        whr, wlr = g.sem("w_qkv_hi_ready"), g.sem("w_qkv_lo_ready")
        pj, vr = g.sem("proj_ready"), g.sem("v_ready")
        sqr, ssr, rsr, nr = g.sem("qk_squares_ready"), g.sem("qk_sumsq_ready"), g.sem("qk_rstd_step"), g.sem("qk_normed_ready")
        tr, tq, tk = g.sem("qk_transposed"), g.sem("q_lo_ready"), g.sem("k_lo_ready")
        qhr, khr = g.sem("q_hi_ready"), g.sem("k_hi_ready")
        sr, ng, er = g.sem("scores_ready"), g.sem("neg_scores_ready"), g.sem("exp_ready")
        wr, wtr, wte = g.sem("weights_ready"), g.sem("weights_transposed"), g.sem("weightsT_ready")
        pv, oe, osr, ofs = g.sem("pv_ready"), g.sem("o_read"), g.sem("o_squares_ready"), g.sem("o_rstd_step")
        vs, fin, hd = g.sem("dve_attn_step"), g.sem("o_written"), g.sem("head_scalars_ready")
        seen, seen_p = g.sem("scores_wait_passed"), g.sem("sumsq_wait_passed")
        with nc.Block() as block:
            @block.sync
            def _(sp):
                sp.dma_start(dist[:], io["c_negdist"]).then_inc(dl, 16)

                def load(h):
                    for n in range(3):
                        wait(sp, wlr, 3 * h + n)
                        sp.dma_start(w[:], w_in[:, :, bass.ds(h * P + n * HALF, P)]).then_inc(wl, 16)

                for n in range(3):
                    sp.dma_start(first_w(n), w_in[:, :, n * HALF:n * HALF + P]).then_inc(wl, 16)
                with sp.Fori(1, HEADS) as h:
                    load(h)

            @block.tensor
            def _(pe):
                def head(h, last_head=False):
                    def transposes(t):
                        pe.wait_ge(nr, h * T + t + 1)
                        wait(pe, tq, h * T + t)
                        wait(pe, tk, h * T + t)
                        for n in range(4):
                            last = nc.tensor.transpose(g.ps[:, 7 - n // 2, (n % 2) * P:(n % 2 + 1) * P], qk[:, t % 2, n].rearrange("p r n -> p (r n)"), g.ident[:])
                        last.then_inc(tr, 1)

                    pe.wait_ge(wlr, 3 * h + 3)
                    wait(pe, ng, h * 2 * T)
                    wait(pe, oe, h * T)
                    for t in range(T):
                        if t >= 4:
                            pe.wait_ge(nr, h * T + t - 3)
                            pe.wait_ge(vr, h * T + t - 3)
                        for j in range(KT):
                            for m, (x, y) in enumerate(((hT, w_hi), (hT, w_lo), (low, w_hi))):
                                last = nc.tensor.matmul(g.ps[:, t % 4, 0:384], x[:, j, t * P:(t + 1) * P],
                                                        y[:, j, :, :].rearrange("p a n -> p (a n)"), start=j == 0 and m == 0, stop=j == KT - 1 and m == 2)
                        last.then_inc(pj, 1)
                        if t >= 1:
                            transposes(t - 1)
                    transposes(T - 1)
                    pe.wait_ge(tq, h * T + T)
                    pe.wait_ge(tk, h * T + T)
                    pe.wait_ge(vr, h * T + T)
                    for u in range(T + 3):
                        if u < T:
                            for c in range(2):
                                if u > 0:
                                    pe.wait_ge(ng, h * 2 * T + 2 * (u - 1) + c + 1)
                                for half in range(2):
                                    for k in (kh, kl):
                                        last = nc.tensor.matmul(g.ps[:, 2 * c + half, :], qs2[:, c, u * P:(u + 1) * P],
                                                                k[:, c, half * HALF:(half + 1) * HALF], start=k is kh, stop=k is kl)
                                last.then_inc(sr, 1)
                        if 2 <= u < T + 2:
                            q = u - 2
                            pe.wait_ge(wr, h * T + q + 1)
                            wait(pe, wte, h * T + q)
                            for k in range(T):
                                last = nc.tensor.transpose(g.ps[:, 4 + k // 4, (k % 4) * P:(k % 4 + 1) * P], wt[:, q % 2, k * P:(k + 1) * P], g.ident[:])
                            last.then_inc(wtr, 1)
                        if u >= 3:
                            q = u - 3
                            pe.wait_ge(wte, h * T + q + 1)
                            wait(pe, oe, h * T + q)
                            for k in range(T):
                                last = nc.tensor.matmul(g.ps[:, 6, 0:VD], wtT[:, q % 2, k * P:(k + 1) * P], v[:, k, :], start=k == 0, stop=k == T - 1)
                            last.then_inc(pv, 1)

                head(0)
                with pe.Fori(1, HEADS - 1) as h:
                    head(h)
                head(HEADS - 1, last_head=True)

            @block.scalar
            def _(act):
                def split_w(h, n):
                    wait(act, pj, h * T)
                    act.wait_ge(wl, 16 * (3 * h + n + 1))
                    nc.scalar.activation(w_hi[:, :, n, :], w[:], ACT.Copy).then_inc(whr, 1)

                act.wait_ge(wl, 48)
                for n in range(3):
                    nc.scalar.activation(w_hi[:, :, n, :], first_w(n), ACT.Copy).then_inc(whr, 1)

                def head(h, last_head=False):
                    wait(act, pv, h * T)
                    act.wait_ge(hd, 2 * h + 2)
                    for t in range(T):
                        act.wait_ge(pj, h * T + t + 1)
                        wait(act, ssr, h * T + t)
                        nc.scalar.activation(sq[:], g.ps[:, t % 4, 0:256], ACT.Square).then_inc(sqr, 1)
                        nc.scalar.activation(v[:, t, :], g.ps[:, t % 4, 256:384], ACT.Copy).then_inc(vr, 1)
                        act.wait_ge(tr, h * T + t + 1)
                        nc.scalar.activation(qs2[:, :, t * P:(t + 1) * P], g.ps[:, 7, 0:2 * P].rearrange("p (c n) -> p c n", c=2), ACT.Copy,
                                             scale=qs[:, 0:1]).then_inc(qhr, 1)
                        nc.scalar.activation(kh[:, :, t * P:(t + 1) * P], g.ps[:, 6, 0:2 * P].rearrange("p (c n) -> p c n", c=2), ACT.Copy,
                                             scale=g.vecs[:, ROW_KN:ROW_KN + 1]).then_inc(khr, 1)
                    for u in range(T + 3):
                        if u < T:
                            for c in range(2):
                                act.wait_ge(ng, h * 2 * T + 2 * u + c + 1)
                                p = pr[:, u % 2, c, :]
                                nc.scalar.activation(p, p, ACT.Exp, scale=-1.0, bias=mx[:, u % 2, c:c + 1],
                                                     accum_out=den[:, u, c:c + 1]).then_inc(er, 1)
                        if 2 <= u < T + 2:
                            q = u - 2
                            if u in (2, 4, 6) and not last_head:
                                split_w(h + 1, u // 2 - 1)
                            act.wait_ge(wtr, h * T + q + 1)
                            if q >= 2:
                                act.wait_ge(pv, h * T + q - 1)
                            nc.scalar.activation(wtT[:, q % 2, :], g.ps[:, 4:6, :].rearrange("p a n -> p (a n)"), ACT.Copy).then_inc(wte, 1)
                        if u >= 3:
                            q = u - 3
                            act.wait_ge(pv, h * T + q + 1)
                            wait(act, fin, h)
                            nc.scalar.activation(o[:, q, :], g.ps[:, 6, 0:VD], ACT.Copy, scale=rd[:, q:q + 1]).then_inc(oe, 1)
                            act.wait_ge(oe, h * T + q + 1)
                            wait(act, osr, h * T + q)
                            nc.scalar.activation(osq[:], o[:, q, :], ACT.Square, accum_out=oss[:, q:q + 1]).then_inc(osr, 1)

                head(0)
                with act.Fori(1, HEADS - 1) as h:
                    head(h)
                head(HEADS - 1, last_head=True)

            @block.gpsimd
            def _(pool):
                def split_w(h):
                    for n in range(3):
                        pool.wait_ge(whr, 3 * h + n + 1)
                        tt(nc.gpsimd, w_lo[:, :, n, :], w[:], w_hi[:, :, n, :].bitcast(F32), ALU.subtract).then_inc(wlr, 1)

                def head(h, last_head=False):
                    for t in range(T):
                        pool.wait_ge(ssr, h * T + t + 1)
                        wait(pool, nr, h * T + t)
                        pool.sem_inc(seen_p, 1)
                        nc.gpsimd.tensor_scalar(rs[:, t, :], ss[:, t, :], 1.0 / QK, EPS, ALU.mult, ALU.add).then_inc(rsr, 1)
                        pool.wait_ge(rsr, h * 2 * T + 2 * t + 1)
                        tt(nc.gpsimd, rs[:, t, :], rs[:, t, :], g.mhalf[:, 0:4], ALU.pow).then_inc(rsr, 1)
                    if not last_head:
                        split_w(h + 1)
                    pool.wait_ge(osr, h * T + T)
                    pool.sem_inc(seen_p, 1)
                    nc.gpsimd.tensor_scalar(ors[:], oss[:], 1.0 / VD, EPS, ALU.mult, ALU.add).then_inc(ofs, 1)
                    pool.wait_ge(ofs, 2 * h + 1)
                    tt(nc.gpsimd, ors[:], ors[:], g.mhalf[:, 0:T], ALU.pow).then_inc(ofs, 1)

                head(0)
                with pool.Fori(1, HEADS - 1) as h:
                    head(h)
                head(HEADS - 1, last_head=True)

            @block.vector
            def _(dve):
                V = nc.vector
                step = Chain(dve, vs)
                for n in range(3):
                    dve.wait_ge(whr, n + 1)
                    tt(V, w_lo[:, :, n, :], first_w(n), w_hi[:, :, n, :].bitcast(F32), ALU.subtract).then_inc(wlr, 1)
                dve.wait_ge(wlr, 3)
                dve.wait_ge(dl, 16)

                def head(h, last_head=False):
                    wait(dve, ng, h * 2 * T)
                    V.tensor_copy(nsl[:], g.negslope[:, bass.ds(h, 1)]).then_inc(hd, 1)
                    V.tensor_copy(qs[:], g.qscale[:, bass.ds(h, 1)]).then_inc(hd, 1)
                    dve.wait_ge(hd, 2 * h + 2)

                    def normed(t):
                        dve.wait_ge(rsr, h * 2 * T + 2 * t + 2)
                        dve.wait_ge(vr, h * T + t + 1)
                        if t >= 2:
                            dve.wait_ge(tr, h * T + t - 1)
                        for r in range(2):
                            ins = tt(V, qk[:, t % 2, :, r, :], g.ps[:, t % 4, 0:256].rearrange("p (a n) -> p a n", n=QK),
                                     rs[:, t, :].unsqueeze(2).to_broadcast([P, 4, QK]), ALU.mult)
                        ins.then_inc(nr, 1)

                    def lower_parts(t):
                        low = slice(QK, P)
                        dve.wait_ge(qhr, h * T + t + 1)
                        q_hi = qs2[low, :, t * P:(t + 1) * P]
                        V.scalar_tensor_tensor(out=q_hi, in0=g.ps[low, 7, 0:2 * P].rearrange("p (c n) -> p c n", c=2), scalar=qs[low, 0:1],
                                               in1=q_hi.bitcast(F32), op0=ALU.mult, op1=ALU.subtract).then_inc(tq, 1)
                        dve.wait_ge(khr, h * T + t + 1)
                        V.scalar_tensor_tensor(out=kl[:, :, t * P:(t + 1) * P], in0=g.ps[:, 6, 0:2 * P].rearrange("p (c n) -> p c n", c=2),
                                               scalar=g.vecs[:, ROW_KN:ROW_KN + 1], in1=kh[:, :, t * P:(t + 1) * P].bitcast(F32),
                                               op0=ALU.mult, op1=ALU.subtract).then_inc(tk, 1)

                    for t in range(T):
                        dve.wait_ge(sqr, h * T + t + 1)
                        V.tensor_reduce(out=ss[:, t, :], in_=sq[:].rearrange("p (a n) -> p a n", n=QK), axis=AX, op=ALU.add).then_inc(ssr, 1)
                        normed(t)
                        lower_parts(t)

                    def neg_scores(u):
                        for c in range(2):
                            if u >= 2:
                                dve.wait_ge(wr, h * T + u - 1)
                            dve.wait_ge(sr, h * 2 * T + 2 * u + c + 1)
                            dve.sem_inc(seen, 1)
                            V.tensor_tensor_reduce(out=pr[:, u % 2, c, :], in0=g.ps[:, 2 * c:2 * c + 2, :].rearrange("p a n -> p (a n)"),
                                                   in1=dist[:, 896 - u * P:896 - u * P + SEQ], scale=nsl[:, 0:1], scalar=3.0e38,
                                                   op0=ALU.add, op1=ALU.min, accum_out=mx[:, u % 2, c:c + 1]).then_inc(ng, 1)

                    neg_scores(0)
                    for u in range(T):
                        if u + 1 < T:
                            neg_scores(u + 1)
                        dve.wait_ge(er, h * 2 * T + 2 * u + 2)
                        base = h * 3 * T + 3 * u
                        V.reciprocal(cf[:], den[:, u, :]).then_inc(vs, 1)
                        dve.wait_ge(vs, base + 1)
                        V.tensor_copy(rd[:, u:u + 1], cf[:, 0:1]).then_inc(vs, 1)
                        V.scalar_tensor_tensor(out=cf[:, 1:2], in0=den[:, u, 0:1], scalar=g.neglam[:, 0:1], in1=cf[:, 1:2],
                                               op0=ALU.mult, op1=ALU.mult).then_inc(vs, 1)
                        dve.wait_ge(vs, base + 3)
                        if u >= 2:
                            dve.wait_ge(wtr, h * T + u - 1)
                        V.scalar_tensor_tensor(out=wt[:, u % 2, :], in0=pr[:, u % 2, 1, :], scalar=cf[:, 1:2], in1=pr[:, u % 2, 0, :],
                                               op0=ALU.mult, op1=ALU.add).then_inc(wr, 1)
                        dve.wait_ge(wr, h * T + u + 1)
                    dve.wait_ge(ofs, 2 * h + 2)
                    tt(V, mixed[:, :, bass.ds(h * VD, VD)], o[:], ors[:].unsqueeze(2).to_broadcast([P, T, VD]), ALU.mult).then_inc(fin, 1)

                head(0)
                with dve.Fori(1, HEADS - 1) as h:
                    head(h)
                head(HEADS - 1, last_head=True)


def project_out(nc, g, mixed, srcT):
    io = g.io
    with ExitStack() as ctx:
        w = ctx.enter_context(nc.sbuf_tensor("w_out_raw", [P, 2, D], F32))
        w_hi, w_lo, low = (ctx.enter_context(nc.sbuf_tensor(n, [P, KT, D], F32R)) for n in ("w_out_hi", "w_out_lo", "mixedT_lo"))
        wl, xl = [g.sem(f"w_out_loaded{j}") for j in range(KT)], g.sem("x_loaded_again")
        tr, mh, ml = g.sem("mixed_transposed"), g.sem("mixedT_hi_ready"), g.sem("mixedT_lo_ready")
        whr, wlr = g.sem("w_out_hi_ready"), g.sem("w_out_lo_ready")
        pr, xa = g.sem("out0_ready"), g.sem("out0_added")
        wv = io["w_out"][0].rearrange("(j p) n -> p j n", p=P)
        gains = [(slice(0, 4), ROW_SUBLN)] + [(slice(4 + j, 5 + j), ROW_SSDN + j) for j in range(4)]
        by_feature = lambda t: g.ps[:, 2 * (t % 2):2 * (t % 2) + 2, :].rearrange("p a (j n) -> p (a j) n", n=P)
        with nc.Block() as block:
            @block.sync
            def _(sp):
                for j in range(KT):
                    wait(sp, wlr, j - 1)
                    sp.dma_start(w[:, j % 2, :], wv[:, j, :]).then_inc(wl[j], 16)
                for t in range(T):
                    sp.dma_start(g.x[:, t, :], io["x"][t * P:(t + 1) * P, :]).then_inc(xl, 16)

            @block.tensor
            def _(pe):
                def transposes(t):
                    wait(pe, mh, t - 1)
                    wait(pe, ml, t - 1)
                    for j in range(KT):
                        last = nc.tensor.transpose(g.ps[:, 2 * (t % 2) + j // 4, (j % 4) * P:(j % 4 + 1) * P], mixed[:, t, j * P:(j + 1) * P], g.ident[:])
                    last.then_inc(tr, 1)

                for t in range(4):
                    transposes(t)
                for t in range(T):
                    if t < 4:
                        transposes(4 + t)
                    pe.wait_ge(ml, t + 1 if t < 4 else T)
                    pe.wait_ge(wlr, KT)
                    wait(pe, xa, t - 1)
                    for half in range(2):
                        n = slice(half * HALF, (half + 1) * HALF)
                        for j in range(KT):
                            for m, (a, b) in enumerate(((srcT, w_hi), (srcT, w_lo), (low, w_hi))):
                                last = nc.tensor.matmul(g.ps[:, 4 + 2 * (t % 2) + half, :], a[:, j, t * P:(t + 1) * P], b[:, j, n],
                                                        start=j == 0 and m == 0, stop=j == KT - 1 and m == 2)
                    last.then_inc(pr, 1)

            @block.scalar
            def _(act):
                for t in range(T):
                    act.wait_ge(tr, t + 1)
                    for j, row in gains:
                        for dst, cut in order_mirrored(t):
                            last = nc.scalar.activation(srcT[:, j, dst], by_feature(t)[:, j, cut], ACT.Copy, scale=g.vecs[:, row:row + 1])
                    last.then_inc(mh, 1)
                    if t < 4:
                        for j in (2 * t, 2 * t + 1):
                            act.wait_ge(wl[j], 16)
                            nc.scalar.activation(w_hi[:, j, :], w[:, j % 2, :], ACT.Copy).then_inc(whr, 1)

            @block.vector
            def _(dve):
                def add(t):
                    dve.wait_ge(xl, 16 * T)
                    dve.wait_ge(pr, t + 1)
                    tt(nc.vector, g.x[:, t, :], g.x[:, t, :], g.ps[:, 4 + 2 * (t % 2):6 + 2 * (t % 2), :].rearrange("p a n -> p (a n)"), ALU.add).then_inc(xa, 1)

                for t in range(T):
                    dve.wait_ge(mh, t + 1)
                    for j, row in gains:
                        for dst, cut in order_mirrored(t):
                            last = nc.vector.scalar_tensor_tensor(out=low[:, j, dst], in0=by_feature(t)[:, j, cut], scalar=g.vecs[:, row:row + 1],
                                                                  in1=srcT[:, j, dst].bitcast(F32), op0=ALU.mult, op1=ALU.subtract)
                    last.then_inc(ml, 1)
                    if t < 4:
                        for j in (2 * t, 2 * t + 1):
                            dve.wait_ge(whr, j + 1)
                            tt(nc.vector, w_lo[:, j, :], w[:, j % 2, :], w_hi[:, j, :].bitcast(F32), ALU.subtract).then_inc(wlr, 1)
                    if t >= 5:
                        add(t - 5)
                for t in range(T - 5, T):
                    add(t)


def route(nc, g, layer):
    io = g.io
    NL = LOGITS
    with ExitStack() as ctx:
        sb = lambda n, s, d=F32: ctx.enter_context(nc.sbuf_tensor(f"{n}_r{layer}", s, d))
        rb = sb("router_b", [P, NL])
        gl, el = sb("group_logits", [P, T, 8]), sb("expert_logits", [P, T, EXPERTS])
        gm, em = sb("group_max", [P, T, 8]), sb("expert_max", [P, T, 8])
        gi, ei = sb("group_idx", [P, T, 8], U32), sb("expert_idx", [P, T, 8], U32)
        gf, ef = sb("group_idx_f", [P, T]), sb("expert_idx_f", [P, T, 2])
        m12 = sb("choice", [P, 2, T, EXPERTS])
        both, pre = sb("chosen", [P, T, EXPERTS]), sb("chosen_before", [P, T, EXPERTS])
        ge, gs, gp = sb("group_exp", [P, T, 4]), sb("group_sum", [P, T]), sb("group_p", [P, T])
        de, dn = sb("expert_exp", [P, T]), sb("expert_den", [P, T])
        cnt, cge = sb("counts", [P, EXPERTS]), sb("count_steps", [P, EXPERTS, 8])
        nb, inc, inc2 = sb("n_blocks", [P, EXPERTS]), sb("blocks_end", [P, EXPERTS]), sb("blocks_end2", [P, EXPERTS])
        rk, rt = sb("slot_of", [P, T, EXPERTS]), sb("slot_tmp", [P, T, EXPERTS])
        df, si, sf = sb("slot_f", [P, 2, T]), sb("slot_parts", [P, 2, 2 * T], I32), sb("slot_parts_f", [P, 2, 2 * T])
        hq, hb = sb("onehot_place", [P, 2 * T, P], F32R), sb("onehot_block", [P, 2 * T, SLOT_BLOCKS], F32R)
        hbf = sb("onehot_block_f", [P, 2 * T, SLOT_BLOCKS])
        pad, tab = sb("slot_empty", [P, SLOT_BLOCKS]), sb("slot_choice", [P, SLOT_BLOCKS])
        EXTRA = MAX_BLOCKS - EXPERTS
        bt, bf = sb("block_cmp", [1, EXTRA, EXPERTS]), sb("block_expert_f", [1, EXTRA])
        npf = sb("n_pairs_f", [1, 2])
        pair_cmp = sb("pair_cmp", [1, EXTRA // 2])
        rl = g.sem(f"router_bias_loaded_{layer}")
        vs, gd, ge_r = g.sem(f"dve_route_step_{layer}"), g.sem(f"softmax_in_{layer}"), g.sem(f"softmax_exp_{layer}")
        ch, rr = g.sem(f"chosen_ready_{layer}"), g.sem(f"ranks_ready_{layer}")
        ohr, tbr = g.sem(f"onehots_ready_{layer}"), g.sem(f"slot_choices_ready_{layer}")
        cuts = [0, 32, 64, 72, 72 + SLOT_BLOCKS, 72 + SLOT_BLOCKS + P, 72 + SLOT_BLOCKS + P + EXPERTS]
        iota_e, grp_e, j128, iota_b, iota_p, first_slot = (g.small[:, a:b] for a, b in zip(cuts, cuts[1:]))
        with nc.Block() as block:
            @block.sync
            def _(sp):
                sp.dma_start(rb[:, 0:GROUPS], io["router_group_b"][layer].partition_broadcast(P)).then_inc(rl, 16)
                sp.dma_start(rb[:, GROUPS:], io["router_expert_b"][layer].rearrange("g e -> (g e)").partition_broadcast(P)).then_inc(rl, 16)
                sp.wait_ge(g.h_stored[layer], 16 * T)

            @block.tensor
            def _(pe):
                pe.wait_ge(ch, 1)
                ranks = g.ps[:, 1, 0:T * EXPERTS]
                nc.tensor.matmul(ranks, g.masks[:, M_LT * P:(M_LT + 1) * P], both[:].rearrange("p t e -> p (t e)"), start=True, stop=False)
                nc.tensor.matmul(ranks, g.masks[:, M_ONE * P:(M_ONE + 1) * P], pre[:].rearrange("p t e -> p (t e)"), start=False, stop=True)
                nc.tensor.matmul(g.ps[:, 2, 0:EXPERTS], g.masks[:, M_ONE * P:(M_ONE + 1) * P], cnt[:], start=True, stop=True).then_inc(rr, 1)
                for m in range(2 * T):
                    if m % 4 == 0:
                        pe.wait_ge(ohr, m // 4 + 1)
                    last = nc.tensor.matmul(g.ps[:, 3, 0:SLOT_BLOCKS], hq[:, m, :], hb[:, m, :], start=m == 0, stop=m == 2 * T - 1)
                last.then_inc(tbr, 1)

            @block.scalar
            def _(act):
                act.wait_ge(gd, 1)
                nc.scalar.activation(ge[:], ge[:], ACT.Exp).then_inc(ge_r, 1)
                act.wait_ge(gd, 2)
                nc.scalar.activation(de[:], de[:], ACT.Exp).then_inc(ge_r, 1)

            @block.vector
            def _(dve):
                V = nc.vector
                step = Chain(dve, vs)
                bE = lambda v: v.unsqueeze(2).to_broadcast([P, T, EXPERTS])
                cE = lambda v: v.unsqueeze(1).to_broadcast([P, T, EXPERTS])
                step(V.memset(gl[:], -BIG))
                dve.wait_ge(rl, 32)
                lg = g.ps[:, 6, 0:T * NL].rearrange("p (t n) -> p t n", n=NL)
                tt(V, gl[:, :, 0:GROUPS], lg[:, :, 0:GROUPS], rb[:, 0:GROUPS].unsqueeze(1).to_broadcast([P, T, GROUPS]), ALU.add)
                step(tt(V, el[:], lg[:, :, GROUPS:], cE(rb[:, GROUPS:]), ALU.add))
                for t in range(T):
                    ins = V.max(gm[:, t, :], gl[:, t, :])
                step(ins)
                for t in range(T):
                    ins = V.max_index(gi[:, t, :], gm[:, t, :], gl[:, t, :])
                step(ins)
                tt(V, ge[:], gl[:, :, 0:GROUPS], gm[:, :, 0:1].to_broadcast([P, T, GROUPS]), ALU.subtract).then_inc(gd, 1)
                step(V.tensor_copy(gf[:], gi[:, :, 0]))
                step(tt(V, rt[:], cE(grp_e), bE(gf[:]), ALU.is_equal))
                step(V.tensor_scalar(rk[:], rt[:], BIG, -BIG, ALU.mult, ALU.add))
                step(tt(V, el[:], el[:], rk[:], ALU.add))
                for t in range(T):
                    ins = V.max(em[:, t, :], el[:, t, :])
                step(ins)
                for t in range(T):
                    ins = V.max_index(ei[:, t, :], em[:, t, :], el[:, t, :])
                step(ins)
                tt(V, de[:], em[:, :, 1], em[:, :, 0], ALU.subtract).then_inc(gd, 1)
                step(V.tensor_copy(ef[:], ei[:, :, 0:2]))
                for k in range(2):
                    ins = tt(V, m12[:, k], cE(iota_e), bE(ef[:, :, k]), ALU.is_equal)
                step(ins)
                V.memset(pre[:, 0, :], 0.0)
                step(tt(V, both[:], m12[:, 0], m12[:, 1], ALU.add))
                for t in range(1, T):
                    step(tt(V, pre[:, t, :], pre[:, t - 1, :], both[:, t - 1, :], ALU.add))
                tt(V, cnt[:], pre[:, T - 1, :], both[:, T - 1, :], ALU.add).then_inc(ch, 1)
                dve.wait_ge(ge_r, 2)
                step(V.tensor_reduce(out=gs[:], in_=ge[:], axis=AX, op=ALU.add))
                step(V.tensor_scalar(dn[:], de[:], 1.0, None, ALU.add))
                step(tt(V, dn[:], dn[:], gs[:], ALU.mult))
                step(V.reciprocal(g.gates[:, 0, :], dn[:]))
                step(tt(V, g.gates[:, 1, :], g.gates[:, 0, :], de[:], ALU.mult))
                dve.wait_ge(rr, 1)
                step(V.tensor_copy(cnt[:], g.ps[:, 2, 0:EXPERTS]))
                step(tt(V, cge[:], cnt[:].unsqueeze(2).to_broadcast([P, EXPERTS, 8]), j128.unsqueeze(1).to_broadcast([P, EXPERTS, 8]), ALU.is_gt))
                step(V.tensor_reduce(out=nb[:], in_=cge[:], axis=AX, op=ALU.add))
                src, dst = nb, inc
                for s in (1, 2, 4, 8, 16):
                    V.tensor_copy(dst[:, 0:s], src[:, 0:s])
                    step(tt(V, dst[:, s:], src[:, s:], src[:, 0:EXPERTS - s], ALU.add))
                    src, dst = dst, (inc2 if dst is inc else inc)
                end, jump = src, dst
                step(tt(V, jump[:], end[:], nb[:], ALU.subtract))
                step(V.tensor_scalar(jump[:], jump[:], float(P), float(P * (EXPERTS - 1)), ALU.mult, ALU.add))
                step(tt(V, jump[:], jump[:], first_slot, ALU.subtract))
                ranks = g.ps[:, 1, 0:T * EXPERTS].rearrange("p (t n) -> p t n", n=EXPERTS)
                tt(V, rk[:], ranks, cE(first_slot), ALU.add)
                step(V.tensor_scalar(rt[:], ranks, float(P), None, ALU.is_ge))
                step(tt(V, rt[:], rt[:], cE(jump[:]), ALU.mult))
                step(tt(V, rk[:], rk[:], rt[:], ALU.add))
                for k in range(2):
                    ins = tt(V, m12[:, k], rk[:], m12[:, k], ALU.mult)
                step(ins)
                step(V.tensor_reduce(out=df[:], in_=m12[:], axis=AX, op=ALU.add))
                M = 2 * T
                step(V.tensor_copy(si[:, 0, :], df[:].rearrange("p k t -> p (k t)")))
                step(V.tensor_scalar(si[:, 1, :], si[:, 0, :], P - 1, None, ALU.bitwise_and))
                step(V.tensor_scalar(si[:, 0, :], si[:, 0, :], P.bit_length() - 1, None, ALU.arith_shift_right))
                step(V.tensor_copy(sf[:], si[:]))
                step(tt(V, hbf[:], iota_b.unsqueeze(1).to_broadcast([P, M, SLOT_BLOCKS]), sf[:, 0, :].unsqueeze(2).to_broadcast([P, M, SLOT_BLOCKS]), ALU.is_equal))
                step(tt(V, hb[:], hbf[:], g.ids[:].unsqueeze(2).to_broadcast([P, M, SLOT_BLOCKS]), ALU.mult))
                for m in range(0, M, 4):
                    tt(V, hq[:, m:m + 4, :], iota_p.unsqueeze(1).to_broadcast([P, 4, P]), sf[:, 1, m:m + 4].unsqueeze(2).to_broadcast([P, 4, P]), ALU.is_equal).then_inc(ohr, 1)
                step(tt(V, bt[:], end[0:1, :].unsqueeze(1).to_broadcast([1, EXTRA, EXPERTS]),
                        iota_b[0:1, 0:EXTRA].unsqueeze(2).to_broadcast([1, EXTRA, EXPERTS]), ALU.is_le))
                step(V.tensor_reduce(out=bf[:], in_=bt[:], axis=AX, op=ALU.add))
                step(V.tensor_scalar(bf[:], bf[:], float(EXPERTS - 1), None, ALU.min))
                step(V.tensor_copy(g.block_expert[:, EXPERTS:MAX_BLOCKS], bf[:]))
                step(V.tensor_copy(g.block_expert[:, 0:EXPERTS], iota_e[0:1, :]))
                step(tt(V, pair_cmp[:], end[0:1, EXPERTS - 1:EXPERTS].to_broadcast([1, EXTRA // 2]), iota_b[0:1, 0:EXTRA:2], ALU.is_gt))
                step(V.tensor_reduce(out=npf[:, 0:1], in_=pair_cmp[:], axis=AX, op=ALU.add))
                step(V.tensor_scalar(g.last_pair[:], npf[:, 0:1], float(EXPERTS // 2 - 1), None, ALU.add))
                dve.wait_ge(tbr, 1)
                step(V.tensor_scalar(pad[:], g.ps[:, 3, 0:SLOT_BLOCKS], 0.0, float(EMPTY), ALU.is_equal, ALU.mult))
                step(V.scalar_tensor_tensor(out=tab[:], in0=g.ps[:, 3, 0:SLOT_BLOCKS], scalar=-1.0, in1=pad[:], op0=ALU.add, op1=ALU.add))
                step(V.tensor_copy(g.slot_y[:], tab[:]))
                step(V.tensor_scalar(g.slot_x[:], g.slot_y[:], 1, None, ALU.arith_shift_right))


def expert_weights(nc, g, layer):
    e = Shared()
    io = g.io
    e.w13 = [io[f"expert_w{n}"][layer].rearrange("e (p j) n -> e p j n", j=KT) for n in (1, 3)]
    e.w2 = io["expert_w2"][layer].rearrange("e (p j) n -> e p (j n)", j=2)
    e.w13l = [[g.sem(f"w{n}_loaded{s}_{layer}") for n in (1, 3)] for s in range(2)]
    e.w2l = [g.sem(f"w2_loaded{s}_{layer}") for s in range(2)]
    return e


def load_w13(sp, e, n, expert, s):
    sp.dma_start(e.raw[:, s, n, :, :], e.w13[n][bass.ds(expert, 1), :, :, :].rearrange("e p j n -> (e p) j n")).then_inc(e.w13l[s][n], 16)


def load_w2(sp, e, expert, s):
    sp.dma_start(e.w2s[:, s, :, :].rearrange("p j n -> p (j n)"), e.w2[bass.ds(expert, 1), :, :].rearrange("e p n -> (e p) n")).then_inc(e.w2l[s], 16)


def experts(nc, g, layer, e):
    with ExitStack() as ctx:
        sb = lambda n, s, d=F32: ctx.enter_context(nc.sbuf_tensor(f"{n}_e{layer}", s, d))
        raw, w2s, w13l, w2l = e.raw, e.w2s, e.w13l, e.w2l
        wh, wl = sb("w13_hi", [P, 2, 2, KT, HID], F32R), sb("w13_lo", [P, 2, 2, KT, HID], F32R)
        xb = sb("x_block", [P, 2, D])
        xh, xlo = sb("xT_hi", [P, 2, KT, P], F32R), sb("xT_lo", [P, 2, KT, P], F32R)
        sg, hid, hT = sb("silu", [P, 2, HID]), sb("hidden", [P, 2, HID]), sb("hiddenT", [P, 2, P])
        yb = sb("y_block", [P, 2, D])
        ix, iy = sb("gather_rows", [P, 2], I32), sb("scatter_rows", [P, 2], I32)
        xl = [g.sem(f"x_block_loaded{s}_{layer}") for s in range(2)]
        yst = [g.sem(f"y_stored{s}_{layer}") for s in range(2)]
        xt, xhr, xlr = g.sem(f"x_transposed_{layer}"), g.sem(f"xT_hi_ready_{layer}"), g.sem(f"xT_lo_ready_{layer}")
        whr, wlr = g.sem(f"w13_hi_ready_{layer}"), g.sem(f"w13_lo_ready_{layer}")
        gu, sil, hr = g.sem(f"gate_up_ready_{layer}"), g.sem(f"silu_done_{layer}"), g.sem(f"hidden_ready_{layer}")
        ht, he, yr = g.sem(f"hidden_transposed_{layer}"), g.sem(f"hiddenT_ready_{layer}"), g.sem(f"y_ready_{layer}")
        yea, yed = g.sem(f"y_low_read_{layer}"), g.sem(f"y_high_read_{layer}")
        ixr, iyr, x0 = g.sem(f"gather_rows_ready_{layer}"), g.sem(f"scatter_rows_ready_{layer}"), g.sem(f"x_block_cleared_{layer}")
        seen = g.sem(f"pool_wait_passed_{layer}")
        FIRST, PAIRS = EXPERTS // 2, MAX_BLOCKS // 2

        def pairs(eng, step, finish=None):
            for i in range(2):
                step(i, 0, None)
                step(i, 1, None)
            with eng.Fori(2, FIRST - 1) as i:
                step(i, 0, None)
                step(i, 1, None)
            m = eng.value_load(g.last_pair[0:1, 0:1], min_val=FIRST - 1, max_val=PAIRS - 1)
            with eng.Fori(FIRST - 1, PAIRS) as i:
                with eng.If(i <= m):
                    step(i, 0, m)
                    step(i, 1, m)
                with eng.Else():
                    eng.nop()
            if finish:
                finish(m)

        def for_next(eng, i, m, f):
            if m is None:
                f()
                return
            with eng.If(i < m):
                f()
            with eng.Else():
                eng.nop()

        with nc.Block() as block:
            @block.sync
            def _(sp):
                def expert_of(k, m):
                    if m is None:
                        return k
                    return sp.value_load(g.block_expert[0:1, bass.ds(k, 1)], min_val=0, max_val=EXPERTS - 1)

                def w13(k, s, m):
                    x = expert_of(k, m)
                    for n in range(2):
                        wait(sp, wlr, 2 * (k - 2) + n + 1)
                        load_w13(sp, e, n, x, s)

                def down_w(k, s, m):
                    x = expert_of(k, m)
                    wait(sp, yr, k - 1)
                    load_w2(sp, e, x, s)

                def step(i, s, m):
                    k = 2 * i + s
                    if s == 0:
                        for_next(sp, i, m, lambda: w13(k + 2, s, m))
                        down_w(k + 1, 1 - s, m)
                    else:
                        for_next(sp, i, m, lambda: (w13(k + 2, s, m), down_w(k + 1, 1 - s, m)))

                pairs(sp, step)

            @block.gpsimd
            def _(pool):
                def gather_x(k, s, turn):
                    wait(pool, xl[s], 16 * turn)
                    pool.sem_inc(seen, 1)
                    nc.gpsimd.tensor_copy(ix[:, s:s + 1], g.slot_x[:, bass.ds(k, 1)]).then_inc(ixr, 1)
                    wait(pool, xt, k - 1)
                    pool.wait_ge(ixr, k + 1)
                    pool.sem_inc(seen, 1)
                    pool.indirect_dma_start(out=xb[:, s, :], out_offset=None, in_=g.h_rows[:, :],
                                            in_offset=bass.IndirectOffsetOnAxis(ap=ix[:, s:s + 1], axis=0),
                                            bounds_check=SEQ - 1, oob_is_err=False).then_inc(xl[s], 16)

                def scatter_y(k, s, turn):
                    wait(pool, yst[s], 16 * turn)
                    pool.sem_inc(seen, 1)
                    nc.gpsimd.tensor_copy(iy[:, s:s + 1], g.slot_y[:, bass.ds(k, 1)]).then_inc(iyr, 1)
                    pool.wait_ge(yea, k + 1)
                    pool.wait_ge(yed, k + 1)
                    pool.wait_ge(iyr, k + 1)
                    pool.sem_inc(seen, 1)
                    pool.indirect_dma_start(out=g.y_rows[:, :], out_offset=bass.IndirectOffsetOnAxis(ap=iy[:, s:s + 1], axis=0),
                                            in_=yb[:, s, :], in_offset=None,
                                            bounds_check=2 * SEQ - 1, oob_is_err=False).then_inc(yst[s], 16)

                nc.gpsimd.memset(xb[:], 0.0).then_inc(x0, 1)
                pool.wait_ge(x0, 1)
                pool.wait_ge(g.h_stored[layer], 16 * T)
                gather_x(0, 0, 0)
                gather_x(1, 1, 0)
                gather_x(2, 0, 1)

                def step(i, s, m):
                    k = 2 * i + s
                    gather_x(k + 3, 1 - s, i + 1 + s)
                    if not (isinstance(k, int) and k == 0):
                        scatter_y(k - 1, 1 - s, i - 1 + s)

                def finish(m):
                    scatter_y(2 * m + 1, 1, m)
                    for s in range(2):
                        pool.wait_ge(yst[s], 16 * (m + 1))
                        pool.sem_inc(seen, 1)
                        pool.wait_ge(xl[s], 16 * (m + 3 - s))
                        pool.sem_inc(seen, 1)

                pairs(pool, step, finish)

            @block.tensor
            def _(pe):
                def transpose_x(k, s, turn):
                    pe.wait_ge(xl[s], 16 * (turn + 1))
                    wait(pe, xhr, 2 * k)
                    wait(pe, xlr, 2 * k)
                    xv = xb[:, s, :].rearrange("p (q j) -> p j q", j=KT)
                    for j in range(KT):
                        last = nc.tensor.transpose(g.ps[:, 2 + j // 4, (j % 4) * P:(j % 4 + 1) * P], xv[:, j, :], g.ident[:])
                    last.then_inc(xt, 1)

                def transpose_hidden(k, s):
                    pe.wait_ge(hr, k + 1)
                    wait(pe, he, k)
                    hv = hid[:, s, :].rearrange("p (q j) -> p j q", j=2)
                    for j in range(2):
                        last = nc.tensor.transpose(g.ps[:, 4, j * P:(j + 1) * P], hv[:, j, :], g.ident[:])
                    last.then_inc(ht, 1)

                def down(k, s, turn):
                    pe.wait_ge(he, k + 1)
                    pe.wait_ge(w2l[s], 16 * (turn + 1))
                    wait(pe, yea, k)
                    wait(pe, yed, k)
                    for half in range(2):
                        for j in range(2):
                            last = nc.tensor.matmul(g.ps[:, 5 + half, :], hT[:, j, :], w2s[:, s, j, half * HALF:(half + 1) * HALF], start=j == 0, stop=j == 1)
                    last.then_inc(yr, 1)

                pe.wait_ge(x0, 1)
                transpose_x(0, 0, 0)

                def step(i, s, m):
                    k = 2 * i + s
                    first = isinstance(k, int) and k == 0
                    if not first:
                        transpose_hidden(k - 1, 1 - s)
                    transpose_x(k + 1, 1 - s, i + s)
                    pe.wait_ge(whr, 2 * k + 2)
                    pe.wait_ge(wlr, 2 * k + 2)
                    pe.wait_ge(xhr, 2 * k + 2)
                    pe.wait_ge(xlr, 2 * k + 2)
                    wait(pe, hr, k - 1)
                    for j in range(KT):
                        for n, (a, b) in enumerate(((xh, wh), (xh, wl), (xlo, wh))):
                            last = nc.tensor.matmul(g.ps[:, s, :], a[:, s, j, :], b[:, s, :, j, :], start=j == 0 and n == 0, stop=j == KT - 1 and n == 2)
                    last.then_inc(gu, 1)
                    if not first:
                        down(k - 1, 1 - s, i - 1 + s)

                def finish(m):
                    transpose_hidden(2 * m + 1, 1)
                    down(2 * m + 1, 1, m)

                pairs(pe, step, finish)

            @block.scalar
            def _(act):
                def split_w(k, s, turn):
                    wait(act, gu, k - 1)
                    for n in range(2):
                        act.wait_ge(w13l[s][n], 16 * (turn + 1))
                        nc.scalar.activation(wh[:, s, n, :, :], raw[:, s, n, :, :], ACT.Copy).then_inc(whr, 1)

                def split_x(k, s):
                    act.wait_ge(xt, k + 1)
                    wait(act, gu, k - 1)
                    for b in range(2):
                        nc.scalar.activation(xh[:, s, 4 * b:4 * b + 4, :].rearrange("p j n -> p (j n)"), g.ps[:, 2 + b, :], ACT.Copy).then_inc(xhr, 1)

                def copy_y(k, s, stored):
                    act.wait_ge(yr, k + 1)
                    wait(act, yst[s], stored)
                    nc.scalar.activation(yb[:, s, 0:HALF], g.ps[:, 5, :], ACT.Copy).then_inc(yea, 1)

                split_w(0, 0, 0)
                split_x(0, 0)

                def step(i, s, m):
                    k = 2 * i + s
                    split_x(k + 1, 1 - s)
                    if s == 0:
                        split_w(k + 1, 1 - s, i + s)
                    else:
                        for_next(act, i, m, lambda: split_w(k + 1, 1 - s, i + s))
                    act.wait_ge(gu, k + 1)
                    wait(act, hr, k - 1)
                    nc.scalar.activation(sg[:, s, :], g.ps[:, s, 0:HID], ACT.Silu).then_inc(sil, 1)
                    if not (isinstance(k, int) and k == 0):
                        copy_y(k - 1, 1 - s, 16 * (i - 1 + s))

                pairs(act, step, lambda m: copy_y(2 * m + 1, 1, 16 * m))

            @block.vector
            def _(dve):
                def split_w(k, s):
                    for n in range(2):
                        dve.wait_ge(whr, 2 * k + n + 1)
                        tt(nc.vector, wl[:, s, n, :, :], raw[:, s, n, :, :], wh[:, s, n, :, :].bitcast(F32), ALU.subtract).then_inc(wlr, 1)

                def split_x(k, s):
                    for b in range(2):
                        dve.wait_ge(xhr, 2 * k + b + 1)
                        tt(nc.vector, xlo[:, s, 4 * b:4 * b + 4, :].rearrange("p j n -> p (j n)"), g.ps[:, 2 + b, :],
                           xh[:, s, 4 * b:4 * b + 4, :].rearrange("p j n -> p (j n)").bitcast(F32), ALU.subtract).then_inc(xlr, 1)

                def copy_hidden(k):
                    dve.wait_ge(ht, k + 1)
                    wait(dve, yr, k)
                    nc.vector.tensor_copy(hT[:].rearrange("p j n -> p (j n)"), g.ps[:, 4, 0:2 * P]).then_inc(he, 1)

                def copy_y(k, s, stored):
                    dve.wait_ge(yr, k + 1)
                    wait(dve, yst[s], stored)
                    nc.vector.tensor_copy(yb[:, s, HALF:], g.ps[:, 6, :]).then_inc(yed, 1)

                split_w(0, 0)
                split_x(0, 0)

                def step(i, s, m):
                    k = 2 * i + s
                    first = isinstance(k, int) and k == 0
                    if not first:
                        copy_hidden(k - 1)
                    split_x(k + 1, 1 - s)
                    if s == 0:
                        split_w(k + 1, 1 - s)
                    else:
                        for_next(dve, i, m, lambda: split_w(k + 1, 1 - s))
                    dve.wait_ge(sil, k + 1)
                    wait(dve, ht, k - 1)
                    tt(nc.vector, hid[:, s, :], sg[:, s, :], g.ps[:, s, HID:], ALU.mult).then_inc(hr, 1)
                    if not first:
                        copy_y(k - 1, 1 - s, 16 * (i - 1 + s))

                def finish(m):
                    copy_hidden(2 * m + 1)
                    copy_y(2 * m + 1, 1, 16 * m)

                pairs(dve, step, finish)


def combine(nc, g, layer, last_layer):
    BUF = 4
    with ExitStack() as ctx:
        yg = ctx.enter_context(nc.sbuf_tensor(f"y_by_token_{layer}", [P, BUF, 2, D], F32))
        gt = [g.sem(f"y_by_token_loaded{s}_{layer}") for s in range(BUF)]
        vs, ad, out = g.sem(f"dve_combine_step_{layer}"), g.sem(f"combined_{layer}"), g.sem(f"out_stored_{layer}")
        yv = g.y_rows.rearrange("(t p k) n -> t p k n", p=P, k=2)
        with nc.Block() as block:
            @block.scalar
            def _(act):
                for t in range(T):
                    wait(act, ad, t - BUF + 1)
                    act.dma_start(yg[:, t % BUF, :, :], yv[t]).then_inc(gt[t % BUF], 16)

            @block.vector
            def _(dve):
                step = Chain(dve, vs)
                for t in range(T):
                    dve.wait_ge(gt[t % BUF], 16 * (t // BUF + 1))
                    for k in range(2):
                        ins = nc.vector.scalar_tensor_tensor(out=g.x[:, t, :], in0=yg[:, t % BUF, k, :], scalar=g.gates[:, k, t:t + 1], in1=g.x[:, t, :],
                                                             op0=ALU.mult, op1=ALU.add)
                        if k == 0:
                            step(ins)
                    ins.then_inc(ad, 1)

            @block.sync
            def _(sp):
                if last_layer:
                    for t in range(T):
                        sp.wait_ge(ad, t + 1)
                        sp.dma_start(g.io["out"][t * P:(t + 1) * P, :], g.x[:, t, :]).then_inc(out, 16)
                    sp.wait_ge(out, 16 * T)


def fourier(nc, g, hT):
    io = g.io
    NG = GROUPS_F
    with ExitStack() as ctx:
        sb = lambda n, s: ctx.enter_context(nc.sbuf_tensor(n, s, F32))
        diff = sb("h_minus_mirror", [P, KT, HALF])
        dch = sb("dft_channels", [P, 2, 2 * P])
        ct, st, alt = sb("cos_tokens", [P, 4, HALF + 1]), sb("sin_tokens", [P, 4, HALF]), sb("alternating", [1, HALF + 1])
        ab = sb("channel_dft", [P, 4, NG, 2 * P])
        a5 = sb("channel_dft_512", [1, NG, P + 1])
        pt, qt, pz = sb("cos_part", [P, NG, HALF]), sb("sin_part", [P, NG, HALF]), sb("cos_part_mirror0", [P, NG, P])
        pn, pnz = sb("cos_part_128", [NG, HALF]), sb("cos_part_128_mirror0", [NG, P])
        wd, wm, wp, wn = sb("w_direct", [P, NG, D]), sb("w_mirror", [P, NG, D]), sb("w_plus", [P, NG, D]), sb("w_128", [NG, D])
        cl, tl, wl = g.sem("dft_channels_loaded"), g.sem("dft_tokens_loaded"), g.sem("w_fourier_loaded")
        fd, fo = g.sem("difference_ready"), g.sem("folded")
        p1, r1, a5p, a5r = g.sem("channel_dft_ready"), g.sem("channel_dft_read"), g.sem("dft_512_ready"), g.sem("dft_512_read")
        p2, pr_, qr, p5, zc = g.sem("token_dft_ready"), g.sem("cos_part_read"), g.sem("sin_part_read"), g.sem("cos_512_ready"), g.sem("mirror0_ready")
        wpr, wmr = g.sem("w_plus_ready"), g.sem("w_minus_ready")
        xr, yr, zr, xs, ya = g.sem("x_part_ready"), g.sem("y_part_ready"), g.sem("z_part_ready"), g.sem("x_part_added"), g.sem("y_part_added")
        cols = lambda t: slice(t * P, (t + 1) * P)
        with nc.Block() as block:
            @block.sync
            def _(sp):
                sp.dma_start(dch[:], io["c_dft_channels"].rearrange("(a p) n -> p a n", p=P)).then_inc(cl, 16)
                sp.dma_start(ct[:], io["c_cos_tokens"].rearrange("(a p) n -> p a n", p=P)).then_inc(tl, 16)
                sp.dma_start(alt[:], io["c_alternating"]).then_inc(tl, 16)
                sp.dma_start(st[:], io["c_sin_tokens"].rearrange("(a p) n -> p a n", p=P)).then_inc(tl, 16)
                sp.dma_start(wd[:], io["w_fourier_direct"].rearrange("g p n -> p g n")).then_inc(wl, 16)
                sp.dma_start(wm[:], io["w_fourier_mirror"].rearrange("g p n -> p g n")).then_inc(wl, 16)
                sp.dma_start(wn[:], io["w_fourier_128"]).then_inc(wl, 16)

            @block.gpsimd
            def _(pool):
                pool.wait_ge(wl, 48)
                for gr in range(NG):
                    tt(nc.gpsimd, wp[:, gr, :], wd[:, gr, :], wm[:, gr, :], ALU.add).then_inc(wpr, 1)
                for gr in range(NG):
                    pool.wait_ge(wpr, gr + 1)
                    tt(nc.gpsimd, wd[:, gr, :], wd[:, gr, :], wm[:, gr, :], ALU.subtract).then_inc(wmr, 1)

            @block.tensor
            def _(pe):
                pe.wait_ge(cl, 16)
                for t in range(4):
                    pe.wait_ge(fo, t + 1)
                    for pair in range(2):
                        u = 2 * t + pair
                        wait(pe, r1, u - 3)
                        for gr in (2 * pair, 2 * pair + 1):
                            o = (gr % 2) * 2 * P
                            for a in range(2):
                                nc.tensor.matmul(g.ps[:, u % 4, o:o + P + 1], hT[:, 2 * gr + a, cols(t)], dch[:, a, 0:P + 1], start=a == 0, stop=a == 1)
                            for a in range(2):
                                last = nc.tensor.matmul(g.ps[:, u % 4, o + P + 1:o + 2 * P], diff[:, 2 * gr + a, cols(t)], dch[:, a, P + 1:], start=a == 0, stop=a == 1)
                        last.then_inc(p1, 1)
                for gr in range(NG):
                    for a in range(2):
                        nc.tensor.matmul(g.ps[0:1, 4, cols(gr)], hT[:, 2 * gr + a, HALF:HALF + 1], dch[:, a, 0:P], start=a == 0, stop=a == 1)
                    for a in range(2):
                        last = nc.tensor.matmul(g.ps[0:1, 5, gr:gr + 1], hT[:, 2 * gr + a, HALF:HALF + 1], dch[:, a, P:P + 1], start=a == 0, stop=a == 1)
                last.then_inc(a5p, 1)
                pe.wait_ge(tl, 48)
                pe.wait_ge(r1, 8)

                def cosines(out, weights, last_row, part):
                    for t in range(4):
                        nc.tensor.matmul(out, weights(t), ct[:, t, part], start=t == 0, stop=False)
                    return nc.tensor.matmul(out, last_row, alt[:, part], start=False, stop=True)

                for v in range(2 * NG):
                    gr = v // 2
                    if v >= 4:
                        pe.wait_ge((pr_, qr)[v % 2], (v - 4) // 2 + 1)
                    if v % 2 == 0:
                        wait(pe, a5r, 2)
                        last = cosines(g.ps[:, v % 4, :], lambda t: ab[:, t, gr, 0:P], a5[:, gr, 0:P], slice(0, HALF))
                    else:
                        for t in range(4):
                            last = nc.tensor.matmul(g.ps[:, v % 4, :], ab[:, t, gr, P:], st[:, t, :], start=t == 0, stop=t == 3)
                    last.then_inc(p2, 1)
                pe.wait_ge(pr_, 3)
                last = cosines(g.ps[0:NG, 0, :], lambda t: ab[:, t, :, P], a5[:, :, P], slice(0, HALF))
                last.then_inc(p2, 1)
                for gr in range(NG):
                    cosines(g.ps[:, 6, gr:gr + 1], lambda t: ab[:, t, gr, 0:P], a5[:, gr, 0:P], slice(HALF, HALF + 1))
                last = cosines(g.ps[0:NG, 6, NG:NG + 1], lambda t: ab[:, t, :, P], a5[:, :, P], slice(HALF, HALF + 1))
                last.then_inc(p5, 1)
                pe.wait_ge(wpr, NG)
                pe.wait_ge(wmr, NG)
                pe.wait_ge(pr_, NG + 1)
                pe.wait_ge(qr, NG)
                pe.wait_ge(zc, 4)

                def x_part(bank, main, special):
                    for half in range(2):
                        n = slice(half * HALF, (half + 1) * HALF)
                        for gr in range(NG):
                            nc.tensor.matmul(g.ps[:, bank + half, :], main[:, gr, :], wp[:, gr, n], start=gr == 0, stop=False)
                        last = nc.tensor.matmul(g.ps[:, bank + half, :], special, wn[:, n], start=False, stop=True)
                    return last

                for t in range(4):
                    bank = 4 * (t % 2)
                    wait(pe, xs, t - 1)
                    x_part(bank, pt[:, :, cols(t)], pn[:, cols(t)]).then_inc(xr, 1)
                    wait(pe, ya, t - 1)
                    for half in range(2):
                        for gr in range(NG):
                            last = nc.tensor.matmul(g.ps[:, bank + 2 + half, :], qt[:, gr, cols(t)], wd[:, gr, half * HALF:(half + 1) * HALF], start=gr == 0, stop=gr == NG - 1)
                    last.then_inc(yr, 1)
                pe.wait_ge(xs, 3)
                x_part(0, pz[:], pnz[:]).then_inc(zr, 1)

            @block.scalar
            def _(act):
                for u in range(8):
                    t, pair = u // 2, u % 2
                    act.wait_ge(p1, u + 1)
                    nc.scalar.activation(ab[:, t, 2 * pair:2 * pair + 2, :].rearrange("p g n -> p (g n)"), g.ps[:, u % 4, :], ACT.Copy).then_inc(r1, 1)
                act.wait_ge(a5p, 1)
                nc.scalar.activation(a5[:, :, 0:P], g.ps[0:1, 4, :].rearrange("p (g n) -> p g n", g=NG), ACT.Copy).then_inc(a5r, 1)
                nc.scalar.activation(a5[:, :, P], g.ps[0:1, 5, 0:NG], ACT.Copy).then_inc(a5r, 1)
                for gr in range(NG):
                    act.wait_ge(p2, 2 * gr + 1)
                    nc.scalar.activation(pt[:, gr, :], g.ps[:, 2 * gr % 4, :], ACT.Copy).then_inc(pr_, 1)
                act.wait_ge(p2, 2 * NG + 1)
                nc.scalar.activation(pn[:], g.ps[0:NG, 0, :], ACT.Copy).then_inc(pr_, 1)
                act.wait_ge(pr_, NG + 1)
                nc.scalar.activation(pz[:, :, 1:], pt[:, :, 1:P], ACT.Copy).then_inc(zc, 1)
                nc.scalar.activation(pnz[:, 1:], pn[:, 1:P], ACT.Copy).then_inc(zc, 1)
                act.wait_ge(p5, 1)
                nc.scalar.activation(pz[:, :, 0], g.ps[:, 6, 0:NG], ACT.Copy).then_inc(zc, 1)
                nc.scalar.activation(pnz[:, 0:1], g.ps[0:NG, 6, NG:NG + 1], ACT.Copy).then_inc(zc, 1)

            @block.vector
            def _(dve):
                V = nc.vector
                for t in range(4):
                    tt(V, diff[:, :, cols(t)], hT[:, :, cols(t)], hT[:, :, cols(4 + t)], ALU.subtract).then_inc(fd, 1)
                    dve.wait_ge(fd, t + 1)
                    a = t * P + (1 if t == 0 else 0)
                    tt(V, hT[:, :, a:(t + 1) * P], hT[:, :, a:(t + 1) * P], hT[:, :, HALF + a:HALF + (t + 1) * P], ALU.add).then_inc(fo, 1)
                for gr in range(NG):
                    dve.wait_ge(p2, 2 * gr + 2)
                    V.tensor_copy(qt[:, gr, :], g.ps[:, (2 * gr + 1) % 4, :]).then_inc(qr, 1)
                flat = lambda b: g.ps[:, b:b + 2, :].rearrange("p a n -> p (a n)")
                for t in range(4):
                    bank = 4 * (t % 2)
                    dve.wait_ge(xr, t + 1)
                    ins = tt(V, g.x[:, t, :], g.x[:, t, :], flat(bank), ALU.add)
                    if t > 0:
                        ins = tt(V, g.x[:, 4 + t, :], g.x[:, 4 + t, :], flat(bank), ALU.add)
                    ins.then_inc(xs, 1)
                    dve.wait_ge(xs, t + 1)
                    dve.wait_ge(yr, t + 1)
                    tt(V, g.x[:, t, :], g.x[:, t, :], flat(bank + 2), ALU.subtract)
                    tt(V, g.x[:, 4 + t, :], g.x[:, 4 + t, :], flat(bank + 2), ALU.add).then_inc(ya, 1)
                dve.wait_ge(ya, 4)
                dve.wait_ge(zr, 1)
                tt(V, g.x[:, 4, :], g.x[:, 4, :], flat(0), ALU.add).then_inc(xs, 1)


@contextmanager
def stage(nc):
    before = nc.snapshot_sems()
    yield
    nc.clear_and_free_semaphores(nc.allocated_since(before))
    nc.all_engine_barrier()


def build(nc, io):
    with ExitStack() as ctx:
        g = Shared()
        g.io = io
        g.sem = lambda name: nc.alloc_semaphore(name=name)
        sb = lambda n, s, d=F32: ctx.enter_context(nc.sbuf_tensor(n, s, d))
        g.h_rows = nc.dram_tensor("h_rows", (SEQ, D), F32, kind="Internal").ap()
        g.y_rows = nc.dram_tensor("y_rows", (2 * SEQ, D), F32, kind="Internal").ap()
        g.ps = ctx.enter_context(nc.psum_tensor("ps", [P, 8, HALF], F32))
        g.ident, g.masks, g.small = sb("ident", [P, P]), sb("masks", [P, 5 * P + 2]), sb("small", [P, 72 + SLOT_BLOCKS + P + EXPERTS])
        g.ids = sb("choice_ids", [P, 2 * T])
        g.vecs, g.dtb, g.dskip = sb("vecs", [P, 44]), sb("dt_bias_a", [P, 32]), sb("dskip", [P, 8])
        g.neglam, g.qscale, g.negslope = sb("neg_lambda", [P, 1]), sb("qscale", [P, HEADS]), sb("neg_slopes", [P, HEADS])
        g.mhalf = sb("minus_half", [P, T])
        g.gates = sb("gates", [P, 2, T])
        g.slot_y, g.slot_x = sb("slot_y", [P, SLOT_BLOCKS], I32), sb("slot_x", [P, SLOT_BLOCKS], I32)
        g.block_expert, g.last_pair = sb("block_expert", [1, MAX_BLOCKS + 2], I32), sb("last_pair", [1, 1], I32)
        g.h_stored = [g.sem(f"h_stored_{n}") for n in range(2)]

        with ExitStack() as c0:
            sc = lambda n, s: c0.enter_context(nc.sbuf_tensor(n, s, F32))
            hT = c0.enter_context(nc.sbuf_tensor("hT_mix0_hi", [P, KT, SEQ], F32R))
            low_space = nc.sbuf_tensor("hT_mix0_lo", [P, KT, SEQ], F32R, side="right")
            low = low_space.__enter__()
            mixed = sc("mixed", [P, T, D])
            with ExitStack() as c1:
                s1 = lambda n, s: c1.enter_context(nc.sbuf_tensor(n, s, F32))
                xbcT, xs, draw = s1("xbcT", [P, XBC_T, SEQ + 4]), s1("xs", [P, T, 640]), s1("dt_raw", [P, T, 16])
                with stage(nc), ExitStack() as c2:
                    w = InputWeights(nc, g, c2)
                    constants = Constants(nc, g, c2)
                    with nc.sbuf_tensor("h_mix0", [P, 2, D], F32) as h:
                        with stage(nc):
                            norm_transpose(nc, g, "mix0", io["norm_mix"][0], hT, h, order_mirrored, False, x=mixed, start=(constants, w), low=low)
                    with stage(nc):
                        prepare_constants(nc, g, constants)
                    with stage(nc):
                        ssd_project(nc, g, w, hT, low, xbcT, xs, mixed, draw)
                with stage(nc):
                    ssd_scan(nc, g, xbcT, xs, mixed, draw)
            with stage(nc):
                attention(nc, g, hT, low, mixed)
            low_space.__exit__(None, None, None)
            g.x = ctx.enter_context(nc.sbuf_tensor("x_sb", [P, T, D], F32, side="right"))
            with stage(nc):
                project_out(nc, g, mixed, hT)
        for layer in range(2):
            if layer == 1:
                with nc.sbuf_tensor("hT_mix1", [P, KT, SEQ], F32) as hT:
                    with nc.sbuf_tensor("h_mix1", [P, 2, D], F32) as h:
                        with stage(nc):
                            norm_transpose(nc, g, "mix1", io["norm_mix"][1], hT, h, order_same, True)
                    with stage(nc):
                        fourier(nc, g, hT)
            with stage(nc), ExitStack() as c2:
                e = expert_weights(nc, g, layer)
                se = lambda n, s: c2.enter_context(nc.sbuf_tensor(f"{n}_{layer}", s, F32))
                e.raw, e.w2s = se("w13_raw", [P, 2, 2, KT, HID]), se("w2", [P, 2, 2, D])
                with nc.sbuf_tensor(f"hT_ffn{layer}", [P, KT, SEQ], F32) as hT, nc.sbuf_tensor(f"h_ffn{layer}", [P, T, D], F32) as h:
                    with stage(nc):
                        norm_transpose(nc, g, f"ffn{layer}", io["norm_ffn"][layer], hT, h, order_same, False, stored=g.h_stored[layer], weights=e, router=layer)
                    with stage(nc):
                        route(nc, g, layer)
                with stage(nc):
                    experts(nc, g, layer, e)
            with stage(nc):
                combine(nc, g, layer, layer == 1)


_INS = ['x', 'norm_mix', 'norm_ffn', 'w_in', 'q_norm', 'k_norm', 'lambda_q1', 'lambda_k1', 'lambda_q2', 'lambda_k2',
        'attn_subln', 'conv_w', 'conv_b', 'dt_bias', 'a_log', 'd_skip', 'ssd_norm', 'w_out', 'w_fourier',
        'router_group_w', 'router_group_b', 'router_expert_w', 'router_expert_b', 'expert_w1', 'expert_w3', 'expert_w2']


def shape_constants():
    import numpy as np
    k, n = np.arange(P)[:, None], np.arange(P)[None, :]
    masks = np.concatenate([k <= n, k > n, k >= n, k < n, np.ones((P, P), bool), k < 64, k >= 64], axis=1).astype(np.float32)
    small = np.concatenate([np.arange(32), np.arange(32) // PER_GROUP, np.arange(1, 9) * P, np.arange(SLOT_BLOCKS), np.arange(P), np.arange(32) * P]).astype(np.float32)
    negdist = -np.abs(k + 896 - np.arange(1920)[None, :]).astype(np.float32)
    ids = (2 * (k[:, :, None] + P * np.arange(T)[None, None, :]) + np.arange(2)[None, :, None] + 1).astype(np.float32)
    ids = ids.reshape(P, 2 * T)
    d, n, s = np.arange(2 * P), np.arange(HALF), np.arange(HALF + 1)
    turn = lambda a, b, size: 2 * np.pi * ((a[:, None] * b[None, :]) % size) / size
    ang = turn(d, d[:P + 1], 2 * P)
    channels = np.concatenate([np.cos(ang), np.sin(ang[:, 1:P])], axis=1) / np.sqrt(SEQ * 2.0 * P)
    channels[:, 0] /= 2
    cos_tokens, sin_tokens = np.cos(turn(n, s, SEQ)), np.sin(turn(n, s[:HALF], SEQ))
    return {"c_ident": np.eye(P, dtype=np.float32), "c_masks": masks, "c_small": small, "c_ids": ids, "c_negdist": negdist,
            "c_dft_channels": channels.astype(np.float32), "c_cos_tokens": cos_tokens.astype(np.float32),
            "c_sin_tokens": sin_tokens.astype(np.float32), "c_alternating": (1.0 - 2.0 * (s % 2))[None].astype(np.float32)}


def kernel(**inputs):
    import numpy as _np
    import concourse.bacc as _bacc
    from concourse.bass_utils import run_bass_kernel_spmd as _run

    nc = _bacc.Bacc("TRN2", target_bir_lowering=False, num_devices=1)
    arrays, io = {}, {}
    token = _np.concatenate([_np.arange(HALF), [HALF], SEQ - _np.arange(1, HALF)])
    ins = {n: inputs[n] for n in _INS}
    ins["x"] = ins["x"][0][token]
    wf = ins.pop("w_fourier")[0].reshape(GROUPS_F, 2 * P, D)
    ins["w_fourier_direct"], ins["w_fourier_mirror"], ins["w_fourier_128"] = wf[:, :P], wf[:, -_np.arange(P)], wf[:, P]
    for name, a in {**ins, **shape_constants()}.items():
        a = _np.ascontiguousarray(a)
        arrays[f"in_{name}"] = a
        io[name] = nc.dram_tensor(f"in_{name}", a.shape, F32, kind="ExternalInput").ap()
    io["out"] = nc.dram_tensor("out_0", (SEQ, D), F32, kind="ExternalOutput").ap()
    build(nc, io)
    r = _run(nc, [arrays], core_ids=[0])
    out = _np.empty_like(r.results[0]["out_0"])
    out[token] = r.results[0]["out_0"]
    return out[None]
```
